# Optimizing a Trainium2 kernel written in Bass

```python
import math
import jax, jax.numpy as jnp
from jax import lax
import numpy as np

D_MODEL = 1024
BATCH = 1
SEQ = 256
DEPTH = 1

MIX_WIDTH = D_MODEL
POOL_WIDTH = MIX_WIDTH // 2
POOL_WINDOWS = (2, 4, 8, 16)
N_POOL_GROUPS = len(POOL_WINDOWS)
POOL_GROUP_DIM = POOL_WIDTH // N_POOL_GROUPS
ATTN_WIDTH = MIX_WIDTH - POOL_WIDTH
HEAD_DIM = 64
N_ATTN_HEADS = ATTN_WIDTH // HEAD_DIM
DILATED_BRANCHES = ((128, 1), (512, 4), (2048, 16))
ATTN_BLOCK = 128
IN_WIDTH = POOL_WIDTH + 3 * ATTN_WIDTH
N_REL_BUCKETS = 32
REL_MAX_EXACT = N_REL_BUCKETS // 2
REL_MAX_DISTANCE = 2048
N_EXPERTS = 32
TOP_K = 4
D_EXPERT = D_MODEL
SWIGLU_LIMIT = 7.0
SWIGLU_ALPHA = 1.702
MOE_BLOCK = 128
PLE_DIM = 256
NORM_EPS = 1e-6
NEG_INF = -1e30


def rmsnorm(x, g):
    xf = x.astype(jnp.float32)
    y = xf * lax.rsqrt(jnp.mean(xf * xf, axis=-1, keepdims=True) + NORM_EPS)
    return (y * g.astype(jnp.float32)).astype(x.dtype)

def pool_mixer(u, w_pool, pool_scale):
    B, S, _ = u.shape
    ug = u.reshape(B, S, N_POOL_GROUPS, POOL_GROUP_DIM)
    t = jnp.arange(S)
    outs = []
    for gi, w in enumerate(POOL_WINDOWS):
        ch = ug[:, :, gi].astype(jnp.float32)
        cs = jnp.cumsum(ch, axis=1)
        prev = jnp.pad(cs, ((0, 0), (w, 0), (0, 0)))[:, :S]
        cnt = jnp.minimum(t + 1, w).astype(jnp.float32)[None, :, None]
        outs.append(((cs - prev) / cnt - ch).astype(u.dtype))
    pooled = jnp.stack(outs, axis=2)
    mixed = jnp.einsum('bsgc,gcd->bsgd', pooled, w_pool)
    return mixed.reshape(B, S, POOL_WIDTH) * pool_scale

def t5_bucket(dist):
    n = jnp.maximum(dist, 1).astype(jnp.float32)
    large = REL_MAX_EXACT + (jnp.log(n / REL_MAX_EXACT) / math.log(REL_MAX_DISTANCE / REL_MAX_EXACT)
                             * (N_REL_BUCKETS - REL_MAX_EXACT)).astype(jnp.int32)
    large = jnp.minimum(large, N_REL_BUCKETS - 1)
    return jnp.where(dist < REL_MAX_EXACT, dist, large)

def dilated_branch(q, k, v, rel_bias, window, dil):
    B, S, H, Dh = q.shape
    w_sub = window // dil
    blk = ATTN_BLOCK
    span = dil * blk
    Sp = -(-S // span) * span
    L = Sp // dil
    nb = L // blk

    def to_sub(t):
        t = jnp.pad(t, ((0, 0), (0, Sp - S), (0, 0), (0, 0)))
        t = t.reshape(B, nb, blk, dil, H, Dh)
        return t.transpose(0, 3, 4, 1, 2, 5)

    qs, ks, vs = to_sub(q), to_sub(k), to_sub(v)
    shift = lambda t: jnp.concatenate([jnp.zeros_like(t[:, :, :, :1]), t[:, :, :, :-1]], axis=3)
    keys = jnp.concatenate([shift(ks), ks], axis=4)
    vals = jnp.concatenate([shift(vs), vs], axis=4)

    s = jnp.einsum('brhnqc,brhnkc->brhnqk', qs, keys).astype(jnp.float32) * (1.0 / math.sqrt(Dh))
    qi = jnp.arange(blk)[:, None]
    ki = jnp.arange(2 * blk)[None, :]
    rel = blk + qi - ki
    bias = rel_bias[t5_bucket(jnp.maximum(rel, 0) * dil)]
    s = s + bias.transpose(2, 0, 1)[:, None].astype(jnp.float32)
    band = (rel >= 0) & (rel <= w_sub)
    first_ok = (jnp.arange(nb)[:, None, None] > 0) | (ki[None] >= blk)
    mask = band[None] & first_ok
    s = jnp.where(mask, s, NEG_INF)
    m = jnp.max(s, axis=-1)
    e = jnp.exp(s - m[..., None])
    l = jnp.sum(e, axis=-1)
    o = jnp.einsum('brhnqk,brhnkc->brhnqc', e, vals.astype(jnp.float32)) / l[..., None]
    lse = m + jnp.log(l)
    o = o.transpose(0, 3, 4, 1, 2, 5).reshape(B, Sp, H, Dh)[:, :S]
    lse = lse.transpose(0, 3, 4, 1, 2).reshape(B, Sp, H)[:, :S]
    return o, lse

def dilated_attention(q, k, v, rel_bias):
    outs, lses = [], []
    for window, dil in DILATED_BRANCHES:
        o, lse = dilated_branch(q, k, v, rel_bias, window, dil)
        outs.append(o)
        lses.append(lse)
    w = jax.nn.softmax(jnp.stack(lses, axis=0), axis=0)
    out = jnp.sum(w[..., None] * jnp.stack(outs, axis=0), axis=0)
    return out.astype(q.dtype)

def moe(h, w_router, b_router, w_gate_up, b_gate_up, w_down, b_down):
    B, S, D = h.shape
    T = B * S
    hf = h.reshape(T, D)
    logits = (hf @ w_router + b_router).astype(jnp.float32)
    topv, topi = lax.top_k(logits, TOP_K)
    gates = jax.nn.softmax(topv, axis=-1)

    expert_ids = topi.reshape(-1)
    token_ids = jnp.repeat(jnp.arange(T), TOP_K)
    gate_flat = gates.reshape(-1)
    order = jnp.argsort(expert_ids)
    sorted_e = expert_ids[order]
    group_sizes = jnp.bincount(expert_ids, length=N_EXPERTS)
    group_starts = jnp.cumsum(group_sizes) - group_sizes
    padded_sizes = (group_sizes + MOE_BLOCK - 1) // MOE_BLOCK * MOE_BLOCK
    padded_ends = jnp.cumsum(padded_sizes)
    padded_starts = padded_ends - padded_sizes
    rank = jnp.arange(T * TOP_K) - group_starts[sorted_e]
    dest = padded_starts[sorted_e] + rank

    n_rows = T * TOP_K + N_EXPERTS * MOE_BLOCK
    n_blocks = n_rows // MOE_BLOCK
    row_token = jnp.zeros((n_rows,), jnp.int32).at[dest].set(token_ids[order])
    row_gate = jnp.zeros((n_rows,), h.dtype).at[dest].set(gate_flat[order].astype(h.dtype))
    block_expert = jnp.minimum(
        jnp.searchsorted(padded_ends, jnp.arange(n_blocks) * MOE_BLOCK, side='right'),
        N_EXPERTS - 1)
    xs = hf[row_token].reshape(n_blocks, MOE_BLOCK, D)

    def expert_block(args):
        xb, e = args
        gu = xb @ w_gate_up[e] + b_gate_up[e]
        g, u = gu[:, :D_EXPERT], gu[:, D_EXPERT:]
        g = jnp.minimum(g, SWIGLU_LIMIT)
        u = jnp.clip(u, -SWIGLU_LIMIT, SWIGLU_LIMIT)
        glu = g * jax.nn.sigmoid(SWIGLU_ALPHA * g)
        return ((u + 1.0) * glu) @ w_down[e] + b_down[e]

    ys = lax.map(expert_block, (xs, block_expert)).reshape(n_rows, D)
    out = jnp.zeros((T, D), h.dtype).at[row_token].add(ys * row_gate[:, None])
    return out.reshape(B, S, D)

def first_inputs(seed: int = 0) -> dict:
    key = jax.random.key(seed)
    ks = jax.random.split(key, 24)
    f32 = jnp.float32
    nrm = lambda k, shape, s: jax.random.normal(k, shape, f32) * s
    gain = lambda k, shape: 1.0 + 0.05 * jax.random.normal(k, shape, f32)
    return {
        "x": nrm(ks[0], (BATCH, SEQ, D_MODEL), 1.0),
        "p": nrm(ks[1], (DEPTH, BATCH, SEQ, PLE_DIM), 1.0),
        "g_mix": gain(ks[2], (DEPTH, D_MODEL)),
        "w_in": nrm(ks[3], (DEPTH, D_MODEL, IN_WIDTH), D_MODEL ** -0.5),
        "w_pool": nrm(ks[4], (DEPTH, N_POOL_GROUPS, POOL_GROUP_DIM, POOL_GROUP_DIM), POOL_GROUP_DIM ** -0.5),
        "pool_scale": gain(ks[5], (DEPTH, POOL_WIDTH)),
        "rel_bias": nrm(ks[6], (N_REL_BUCKETS, N_ATTN_HEADS), 0.5),
        "w_out": nrm(ks[7], (DEPTH, MIX_WIDTH, D_MODEL), MIX_WIDTH ** -0.5),
        "g_ffn": gain(ks[8], (DEPTH, D_MODEL)),
        "w_router": nrm(ks[9], (DEPTH, D_MODEL, N_EXPERTS), D_MODEL ** -0.5),
        "b_router": nrm(ks[10], (DEPTH, N_EXPERTS), 0.01),
        "w_gate_up": nrm(ks[11], (DEPTH, N_EXPERTS, D_MODEL, 2 * D_EXPERT), D_MODEL ** -0.5),
        "b_gate_up": nrm(ks[12], (DEPTH, N_EXPERTS, 2 * D_EXPERT), 0.01),
        "w_down": nrm(ks[13], (DEPTH, N_EXPERTS, D_EXPERT, D_MODEL), D_EXPERT ** -0.5),
        "b_down": nrm(ks[14], (DEPTH, N_EXPERTS, D_MODEL), 0.01),
        "g_ple": gain(ks[15], (DEPTH, D_MODEL)),
        "w_ple_gate": nrm(ks[16], (DEPTH, D_MODEL, D_MODEL), D_MODEL ** -0.5),
        "w_ple_proj": nrm(ks[17], (DEPTH, PLE_DIM, D_MODEL), PLE_DIM ** -0.5),
        "g_final": gain(ks[18], (D_MODEL,)),
    }

def first_block(x, p, g_mix, w_in, w_pool, pool_scale, rel_bias, w_out, g_ffn,
              w_router, b_router, w_gate_up, b_gate_up, w_down, b_down,
              g_ple, w_ple_gate, w_ple_proj, g_final):
    B, S, _ = x.shape
    for i in range(DEPTH):
        h = rmsnorm(x, g_mix[i])
        z = jnp.einsum('bsd,de->bse', h, w_in[i])
        u = z[..., :POOL_WIDTH]
        qkv = z[..., POOL_WIDTH:].reshape(B, S, 3, N_ATTN_HEADS, HEAD_DIM)
        q, k, v = qkv[:, :, 0], qkv[:, :, 1], qkv[:, :, 2]
        a_out = pool_mixer(u, w_pool[i], pool_scale[i])
        b_out = dilated_attention(q, k, v, rel_bias).reshape(B, S, ATTN_WIDTH)
        mix = jnp.concatenate([a_out, b_out], axis=-1)
        x = x + jnp.einsum('bse,ed->bsd', mix, w_out[i])
        x = x + moe(rmsnorm(x, g_ffn[i]), w_router[i], b_router[i], w_gate_up[i],
                    b_gate_up[i], w_down[i], b_down[i])
        gate = jax.nn.sigmoid(jnp.einsum('bsd,de->bse', rmsnorm(x, g_ple[i]), w_ple_gate[i]))
        x = x + jnp.einsum('bsp,pd->bsd', p[i], w_ple_proj[i]) * gate
    return rmsnorm(x, g_final)


DEPTH_2 = 2

N_A_LAYERS = DEPTH_2 // 2
N_B_LAYERS = DEPTH_2 - N_A_LAYERS
LRU_WIDTH = D_MODEL
LRU_HEADS = 8
LRU_BLOCK = LRU_WIDTH // LRU_HEADS
CONV_WIDTH = 4
LRU_C = 8.0
ATTN_HEADS = 16
ATTN_HEAD_DIM = 64
ATTN_WIDTH_2 = ATTN_HEADS * ATTN_HEAD_DIM
Q_BLOCK = 128
PEER_HEADS = 8
PEER_NKEYS = 128
PEER_EXPERTS = PEER_NKEYS * PEER_NKEYS
PEER_TOPK = 16
PEER_QDIM = 256
PEER_HALF = PEER_QDIM // 2
PEER_CHUNK = 128
EPS = 1e-6


def rms_norm(x, g):
    xf = x.astype(jnp.float32)
    y = xf * lax.rsqrt(jnp.mean(xf * xf, axis=-1, keepdims=True) + EPS)
    return (y * g.astype(jnp.float32)).astype(x.dtype)

def rglru_block(h, w_in, conv_w, conv_b, w_r, w_i, b_r, b_i, lam, w_out):
    B, S, _ = h.shape
    proj = h @ w_in
    y_branch, x_branch = jnp.split(proj, 2, axis=-1)
    xc = lax.conv_general_dilated(x_branch, conv_w[:, None, :], window_strides=(1,),
                                  padding=((CONV_WIDTH - 1, 0),),
                                  dimension_numbers=('NWC', 'WIO', 'NWC'),
                                  feature_group_count=LRU_WIDTH) + conv_b
    xb = xc.reshape(B, S, LRU_HEADS, LRU_BLOCK)
    r = jax.nn.sigmoid(jnp.einsum('bshi,hij->bshj', xb, w_r).reshape(B, S, LRU_WIDTH).astype(jnp.float32)
                       + b_r.astype(jnp.float32))
    ig = jax.nn.sigmoid(jnp.einsum('bshi,hij->bshj', xb, w_i).reshape(B, S, LRU_WIDTH).astype(jnp.float32)
                        + b_i.astype(jnp.float32))
    log_a = -LRU_C * r * jax.nn.softplus(-lam.astype(jnp.float32))
    a = jnp.exp(log_a)
    u = jnp.sqrt(-jnp.expm1(2.0 * log_a)) * ig * xc.astype(jnp.float32)

    def combine(left, right):
        a1, b1 = left
        a2, b2 = right
        return a1 * a2, a2 * b1 + b2

    _, hseq = lax.associative_scan(combine, (a, u), axis=1)
    gated = (jax.nn.gelu(y_branch.astype(jnp.float32)) * hseq).astype(h.dtype)
    return gated @ w_out

def stick_breaking_attention(q, k, v):
    S = q.shape[1]
    scale = ATTN_HEAD_DIM ** -0.5
    outs = []
    for blk in range(S // Q_BLOCK):
        q0 = blk * Q_BLOCK
        end = q0 + Q_BLOCK
        qb = q[:, q0:end].astype(jnp.float32)
        kb = k[:, :end].astype(jnp.float32)
        z = jnp.einsum('bqhd,bkhd->bhqk', qb, kb) * scale
        t_pos = q0 + jnp.arange(Q_BLOCK)[:, None]
        s_pos = jnp.arange(end)[None, :]
        causal = s_pos < t_pos
        lbeta = jax.nn.log_sigmoid(z)
        l1m = jnp.where(causal, lbeta - z, 0.0)
        rc = lax.cumsum(l1m, axis=3, reverse=True)
        A = jnp.where(causal, jnp.exp(lbeta + rc - l1m), 0.0)
        outs.append(jnp.einsum('bhqk,bkhd->bqhd', A, v[:, :end].astype(jnp.float32)))
    return jnp.concatenate(outs, axis=1).astype(v.dtype)

def peer_ffn(h, w_q, sub_keys, u_tab, v_tab):
    B, S, D = h.shape
    T = B * S
    xt = h.reshape(T, D)
    q = (xt @ w_q).reshape(T, PEER_HEADS, 2, PEER_HALF).astype(jnp.float32)
    s = jnp.einsum('thpd,hpnd->thpn', q, sub_keys.astype(jnp.float32))
    sv, si = lax.top_k(s, PEER_TOPK)
    cand = sv[:, :, 0, :, None] + sv[:, :, 1, None, :]
    cv, ci = lax.top_k(cand.reshape(T, PEER_HEADS, PEER_TOPK * PEER_TOPK), PEER_TOPK)
    i1 = jnp.take_along_axis(si[:, :, 0], ci // PEER_TOPK, axis=-1)
    i2 = jnp.take_along_axis(si[:, :, 1], ci % PEER_TOPK, axis=-1)
    eidx = (i1 * PEER_NKEYS + i2).reshape(T, PEER_HEADS * PEER_TOPK)
    gates = jax.nn.softmax(cv, axis=-1).reshape(T, PEER_HEADS * PEER_TOPK)
    n_chunks = T // PEER_CHUNK

    def chunk_fn(args):
        xc, ic, gc = args
        uc = jnp.take(u_tab, ic, axis=0)
        vc = jnp.take(v_tab, ic, axis=0)
        act = jax.nn.gelu(jnp.einsum('cd,ckd->ck', xc, uc).astype(jnp.float32))
        return jnp.einsum('ck,ckd->cd', (gc * act).astype(vc.dtype), vc)

    out = lax.map(chunk_fn, (xt.reshape(n_chunks, PEER_CHUNK, D),
                             eidx.reshape(n_chunks, PEER_CHUNK, PEER_HEADS * PEER_TOPK),
                             gates.reshape(n_chunks, PEER_CHUNK, PEER_HEADS * PEER_TOPK)))
    return out.reshape(B, S, D).astype(h.dtype)

def per_layer_embed(h, p_i, g, w_gate, w_proj):
    gate = jax.nn.sigmoid((rms_norm(h, g) @ w_gate).astype(jnp.float32))
    return h + (gate * (p_i @ w_proj).astype(jnp.float32)).astype(h.dtype)

def second_inputs(seed: int = 0) -> dict:
    key = jax.random.key(seed)
    ks = jax.random.split(key, 28)
    nrm = jax.random.normal
    f32 = jnp.float32
    a8 = jax.random.uniform(ks[9], (N_A_LAYERS, LRU_WIDTH), f32, 0.9, 0.999)
    a0 = a8 ** (1.0 / LRU_C)
    return {
        'x': nrm(ks[0], (BATCH, SEQ, D_MODEL), f32),
        'p': nrm(ks[1], (DEPTH_2, BATCH, SEQ, PLE_DIM), f32),
        'norm_mix': 1.0 + 0.02 * nrm(ks[2], (DEPTH_2, D_MODEL), f32),
        'a_w_in': nrm(ks[3], (N_A_LAYERS, D_MODEL, 2 * LRU_WIDTH), f32) * D_MODEL ** -0.5,
        'a_conv_w': nrm(ks[4], (N_A_LAYERS, CONV_WIDTH, LRU_WIDTH), f32) * CONV_WIDTH ** -0.5,
        'a_conv_b': 0.02 * nrm(ks[5], (N_A_LAYERS, LRU_WIDTH), f32),
        'a_w_r': nrm(ks[6], (N_A_LAYERS, LRU_HEADS, LRU_BLOCK, LRU_BLOCK), f32) * LRU_BLOCK ** -0.5,
        'a_w_i': nrm(ks[7], (N_A_LAYERS, LRU_HEADS, LRU_BLOCK, LRU_BLOCK), f32) * LRU_BLOCK ** -0.5,
        'a_b_r': 0.02 * nrm(ks[8], (N_A_LAYERS, LRU_WIDTH), f32),
        'a_b_i': 0.02 * nrm(ks[10], (N_A_LAYERS, LRU_WIDTH), f32),
        'a_lambda': jnp.log(a0) - jnp.log1p(-a0),
        'a_w_out': nrm(ks[11], (N_A_LAYERS, LRU_WIDTH, D_MODEL), f32) * LRU_WIDTH ** -0.5,
        'kv_norm': 1.0 + 0.02 * nrm(ks[12], (D_MODEL,), f32),
        'w_kv': nrm(ks[13], (D_MODEL, 2 * ATTN_WIDTH_2), f32) * D_MODEL ** -0.5,
        'b_w_q': nrm(ks[14], (N_B_LAYERS, D_MODEL, ATTN_WIDTH_2), f32) * D_MODEL ** -0.5,
        'b_w_o': nrm(ks[15], (N_B_LAYERS, ATTN_WIDTH_2, D_MODEL), f32) * ATTN_WIDTH_2 ** -0.5,
        'norm_ffn': 1.0 + 0.02 * nrm(ks[16], (DEPTH_2, D_MODEL), f32),
        'peer_w_q': nrm(ks[17], (DEPTH_2, D_MODEL, PEER_HEADS * PEER_QDIM), f32) * D_MODEL ** -0.5,
        'peer_sub_keys': nrm(ks[18], (DEPTH_2, PEER_HEADS, 2, PEER_NKEYS, PEER_HALF), f32) * PEER_HALF ** -0.5,
        'peer_u': nrm(ks[19], (DEPTH_2, PEER_EXPERTS, D_MODEL), f32) * D_MODEL ** -0.5,
        'peer_v': nrm(ks[20], (DEPTH_2, PEER_EXPERTS, D_MODEL), f32) * (PEER_HEADS * PEER_TOPK) ** -0.5,
        'norm_ple': 1.0 + 0.02 * nrm(ks[21], (DEPTH_2, D_MODEL), f32),
        'ple_w_gate': nrm(ks[22], (DEPTH_2, D_MODEL, D_MODEL), f32) * D_MODEL ** -0.5,
        'ple_w_proj': nrm(ks[23], (DEPTH_2, PLE_DIM, D_MODEL), f32) * PLE_DIM ** -0.5,
        'final_norm': 1.0 + 0.02 * nrm(ks[24], (D_MODEL,), f32),
    }

def second_block(x, p, norm_mix, a_w_in, a_conv_w, a_conv_b, a_w_r, a_w_i, a_b_r, a_b_i, a_lambda,
              a_w_out, kv_norm, w_kv, b_w_q, b_w_o, norm_ffn, peer_w_q, peer_sub_keys, peer_u,
              peer_v, norm_ple, ple_w_gate, ple_w_proj, final_norm):
    B, S, _ = x.shape
    h = x
    k_shared = None
    v_shared = None
    for i in range(DEPTH_2):
        hn = rms_norm(h, norm_mix[i])
        if i < N_A_LAYERS:
            j = i
            h = h + rglru_block(hn, a_w_in[j], a_conv_w[j], a_conv_b[j], a_w_r[j], a_w_i[j],
                                a_b_r[j], a_b_i[j], a_lambda[j], a_w_out[j])
        else:
            j = i - N_A_LAYERS
            if i == N_A_LAYERS:
                kvp = rms_norm(h, kv_norm) @ w_kv
                k_flat, v_flat = jnp.split(kvp, 2, axis=-1)
                k_shared = k_flat.reshape(B, S, ATTN_HEADS, ATTN_HEAD_DIM)
                v_shared = v_flat.reshape(B, S, ATTN_HEADS, ATTN_HEAD_DIM)
            q = (hn @ b_w_q[j]).reshape(B, S, ATTN_HEADS, ATTN_HEAD_DIM)
            o = stick_breaking_attention(q, k_shared, v_shared).reshape(B, S, ATTN_WIDTH_2)
            h = h + o @ b_w_o[j]
        h = h + peer_ffn(rms_norm(h, norm_ffn[i]), peer_w_q[i], peer_sub_keys[i], peer_u[i], peer_v[i])
        h = per_layer_embed(h, p[i], norm_ple[i], ple_w_gate[i], ple_w_proj[i])
    return rms_norm(h, final_norm)


def setup_inputs(seed=0):
    out = dict(first_inputs(seed))
    for name, value in second_inputs(seed + 1).items():
        if name != "x":
            out[name + "_2"] = value
    return out


def reference(
    x, p, g_mix, w_in, w_pool, pool_scale, rel_bias, w_out, g_ffn, w_router, b_router,
    w_gate_up, b_gate_up, w_down, b_down, g_ple, w_ple_gate, w_ple_proj, g_final, p_2,
    norm_mix_2, a_w_in_2, a_conv_w_2, a_conv_b_2, a_w_r_2, a_w_i_2, a_b_r_2, a_b_i_2,
    a_lambda_2, a_w_out_2, kv_norm_2, w_kv_2, b_w_q_2, b_w_o_2, norm_ffn_2, peer_w_q_2,
    peer_sub_keys_2, peer_u_2, peer_v_2, norm_ple_2, ple_w_gate_2, ple_w_proj_2, final_norm_2,
):
    x = first_block(
        x, p, g_mix, w_in, w_pool, pool_scale, rel_bias, w_out, g_ffn, w_router, b_router,
        w_gate_up, b_gate_up, w_down, b_down, g_ple, w_ple_gate, w_ple_proj, g_final,
    )
    return second_block(
        x, p_2, norm_mix_2, a_w_in_2, a_conv_w_2, a_conv_b_2, a_w_r_2, a_w_i_2, a_b_r_2,
        a_b_i_2, a_lambda_2, a_w_out_2, kv_norm_2, w_kv_2, b_w_q_2, b_w_o_2, norm_ffn_2,
        peer_w_q_2, peer_sub_keys_2, peer_u_2, peer_v_2, norm_ple_2, ple_w_gate_2, ple_w_proj_2,
        final_norm_2,
    )


_drawn_inputs = setup_inputs


def setup_inputs(seed=0):
    import zlib

    import numpy as np

    out = dict(_drawn_inputs(seed))
    spreads = {}
    factors = {'b_gate_up': 8.0,
     'b_down': 8.0,
     'g_ple': 6.614,
     'norm_mix_2': 5.139,
     'a_b_r_2': 8.0,
     'a_b_i_2': 8.0,
     'kv_norm_2': 14.609,
     'norm_ffn_2': 35.966,
     'norm_ple_2': 64.0,
     'final_norm_2': 8.045}
    for name, (base, spread) in spreads.items():
        noise = np.random.default_rng([zlib.crc32(name.encode()), seed]).standard_normal(out[name].shape)
        drawn = base * np.exp(spread * noise) if base else spread * noise
        out[name] = __import__('jax').numpy.asarray(drawn.astype(out[name].dtype))
    for name, factor in factors.items():
        out[name] = (out[name] * factor).astype(out[name].dtype)
    return out
```

```python
from contextlib import ExitStack

import numpy as np

import concourse.bass as bass
import concourse.mybir as mybir

F32 = mybir.dt.float32
BF16 = mybir.dt.bfloat16
I32 = mybir.dt.int32
U32 = mybir.dt.uint32
ACT = mybir.ActivationFunctionType
ALU = mybir.AluOpType
AX_X = mybir.AxisListType.X

P = 128
T = 256
D = 1024
DT = D // P
TT = T // P
W = DT * T
BANK = 512
EPS = 1e-6
NEG = -1e30

RING = 8
SLOT = 1024

HEADS1, DH = 8, 64
SPAN = 3 * P
POOL_WINDOWS = (2, 4, 8, 16)
PAD = 16

EXPERTS, TOP_K = 32, 4
CAP = 128
PASSES = T // CAP
LIMIT, ALPHA = 7.0, 1.702
MOE_SLOTS, MOE_SLOT = 12, 2048

HEADS2 = 16
CONV = 4

PH, PTOP, PKEYS = 8, 16, 128
CHUNKS = PKEYS
GROUP = 4
BODY = 8
READS = 4 + CHUNKS // 2

C_IDENT, C_ONES, C_TRIU, C_NTRI, C_NONES, C_IOTA = (P * k for k in range(6))
C_INV = 6 * P
C_COLS = C_INV + 4 * PAD
PARAMS = {}
for _name, _n in (("g_mix", DT), ("g_ffn", DT), ("g_ple", DT), ("g_final", DT), ("pool_scale", 4),
                  ("norm_mix", 2 * DT), ("conv_w", CONV * DT), ("conv_b", DT), ("b_r", DT), ("b_i", DT),
                  ("lam", DT), ("kv_norm", DT), ("norm_ffn", 2 * DT), ("norm_ple", 2 * DT), ("final", DT)):
    PARAMS[_name] = sum(n for _, n in PARAMS.values()), _n
P_COLS = sum(n for _, n in PARAMS.values())


def bucket(d):
    n = np.maximum(d, 1).astype(np.float32)
    large = 16 + (np.log(n / np.float32(16)) / np.float32(np.log(128)) * np.float32(16)).astype(np.int32)
    return np.where(d < 16, d, np.minimum(large, 31))


def constants():
    k, m = np.arange(P)[:, None], np.arange(P)[None, :]
    base = np.concatenate([
        k == m, np.ones((P, P)), k < m, -1.0 * (k > m), -np.ones((P, P)), np.broadcast_to(m, (P, P)),
        np.broadcast_to(np.concatenate([1.0 / np.minimum(np.arange(PAD) + 1, w) for w in POOL_WINDOWS]), (P, 4 * PAD)),
    ], axis=1).astype(np.float32)
    dist = T - 1 - np.arange(SPAN)
    reach = (dist >= 0) * ((dist <= 128).astype(int) + (dist % 4 == 0) + (dist % 16 == 0))
    mask = np.where(reach > 0, np.log(np.maximum(reach, 1)), NEG).astype(np.float32)
    hot = (bucket(np.maximum(dist, 0))[None, :] == np.arange(32)[:, None]).astype(np.float32)
    return base, np.ascontiguousarray(np.broadcast_to(mask, (P, SPAN))), hot


def plan():
    first, n = {}, 0
    for name, chunks in (
        ("w_in", 16), ("w_pool", 1), ("w_out", 8), ("w_router", 1), ("b_down", 1), ("proj0", 2), ("ple0", 8),
        ("a_in", 16), ("w_r", 1), ("w_i", 1), ("a_out", 8),
        ("wq0", 16), ("keys0", 2), ("u0", CHUNKS), ("v0", CHUNKS), ("proj1", 2), ("ple1", 8),
        ("kv", 16), ("bq", 8), ("bo", 8),
        ("wq1", 16), ("keys1", 2), ("u1", CHUNKS), ("v1", CHUNKS), ("proj2", 2), ("ple2", 8),
    ):
        first[name] = n
        n += chunks
    return first


class Tally:

    def __init__(self, eng, sem):
        self.eng, self.sem, self.n, self.turns = eng, sem, 0, 0

    def mark(self, ins):
        ins.then_inc(self.sem, 1)
        self.n += 1
        return self.n

    def wait(self, n=None):
        self.eng.wait_ge(self.sem, self.turns + (self.n if n is None else n))

    def link(self, ins):
        self.mark(ins)
        self.wait()

    def enter(self, turn, per):
        self.turns, self.start, self.per = turn * per, self.n, per

    def leave(self, count):
        assert self.n == self.start + self.per, (self.n - self.start, self.per)
        self.n, self.turns = self.start + self.per * count, 0


def program(nc, io, out):
    first = plan()
    with ExitStack() as ctx:
        def sb(name, shape, dt=F32):
            return ctx.enter_context(nc.sbuf_tensor(name, shape, dt))

        def sem(name):
            return ctx.enter_context(nc.semaphore(name))

        big = sb("big", [P, CHUNKS * T])
        ring = sb("ring", [P, RING, SLOT])
        xT = sb("xT", [P, W])
        hT = sb("hT", [P, W])
        mT = sb("mT", [P, W])
        con = sb("con", [P, C_COLS])
        par = sb("par", [P, P_COLS])
        rs = sb("rs", [P, 2 * T])
        eps = sb("eps", [P, 1])
        small = sb("small", [P, 4064])
        pT = sb("pT", [P, 2 * T])
        ps = ctx.enter_context(nc.psum_tensor("ps", [P, 8, BANK], F32))
        toeplitz = nc.dram_tensor("toeplitz", (HEADS1, P, SPAN), F32, kind="Internal").ap()
        expert_out = nc.dram_tensor("expert_out", (EXPERTS * CAP, D), F32, kind="Internal").ap()

        ident, ones = con[:, C_IDENT:C_IDENT + P], con[:, C_ONES:C_ONES + P]
        triu, ntri = con[:, C_TRIU:C_TRIU + P], con[:, C_NTRI:C_NTRI + P]
        nones, iota = con[:, C_NONES:C_NONES + P], con[:, C_IOTA:C_IOTA + P]

        def col(name, k=0):
            a, n = PARAMS[name]
            return par[:, a + k:a + k + 1]

        def tile(buf, c, n=T):
            return buf[:, c * n:(c + 1) * n]

        def half(bank, e):
            return ps[:, bank + e // 2, (e % 2) * T:(e % 2 + 1) * T]

        w_loaded = [sem(f"w_loaded{k}") for k in range(RING)]
        w_used = sem("w_used")
        x_loaded, con_loaded, par_loaded = sem("x_loaded"), sem("con_loaded"), sem("par_loaded")
        attn_loaded, bias_loaded = sem("attn_loaded"), sem("bias_loaded")
        x_ready, h_ready = sem("x_ready"), sem("h_ready")
        sq_ready, ss_done, rms_ready = sem("sq_ready"), sem("ss_done"), sem("rms_ready")
        eps_ready, p_loaded = sem("eps_ready"), sem("p_loaded")
        dve_step, act_step = sem("dve_step"), sem("act_step")
        names = (
            "rb_ready row_done row_ready toep_loaded u_copied qk_ready v_ready pooled_ready mixed_done "
            "score_done biased prob_exp prob_ready pt_done pt_ready pv_done mix_ready "
            "htok_done htok_ready logits_done neg_top gate_exp mask_ready rank_done count_ready gmat_in gmat_done gmat_ready "
            "slots_ready diag_ready sel_ready gathered xg_ready sig_in sig_ready hid_ready y_done y_ready yt_done "
            "ytok_ready y_stored y_fetched combined added "
            "proj_done gate_ready "
            "conv_ready yg_ready lam_in lam_exp ri_ready lru_exp lru_e lru_sqrt gated_ready "
            "pq_ready s_done bank_read cv_ready cv_exp sel_done selT_done selT_ready oh_ready g_done g_used "
            "q2_ready k2_ready v2_ready z_done spm_ready rc_done arg_ready a_exp w_exp a_ready o_done o_ready "
            "out_ready out_stored moe_step moe_used"
        ).split()
        S = {n: sem(n) for n in names}
        row_stored = [sem(f"row_stored{k}") for k in range(2)]
        moe_loaded = [sem(f"moe_loaded{k}") for k in range(MOE_SLOTS)]

        def used_through(eng, seg, chunks):
            eng.wait_ge(w_used, first[seg] + chunks)

        TAIL = MOE_SLOTS * MOE_SLOT
        tail = big[:, TAIL:CHUNKS * T]
        q1, k1, v1 = (tail[:, k * 1024:(k + 1) * 1024] for k in range(3))
        toep = tail[:, 3072:3072 + HEADS1 * SPAN]
        upad = tail[:, 6144:6144 + 4 * (PAD + T)]
        moe_bias = tail[:, 7424:7936]
        winsum = small[:, 0:4 * (PAD + T)]
        winsum2 = small[:, 1088:2176]
        cmask, hot = small[:, 2176:2560], small[0:32, 2560:2944]
        relb, rb = small[0:32, 2944:2952], small[0:32, 3040:4064]
        stat1 = small[:, 2952:3000]
        prob = [hT[:, k * SPAN:(k + 1) * SPAN] for k in range(2)]
        probT = [hT[:, (2 + k) * SPAN:(3 + k) * SPAN] for k in range(2)]
        row = [mT[:, k * SPAN:(k + 1) * SPAN] for k in range(2)]

        r_max, r_idx = small[:, 0:16], small[:, 16:32]
        r_idxf, r_nmax = small[:, 32:40], small[:, 40:42]
        r_exp, r_sum, r_rec, r_gate = small[:, 48:56], small[:, 56:58], small[:, 58:60], small[:, 60:68]
        r_bias, r_logit = small[:, 3008:3040], small[:, 160:224]
        r_hot = small[:, 256:512]
        r_mask, r_gmat = small[:, 512:576], small[:, 576:640]
        r_rank1 = small[:, 640:640 + TT * (EXPERTS + 1)]
        r_tmp = small[:, 768:1024]
        r_slotf, r_slot = small[:, 1024:1032], small[:, 1032:1040].bitcast(U32)
        r_pass, r_step = small[:, 1056:1064], small[:, 1064:1072]
        r_cntf, r_cnt = small[0:1, 4062:4063], small[0:1, 4063:4064].bitcast(I32)
        r_gmatT = small[0:32, 1280:1280 + T]
        r_diag = small[:, 1536:1536 + 8 * P]
        m_sel = small[:, 2560:2560 + TT * CAP]
        MW = DT * CAP
        m_xg, m_g, m_u, m_sig, m_h, m_y, m_tok = (tail[:, MW * k:MW * (k + 1)] for k in range(7))
        fetched = big[:, 0:TT * TOP_K * D]

        lru = [big[:, k * W:(k + 1) * W] for k in range(8)]
        sp = small[:, 0:96]
        k2, q2, v2 = lru[0], lru[1], lru[2]
        st = [big[:, 3 * W + k * SPAN:3 * W + (k + 1) * SPAN] for k in range(24)]

        pq = big[:, CHUNKS * T - 2 * W:CHUNKS * T]
        sv = small[:, 0:256]
        si = small[:, 256:512].bitcast(U32)
        sif = small[:, 512:768]
        cand, cand2 = small[:, 768:1024], small[:, 1024:1280]
        p_tmp = small[:, 1280:1408]
        cv = small[:, 1408:1664]
        ci = small[:, 1664:1792].bitcast(U32)
        cc = small[:, 1792:1920].bitcast(U32)
        ccf = small[:, 1920:2048]
        pick = small[:, 2048:3072].bitcast(BF16)
        i12 = small[:, 3072:3584]
        p_sum = small[:, 3584:3600]
        selT = small[:, 0:3 * T]

        block = ctx.enter_context(nc.Block())

        @block.sync
        def _(sync):
            def free(n):
                if n >= RING:
                    sync.wait_ge(w_used, n - RING + 1)

            def load(n, src, cols=SLOT, rows=P):
                free(n)
                sync.dma_start(ring[0:rows, n % RING, 0:cols], src).then_inc(w_loaded[n % RING], 16)

            def dense(seg, w, halves=1):
                for h in range(halves):
                    for c in range(DT):
                        load(first[seg] + h * DT + c, w[c * P:(c + 1) * P, h * SLOT:(h + 1) * SLOT])

            def ple(k, p, proj, gate):
                if k:
                    sync.wait_ge(w_used, first[f"proj{k - 1}"] + 2)
                sync.dma_start(pT[:, :], p).then_inc(p_loaded, 16)
                for c in range(2):
                    load(first[f"proj{k}"] + c, proj[c * P:(c + 1) * P, :])
                dense(f"ple{k}", gate)

            def table(seg, src):
                n = first[seg]
                with sync.Fori(0, CHUNKS // RING) as i:
                    for k in range(RING):
                        sync.wait_ge(w_used, n + k - RING + 1 + i * RING)
                        sync.dma_start(ring[:, (n + k) % RING, :], src[i * RING + k])\
                            .then_inc(w_loaded[(n + k) % RING], 16)

            def expert_chunk(e, k):
                dst = big[:, k * MOE_SLOT:(k + 1) * MOE_SLOT]
                if k < DT:
                    src = io["w_gate_up"][e, k * P:(k + 1) * P, :]
                else:
                    src = io["w_down"][e, (k - DT) * 2 * P:(k - DT + 1) * 2 * P, :].rearrange("(s p) d -> p s d", p=P)
                    dst = dst.rearrange("p (s d) -> p s d", s=2)
                sync.dma_start(dst, src).then_inc(moe_loaded[k], 16)

            def expert_weights(level, start=0):
                if level:
                    sync.wait_ge(S["combined"], level)
                with sync.Fori(start, EXPERTS) as e:
                    for k in range(MOE_SLOTS):
                        sync.wait_ge(S["moe_used"], (EXPERTS * level - 1) * MOE_SLOTS + k + 1 + e * MOE_SLOTS)
                        expert_chunk(e, k)

            sync.dma_start(xT[:, :], io["x"]).then_inc(x_loaded, 16)
            sync.dma_start(con[:, :], io["consts"]).then_inc(con_loaded, 16)
            sync.dma_start(par[:, :], io["params"]).then_inc(par_loaded, 16)
            sync.dma_start(cmask, io["reach"]).then_inc(attn_loaded, 16)
            sync.dma_start(hot, io["hot"]).then_inc(attn_loaded, 16)
            sync.dma_start(relb, io["rel_bias"]).then_inc(attn_loaded, 16)
            sync.dma_start(moe_bias, io["b_gate_up"]).then_inc(bias_loaded, 16)
            sync.dma_start(r_bias, io["b_router"].partition_broadcast(P)).then_inc(bias_loaded, 16)
            dense("w_in", io["w_in"], 2)
            load(first["w_pool"], io["w_pool"], 4 * P)
            dense("w_out", io["w_out"])
            load(first["w_router"], io["w_router"], DT * EXPERTS)
            load(first["b_down"], io["b_down"], rows=EXPERTS)
            for k in range(MOE_SLOTS):
                expert_chunk(0, k)
            expert_weights(0, 1)
            sync.wait_ge(S["count_ready"], 1)
            count = sync.value_load(r_cnt, min_val=0, max_val=T)
            with ExitStack() as nest:
                for level in range(1, PASSES):
                    nest.enter_context(sync.If(count > CAP * level))
                    expert_weights(level)
            ple(0, io["p0"], io["w_ple_proj"], io["w_ple_gate"])
            dense("a_in", io["a_w_in"], 2)
            load(first["w_r"], io["w_r"])
            load(first["w_i"], io["w_i"])
            dense("a_out", io["a_w_out"])
            for L in range(2):
                dense(f"wq{L}", io["peer_w_q"][L], 2)
                for k in range(2):
                    load(first[f"keys{L}"] + k, io["sub_keys"][L, :, k * SLOT:(k + 1) * SLOT])
                table(f"u{L}", io[f"u{L}"])
                table(f"v{L}", io[f"v{L}"])
                ple(L + 1, io["p2"][L], io["ple_w_proj"][L], io["ple_w_gate"][L])
                if L == 0:
                    dense("kv", io["w_kv"], 2)
                    dense("bq", io["b_w_q"])
                    dense("bo", io["b_w_o"])
            sync.wait_ge(S["out_ready"], 8)
            sync.dma_start(out, mT[:, :]).then_inc(S["out_stored"], 16)
            sync.wait_ge(S["out_stored"], 16)

        @block.tensor
        def _(pe):
            def chunk(n):
                pe.wait_ge(w_loaded[n % RING], 16 * (n // RING + 1))
                return ring[:, n % RING, :]

            def sum_squares(k):
                for j in range(4):
                    pe.wait_ge(sq_ready, 4 * k + j + 1)
                    for c in (2 * j, 2 * j + 1):
                        last = pe.matmul(ps[:, 7, 0:T], ones, tile(mT, c), start=(c == 0), stop=(c == DT - 1))
                last.then_inc(ss_done, 1)

            def dense(n, src, bank, ready=None, at=0, between=None):
                for c in range(DT):
                    if ready is not None:
                        pe.wait_ge(ready, at + c + 1)
                    w = chunk(n + c)
                    for e in range(DT):
                        last = pe.matmul(half(bank, e), w[:, e * P:(e + 1) * P], src(c),
                                         start=(c == 0 and e % 2 == 0), stop=(c == DT - 1), skip_group_check=True)
                    last.then_inc(w_used, 1)
                    if between:
                        between(c)

            def token_major(n, src, ready, at, cols, outs):
                for c in range(DT):
                    pe.wait_ge(ready, at + c + 1)
                    w = chunk(n + c)
                    for tt in range(TT):
                        for k, o in enumerate(outs[tt]):
                            last = pe.matmul(o, tile(src, c)[:, tt * P:(tt + 1) * P],
                                             w[:, cols + k * BANK:cols + (k + 1) * BANK],
                                             start=(c == 0), stop=(c == DT - 1), skip_group_check=True)
                    last.then_inc(w_used, 1)

            hsrc = lambda c: tile(hT, c)
            msrc = lambda c: tile(mT, c)

            pe.wait_ge(con_loaded, 16)
            sum_squares(0)
            pe.wait_ge(attn_loaded, 48)

            def bias_row(h):
                pe.wait_ge(S["rb_ready"], h + 1)
                if h >= 2:
                    pe.wait_ge(S["row_ready"], h - 1)
                pe.matmul(ps[:, 4 + h % 2, 0:SPAN], rb[:, h * P:(h + 1) * P], hot, start=True, stop=True)\
                    .then_inc(S["row_done"], 1)

            dense(first["w_in"], hsrc, 0, h_ready, 0, between=bias_row)
            pe.wait_ge(S["row_ready"], HEADS1)
            pe.wait_ge(rms_ready, 1)
            for c in range(DT):
                w = chunk(first["w_in"] + DT + c)
                for e in range(4):
                    pe.matmul(half(4, e), w[:, e * P:(e + 1) * P], hsrc(c),
                              start=(c == 0 and e % 2 == 0), stop=(c == DT - 1), skip_group_check=True)
                for tt in range(TT):
                    last = pe.matmul(ps[:, 6 + tt, :], hsrc(c)[:, tt * P:(tt + 1) * P], w[:, BANK:2 * BANK],
                                     start=(c == 0), stop=(c == DT - 1), skip_group_check=True)
                last.then_inc(w_used, 1)

            def scores(h):
                lo = 64 * (h % 2)
                q, k = tile(q1, h // 2), tile(k1, h // 2)
                if h == 0:
                    pe.wait_ge(S["qk_ready"], 4)
                    pe.wait_ge(S["u_copied"], 4)
                if h >= 2:
                    pe.wait_ge(S["prob_ready"], h - 1)
                pe.matmul(ps[:, h % 2, 0:P], q[lo:lo + DH, 0:P], k[lo:lo + DH, 0:P], start=True, stop=True)
                pe.matmul(ps[:, h % 2, P:SPAN], q[lo:lo + DH, P:T], k[lo:lo + DH, 0:T], start=True, stop=True)\
                    .then_inc(S["score_done"], 1)

            def turn(h):
                pe.wait_ge(S["prob_ready"], h + 1)
                if h >= 2:
                    pe.wait_ge(S["pt_ready"], h - 1)
                for b in range(3):
                    last = pe.transpose(ps[:, 2 + h % 2, b * P:(b + 1) * P], prob[h % 2][:, b * P:(b + 1) * P], ident)
                last.then_inc(S["pt_done"], 1)

            def values(h):
                lo = 64 * (h % 2)
                if h == 0:
                    pe.wait_ge(S["v_ready"], 2)
                pe.wait_ge(S["pt_ready"], h + 1)
                if h >= 4:
                    pe.wait_ge(S["mix_ready"], h - 3)
                o = ps[lo:lo + DH, 4 + (h // 2) % 2, 0:T]
                v = [v1[:, tt * BANK + h * DH:tt * BANK + (h + 1) * DH] for tt in range(TT)]
                pt = probT[h % 2]
                pe.matmul(o[:, 0:P], v[0], pt[:, 0:P], start=True, stop=True)
                pe.matmul(o[:, P:T], v[0], pt[:, P:2 * P], start=True, stop=False)
                pe.matmul(o[:, P:T], v[1], pt[:, 2 * P:SPAN], start=False, stop=True).then_inc(S["pv_done"], 1)

            for s in range(HEADS1 + 2):
                if s < HEADS1:
                    scores(s)
                if 1 <= s <= HEADS1:
                    turn(s - 1)
                if s >= 2:
                    values(s - 2)
            w = chunk(first["w_pool"])
            pe.wait_ge(S["v_ready"], 2)
            for g in range(4):
                pe.wait_ge(S["pooled_ready"], g + 1)
                last = pe.matmul(half(6, g), w[:, g * P:(g + 1) * P], upad[:, g * (PAD + T) + PAD:(g + 1) * (PAD + T)],
                                 start=True, stop=True)
            last.then_inc(w_used, 1)
            pe.wait_ge(S["mix_ready"], HEADS1 + 4)
            dense(first["w_out"], msrc, 0)

            sum_squares(1)
            pe.wait_ge(h_ready, 2 * DT)
            w = chunk(first["w_router"])
            for tt in range(TT):
                for c in range(DT):
                    last = pe.matmul(ps[:, 4, tt * EXPERTS:(tt + 1) * EXPERTS], tile(hT, c)[:, tt * P:(tt + 1) * P],
                                     w[:, c * EXPERTS:(c + 1) * EXPERTS], start=(c == 0), stop=(c == DT - 1))
            last.then_inc(w_used, 1)
            for tt in range(TT):
                for c in range(DT):
                    last = pe.transpose(ps[:, 2 * tt + c // 4, (c % 4) * P:(c % 4 + 1) * P],
                                        tile(hT, c)[:, tt * P:(tt + 1) * P], ident)
                last.then_inc(S["htok_done"], 1)
            pe.wait_ge(S["mask_ready"], 2)
            pe.matmul(ps[:, 5, 0:32], triu, r_mask[:, 0:32], start=True, stop=True)
            pe.matmul(ps[:, 5, 32:64], triu, r_mask[:, 32:64], start=True, stop=False)
            pe.matmul(ps[:, 5, 32:64], ones, r_mask[:, 0:32], start=False, stop=True)
            pe.matmul(ps[:, 5, 64:96], ones, r_mask[:, 0:32], start=True, stop=False)
            pe.matmul(ps[:, 5, 64:96], ones, r_mask[:, 32:64], start=False, stop=True).then_inc(S["rank_done"], 1)
            pe.wait_ge(S["gmat_in"], 2)
            for tt in range(TT):
                last = pe.transpose(ps[0:32, 6, tt * P:(tt + 1) * P], r_gmat[:, tt * 32:(tt + 1) * 32], ident)
            last.then_inc(S["gmat_done"], 1)

            def expert_pass(level):
                def gather(count):
                    pe.wait_ge(S["sel_ready"], count)
                    for c in range(DT):
                        for tt in range(TT):
                            last = pe.matmul(ps[:, c // 4, (c % 4) * CAP:(c % 4 + 1) * CAP],
                                             mT[:, tt * D + c * P:tt * D + (c + 1) * P],
                                             m_sel[:, tt * CAP:(tt + 1) * CAP], start=(tt == 0), stop=(tt == TT - 1))
                    last.then_inc(S["gathered"], 1)

                if level == 0:
                    pe.wait_ge(S["htok_ready"], 4)
                    pe.wait_ge(S["gmat_ready"], 1)
                gather(33 * level + 1)
                with pe.Fori(0, EXPERTS) as e:
                    n = e + EXPERTS * level if level else e
                    pe.wait_ge(S["xg_ready"], e * 2 + 66 * level + 2)
                    for c in range(DT):
                        pe.wait_ge(moe_loaded[c], n * 16 + 16)
                        for f in range(2 * DT):
                            last = pe.matmul(ps[:, 2 + f // 4, (f % 4) * CAP:(f % 4 + 1) * CAP],
                                             big[:, c * MOE_SLOT + f * P:c * MOE_SLOT + (f + 1) * P],
                                             m_xg[:, c * CAP:(c + 1) * CAP],
                                             start=(c == 0 and f % 4 == 0), stop=(c == DT - 1), skip_group_check=True)
                        last.then_inc(S["moe_used"], 1)
                    gather(e + 33 * level + 2)
                    for k in range(DT, MOE_SLOTS):
                        pe.wait_ge(S["hid_ready"], n * 2 + 1 + (k - DT) // 2)
                        pe.wait_ge(moe_loaded[k], n * 16 + 16)
                        for s in range(2):
                            f = 2 * (k - DT) + s
                            for c in range(DT):
                                last = pe.matmul(ps[:, 6 + c // 4, (c % 4) * CAP:(c % 4 + 1) * CAP],
                                                 big[:, k * MOE_SLOT + s * D + c * P:k * MOE_SLOT + s * D + (c + 1) * P],
                                                 m_h[:, f * CAP:(f + 1) * CAP],
                                                 start=(f == 0 and c % 4 == 0), stop=(f == DT - 1), skip_group_check=True)
                        last.then_inc(S["moe_used"], 1)
                    pe.wait_ge(S["xg_ready"], e * 2 + 66 * level + 4)
                    for b in range(2):
                        pe.wait_ge(S["y_ready"], n * 2 + b + 1)
                        for c in range(4 * b, 4 * b + 4):
                            last = pe.transpose(ps[:, b, (c % 4) * P:(c % 4 + 1) * P], m_y[:, c * CAP:(c + 1) * CAP], ident)
                        last.then_inc(S["yt_done"], 1)
                    pe.wait_ge(S["ytok_ready"], n * 2 + 2)

            def combine(level):
                pe.wait_ge(S["diag_ready"], 8 * (level + 1))
                pe.wait_ge(S["y_fetched"], 16 * 8 * (level + 1))
                if level == 0:
                    w = chunk(first["b_down"])
                    for c in range(DT):
                        last = pe.matmul(half(0, c), w[0:EXPERTS, c * P:(c + 1) * P], r_gmatT, start=(c % 2 == 0),
                                         stop=False, skip_group_check=True)
                    last.then_inc(w_used, 1)
                for c in range(DT):
                    for tt in range(TT):
                        for k in range(TOP_K):
                            a = (tt * TOP_K + k) * D + c * P
                            last = pe.matmul(half(0, c)[:, tt * P:(tt + 1) * P], fetched[:, a:a + P],
                                             r_diag[:, (tt * TOP_K + k) * P:(tt * TOP_K + k + 1) * P],
                                             start=(level > 0 and c % 2 == 0 and tt == 0 and k == 0),
                                             stop=(k == TOP_K - 1), skip_group_check=True)
                last.then_inc(S["combined"], 1)

            expert_pass(0)
            combine(0)
            count = pe.value_load(r_cnt, min_val=0, max_val=T)
            with ExitStack() as nest:
                for level in range(1, PASSES):
                    nest.enter_context(pe.If(count > CAP * level))
                    pe.wait_ge(S["added"], 4 * level)
                    expert_pass(level)
                    combine(level)

            def ple(k, norm, reads):
                pe.wait_ge(x_ready, 4 * (norm - 1) + 4)
                n = first[f"proj{k}"]
                pe.wait_ge(p_loaded, 16 * (k + 1))
                for c in range(2):
                    w = chunk(n + c)
                    for e in range(DT):
                        last = pe.matmul(half(0, e), w[:, e * P:(e + 1) * P], tile(pT, c),
                                         start=(c == 0 and e % 2 == 0), stop=(c == 1), skip_group_check=True)
                    last.then_inc(w_used, 1)
                sum_squares(norm)
                dense(first[f"ple{k}"], hsrc, 4, h_ready, DT * reads)

            ple(0, 2, 2)
            sum_squares(3)

            sum_squares(4)
            dense(first["a_in"], hsrc, 0, h_ready, 3 * DT)
            dense(first["a_in"] + DT, hsrc, 4)
            for k, seg in enumerate(("w_r", "w_i")):
                w = chunk(first[seg])
                if k == 1:
                    pe.wait_ge(S["yg_ready"], 4)
                for h in range(DT):
                    if k == 0:
                        pe.wait_ge(S["conv_ready"], DT)
                    last = pe.matmul(half(4 * k, h), w[:, h * P:(h + 1) * P], tile(lru[0], h), start=True, stop=True)
                last.then_inc(w_used, 1)
            for c in range(4):
                pe.wait_ge(S["ri_ready"], 16)
            dense(first["a_out"], msrc, 0, S["gated_ready"], 0)

            def peer(L, norm, at):
                sum_squares(norm)
                dense(first[f"wq{L}"], hsrc, 0, h_ready, at)
                dense(first[f"wq{L}"] + DT, hsrc, 4)
                keys = [chunk(first[f"keys{L}"] + k) for k in range(2)]
                pe.wait_ge(S["pq_ready"], 8 * L + 8)
                for tt in range(TT):
                    for hp in range(16):
                        last = pe.matmul(ps[:, 4 * tt + hp // 4, (hp % 4) * P:(hp % 4 + 1) * P],
                                         tile(pq, hp)[:, tt * P:(tt + 1) * P],
                                         keys[hp // 8][:, (hp % 8) * P:(hp % 8 + 1) * P], start=True, stop=True)
                        if tt and hp % 8 == 7:
                            last.then_inc(w_used, 1)
                    if tt == 0:
                        last.then_inc(S["s_done"], 1)
                n = first[f"u{L}"]
                with pe.Fori(0, CHUNKS // RING) as i:
                    for k in range(RING):
                        m = n + k
                        pe.wait_ge(w_loaded[m % RING], 16 * (m // RING + 1) + i * 16)
                        if k % 2 == 0:
                            pe.wait_ge(S["bank_read"], READS * L + k // 2 + 1 + i * 4)
                        for c in range(DT):
                            last = pe.matmul(half(0, k), ring[:, m % RING, c * P:(c + 1) * P], hsrc(c),
                                             start=(c == 0), stop=(c == DT - 1))
                        last.then_inc(w_used, 1)
                pe.wait_ge(S["sel_done"], L + 1)
                for k in range(3):
                    for tt in range(TT):
                        src = (i12[:, (k * TT + tt) * P:(k * TT + tt + 1) * P] if k < 2 else cv[:, tt * P:(tt + 1) * P])
                        last = pe.transpose(ps[:, 4 + k, tt * P:(tt + 1) * P], src, ident)
                last.then_inc(S["selT_done"], 1)
                with pe.Fori(0, T // BODY) as i:
                    for s in range(BODY):
                        pe.wait_ge(S["oh_ready"], T * L + s + 1 + i * BODY)
                        pe.matmul(ps[:, 4 + s // GROUP, (s % GROUP) * P:(s % GROUP + 1) * P],
                                  mT[:, s * P:(s + 1) * P], mT[:, (BODY + s) * P:(BODY + s + 1) * P],
                                  start=True, stop=True).then_inc(S["g_done"], 1)
                pe.wait_ge(S["g_used"], 64 * L + 64)
                for e in range(DT):
                    pe.matmul(half(0, e), ident, tile(xT, e), start=(e % 2 == 0), stop=False, skip_group_check=True)
                n = first[f"v{L}"]
                with pe.Fori(0, CHUNKS // RING) as i:
                    for k in range(RING):
                        m = n + k
                        pe.wait_ge(w_loaded[m % RING], 16 * (m // RING + 1) + i * 16)
                        for e in range(DT):
                            last = pe.matmul(half(0, e), ring[:, m % RING, e * P:(e + 1) * P],
                                             big[:, bass.ds(i * (RING * T) + k * T, T)],
                                             start=False, stop=True, skip_group_check=True)
                        last.then_inc(w_used, 1)

            peer(0, 5, 4 * DT)
            ple(1, 6, 5)

            sum_squares(7)
            dense(first["kv"], hsrc, 0, h_ready, 6 * DT)
            token_major(first["kv"] + DT, hT, h_ready, 6 * DT, 0, [[ps[:, 4 + 2 * tt + k, :] for k in range(2)] for tt in range(TT)])
            pe.wait_ge(S["k2_ready"], 4)
            dense(first["bq"], msrc, 0, h_ready, 7 * DT)

            def logits(h):
                lo = 64 * (h % 2)
                q, k = tile(q2, h // 2), tile(k2, h // 2)
                if h == 0:
                    pe.wait_ge(S["q2_ready"], 4)
                    pe.wait_ge(S["v2_ready"], 4)
                if h >= 4:
                    pe.wait_ge(S["arg_ready"], h - 3)
                z = ps[:, h % 4, 0:SPAN]
                pe.matmul(z[:, 0:T], k[lo:lo + DH, 0:P], q[lo:lo + DH, 0:T], start=True, stop=True)
                pe.matmul(z[:, T:SPAN], k[lo:lo + DH, P:T], q[lo:lo + DH, P:T], start=True, stop=True)\
                    .then_inc(S["z_done"], 1)

            def suffix(h):
                g = h % 4
                pe.wait_ge(S["spm_ready"], h + 1)
                if h >= 2:
                    pe.wait_ge(S["arg_ready"], h - 1)
                r = ps[:, 4 + h % 2, 0:SPAN]
                pe.matmul(r[:, 0:P], ntri, st[8 + g][:, 0:P], start=True, stop=True)
                pe.matmul(r[:, P:T], ntri, st[4 + g][:, P:T], start=True, stop=False)
                pe.matmul(r[:, P:T], nones, st[8 + g][:, T:SPAN], start=False, stop=True)
                pe.matmul(r[:, T:SPAN], ntri, st[8 + g][:, T:SPAN], start=True, stop=True).then_inc(S["rc_done"], 1)

            def heads_out(h):
                lo, g = 64 * (h % 2), h % 4
                pe.wait_ge(S["a_ready"], h + 1)
                if h >= 4:
                    pe.wait_ge(S["o_ready"], h - 3)
                o = ps[lo:lo + DH, 6 + (h // 2) % 2, 0:T]
                v = [v2[:, tt * D + h * DH:tt * D + (h + 1) * DH] for tt in range(TT)]
                a = st[12 + g]
                pe.matmul(o[:, 0:P], v[0], a[:, 0:P], start=True, stop=True)
                pe.matmul(o[:, P:T], v[0], a[:, P:T], start=True, stop=False)
                pe.matmul(o[:, P:T], v[1], a[:, T:SPAN], start=False, stop=True).then_inc(S["o_done"], 1)

            for g in range(HEADS2 // 4 + 1):
                for h in range(4 * g, 4 * g + 4):
                    if g < HEADS2 // 4:
                        logits(h)
                    if g >= 1:
                        heads_out(h - 4)
                if g < HEADS2 // 4:
                    for h in range(4 * g, 4 * g + 4):
                        suffix(h)
            pe.wait_ge(S["o_ready"], HEADS2)
            dense(first["bo"], msrc, 0)
            peer(1, 8, 8 * DT)
            ple(2, 9, 9)
            sum_squares(10)

        @block.scalar
        def _(act):
            step = Tally(act, act_step)

            def squares(k):
                if k == 0:
                    act.wait_ge(x_loaded, 16)
                for j in range(4):
                    if k:
                        act.wait_ge(x_ready, 4 * (k - 1) + j + 1)
                    act.activation(tile(mT, j, 512), tile(xT, j, 512), ACT.Square).then_inc(sq_ready, 1)
                act.wait_ge(ss_done, k + 1)
                act.activation(rs[:, 0:T], ps[:, 7, 0:T], ACT.Sqrt, scale=1.0 / D, bias=eps[:, :])\
                    .then_inc(rms_ready, 1)

            act.wait_ge(eps_ready, 1)
            squares(0)
            used_through(act, "w_in", 8)
            for g in range(4):
                act.copy(upad[:, g * (PAD + T) + PAD:(g + 1) * (PAD + T)], half(0, g)).then_inc(S["u_copied"], 1)
            for b in range(2):
                act.copy(tile(q1, b, 512), ps[:, 2 + b, :]).then_inc(S["qk_ready"], 1)
            used_through(act, "w_in", 16)
            for b in range(2):
                act.copy(tile(k1, b, 512), ps[:, 4 + b, :]).then_inc(S["qk_ready"], 1)

            def exps(h):
                act.wait_ge(S["biased"], h + 1)
                n = stat1[:, 6 * (h % 8):6 * (h % 8) + 6]
                p = prob[h % 2]
                act.activation(p[:, 0:P], p[:, 0:P], ACT.Exp, bias=n[:, 0:1], accum_out=n[:, 2:3])
                act.activation(p[:, P:SPAN], p[:, P:SPAN], ACT.Exp, bias=n[:, 1:2], accum_out=n[:, 3:4])\
                    .then_inc(S["prob_exp"], 1)

            def copy_pt(h):
                act.wait_ge(S["pt_done"], h + 1)
                if h >= 2:
                    act.wait_ge(S["pv_done"], h - 1)
                act.copy(probT[h % 2], ps[:, 2 + h % 2, 0:SPAN]).then_inc(S["pt_ready"], 1)

            def copy_o(h):
                lo = 64 * (h % 2)
                act.wait_ge(S["pv_done"], h + 1)
                if h == 0:
                    for k in range(2):
                        act.wait_ge(row_stored[k], 16 * (HEADS1 // 2))
                act.copy(tile(mT, 4 + h // 2)[lo:lo + DH, :], ps[lo:lo + DH, 4 + (h // 2) % 2, 0:T])\
                    .then_inc(S["mix_ready"], 1)

            for s in range(HEADS1 + 2):
                if s < HEADS1:
                    exps(s)
                if 1 <= s <= HEADS1:
                    copy_pt(s - 1)
                if s >= 2:
                    copy_o(s - 2)
            used_through(act, "w_pool", 1)
            for g in range(4):
                act.activation(tile(mT, g), half(6, g), ACT.Copy, scale=col("pool_scale", g)).then_inc(S["mix_ready"], 1)

            squares(1)
            for tt in range(TT):
                act.wait_ge(S["htok_done"], tt + 1)
                for b in range(2):
                    act.copy(mT[:, tt * D + b * BANK:tt * D + (b + 1) * BANK], ps[:, 2 * tt + b, :])\
                        .then_inc(S["htok_ready"], 1)
            for tt in range(TT):
                act.wait_ge(S["neg_top"], tt + 1)
                act.activation(r_exp[:, tt * 4:tt * 4 + 4], r_max[:, tt * 8:tt * 8 + 4], ACT.Exp,
                               bias=r_nmax[:, tt:tt + 1], accum_out=r_sum[:, tt:tt + 1]).then_inc(S["gate_exp"], 1)

            def expert_pass(level):
                base = EXPERTS * level

                def gathered(count):
                    act.wait_ge(S["gathered"], count)
                    for b in range(2):
                        act.copy(tile(m_xg, b, 512), ps[:, b, :]).then_inc(S["xg_ready"], 1)

                def expert(e):
                    n = e + base
                    for b in range(2):
                        act.wait_ge(S["sig_in"], n * 2 + b + 1)
                        act.activation(tile(m_sig, b, 512), tile(m_g, b, 512), ACT.Sigmoid, scale=ALPHA)\
                            .then_inc(S["sig_ready"], 1)
                    gathered(e + 33 * level + 2)
                    act.wait_ge(S["moe_used"], n * MOE_SLOTS + MOE_SLOTS)
                    for b in range(2):
                        act.copy(tile(m_y, b, 512), ps[:, 6 + b, :]).then_inc(S["y_ready"], 1)
                    if level or not isinstance(e, int):
                        act.wait_ge(S["y_stored"], n * 16)
                    for b in range(2):
                        act.wait_ge(S["yt_done"], n * 2 + b + 1)
                        act.copy(tile(m_tok, b, 512), ps[:, b, :]).then_inc(S["ytok_ready"], 1)
                    act.wait_ge(S["ytok_ready"], n * 2 + 2)
                    act.dma_start(expert_out[bass.ds(e * CAP, CAP), :], m_tok).then_inc(S["y_stored"], 16)

                gathered(33 * level + 1)
                if level == 0:
                    expert(0)
                with act.Fori(0 if level else 1, EXPERTS) as e:
                    expert(e)

            expert_pass(0)
            act.wait_ge(S["count_ready"], 1)
            count = act.value_load(r_cnt, min_val=0, max_val=T)
            with ExitStack() as nest:
                for level in range(1, PASSES):
                    nest.enter_context(act.If(count > CAP * level))
                    expert_pass(level)

            def ple(k, norm):
                squares(norm)
                used_through(act, f"ple{k}", 8)
                for b in range(4):
                    act.activation(tile(mT, b, 512), ps[:, 4 + b, :], ACT.Sigmoid).then_inc(S["gate_ready"], 1)

            ple(0, 2)
            squares(3)

            squares(4)
            act.wait_ge(S["lam_in"], 1)
            act.activation(sp[:, 8:16], sp[:, 0:8], ACT.Exp, scale=-1.0).then_inc(S["lam_exp"], 1)
            used_through(act, "a_in", 16)
            for b in range(4):
                act.activation(tile(lru[1], b, 512), ps[:, 4 + b, :], ACT.Gelu_apprx_tanh).then_inc(S["yg_ready"], 1)
            for k, name in enumerate(("b_r", "b_i")):
                used_through(act, ("w_r", "w_i")[k], 1)
                for h in range(DT):
                    act.activation(tile(lru[2 + k], h), half(4 * k, h), ACT.Sigmoid, bias=col(name, h))\
                        .then_inc(S["ri_ready"], 1)
            act.wait_ge(S["ri_ready"], 16)
            act.wait_ge(S["lam_in"], 2)
            for h in range(DT):
                act.activation(tile(lru[4], h), tile(lru[2], h), ACT.Exp, scale=sp[:, 72 + h:73 + h])
                act.activation(tile(lru[5], h), tile(lru[2], h), ACT.Tanh, scale=sp[:, 80 + h:81 + h])\
                    .then_inc(S["lru_exp"], 1)
            for b in range(4):
                act.wait_ge(S["lru_e"], b + 1)
                act.activation(tile(lru[6], b, 512), tile(lru[5], b, 512), ACT.Sqrt).then_inc(S["lru_sqrt"], 1)

            def peer(L, norm):
                squares(norm)
                for k in range(2):
                    used_through(act, f"wq{L}", 8 * (k + 1))
                    for b in range(4):
                        act.copy(pq[:, (4 * k + b) * 512:(4 * k + b + 1) * 512], ps[:, 4 * k + b, :])\
                            .then_inc(S["pq_ready"], 1)
                act.wait_ge(S["s_done"], L + 1)
                for b in range(4):
                    act.copy(tile(mT, b, 512), ps[:, b, :]).then_inc(S["bank_read"], 1)
                n = first[f"u{L}"]
                with act.Fori(0, CHUNKS // RING) as i:
                    for k in range(RING // 2):
                        act.wait_ge(w_used, n + 2 * k + 2 + i * RING)
                        act.activation(big[:, bass.ds(i * (RING * T) + k * BANK, BANK)], ps[:, k, :],
                                       ACT.Gelu_apprx_tanh).then_inc(S["bank_read"], 1)
                act.wait_ge(S["cv_ready"], L + 1)
                act.activation(cv, cv, ACT.Exp).then_inc(S["cv_exp"], 1)

            peer(0, 5)
            ple(1, 6)

            squares(7)
            used_through(act, "kv", 8)
            for b in range(4):
                act.copy(tile(k2, b, 512), ps[:, b, :]).then_inc(S["k2_ready"], 1)
            used_through(act, "bq", 8)
            for b in range(4):
                act.activation(tile(q2, b, 512), ps[:, b, :], ACT.Copy, scale=DH ** -0.5).then_inc(S["q2_ready"], 1)
            for g in range(HEADS2 // 4 + 1):
                if g < HEADS2 // 4:
                    for h in range(4 * g, 4 * g + 4):
                        a = st[h % 4]
                        act.wait_ge(S["z_done"], h + 1)
                        step.link(act.activation(a, ps[:, h % 4, 0:SPAN], ACT.Abs))
                        step.link(act.activation(a, a, ACT.Exp, scale=-1.0))
                        if h >= 4:
                            act.wait_ge(S["spm_ready"], h - 3)
                        act.activation(st[16 + h % 4], a, ACT.Ln, bias=1.0).then_inc(S["a_exp"], 1)
                    for h in range(4 * g, 4 * g + 4):
                        act.wait_ge(S["arg_ready"], h + 1)
                        if h >= 4:
                            act.wait_ge(S["o_done"], h - 3)
                        act.activation(st[12 + h % 4], st[20 + h % 4], ACT.Exp).then_inc(S["w_exp"], 1)
                if g < HEADS2 // 4:
                    for h in range(4 * g, 4 * g + 4):
                        lo = 64 * (h % 2)
                        act.wait_ge(S["o_done"], h + 1)
                        act.copy(tile(mT, h // 2)[lo:lo + DH, :], ps[lo:lo + DH, 6 + (h // 2) % 2, 0:T])\
                            .then_inc(S["o_ready"], 1)
            peer(1, 8)
            ple(2, 9)
            squares(10)

        @block.vector
        def _(dve):
            step = Tally(dve, dve_step)
            link, mark = step.link, step.mark

            def norm(k, gains, dsts=(hT,), sem_=h_ready):
                dve.wait_ge(rms_ready, k + 1)
                link(dve.reciprocal(rs[:, T:2 * T], rs[:, 0:T]))
                for dst, (name, at) in zip(dsts, gains):
                    for c in range(DT):
                        dve.scalar_tensor_tensor(tile(dst, c), tile(xT, c), col(name, at + c), rs[:, T:2 * T],
                                                 op0=ALU.mult, op1=ALU.mult).then_inc(sem_, 1)

            def add_to_x(seg, chunks):
                used_through(dve, seg, chunks)
                for b in range(4):
                    dve.tensor_tensor(tile(xT, b, 512), ps[:, b, :], tile(xT, b, 512), ALU.add).then_inc(x_ready, 1)

            dve.memset(eps[:, :], EPS).then_inc(eps_ready, 1)
            dve.wait_ge(attn_loaded, 48)
            dve.wait_ge(con_loaded, 16)
            for h in range(HEADS1):
                dve.tensor_scalar(rb[:, h * P:(h + 1) * P], ones[0:32, :], relb[:, h:h + 1], None, ALU.mult)\
                    .then_inc(S["rb_ready"], 1)
            dve.memset(upad, 0.0).then_inc(dve_step, 1)
            step.n += 1
            dve.wait_ge(x_loaded, 16)
            dve.wait_ge(par_loaded, 16)
            norm(0, [("g_mix", 0)])
            dve.wait_ge(h_ready, DT)
            for h in range(HEADS1):
                dve.wait_ge(S["row_done"], h + 1)
                if h >= 2:
                    dve.wait_ge(row_stored[h % 2], 16 * (h // 2))
                dve.tensor_tensor(row[h % 2], ps[:, 4 + h % 2, 0:SPAN], cmask, ALU.add).then_inc(S["row_ready"], 1)
            dve.wait_ge(S["u_copied"], 4)
            up = upad.rearrange("p (g t) -> p g t", g=4)
            s0 = winsum.rearrange("p (g t) -> p g t", g=4)
            s1 = winsum2.rearrange("p (g t) -> p g t", g=4)
            E = PAD + T
            link(dve.tensor_tensor(s0[:, :, 1:E], up[:, :, 1:E], up[:, :, 0:E - 1], ALU.add))
            link(dve.tensor_tensor(s1[:, 1:4, 3:E], s0[:, 1:4, 3:E], s0[:, 1:4, 1:E - 2], ALU.add))
            link(dve.tensor_tensor(s0[:, 2:4, 7:E], s1[:, 2:4, 7:E], s1[:, 2:4, 3:E - 4], ALU.add))
            link(dve.tensor_tensor(s1[:, 3, 15:E], s0[:, 3, 15:E], s0[:, 3, 7:E - 8], ALU.add))
            for g, w in enumerate(POOL_WINDOWS):
                s = (s0, s1)[g % 2][:, g, PAD:E]
                link(dve.tensor_scalar(s[:, PAD:T], s[:, PAD:T], 1.0 / w, None, ALU.mult))
                link(dve.tensor_tensor(s[:, 0:PAD], s[:, 0:PAD], con[:, C_INV + g * PAD:C_INV + (g + 1) * PAD], ALU.mult))
                dve.tensor_tensor(up[:, g, PAD:E], s, up[:, g, PAD:E], ALU.subtract).then_inc(S["pooled_ready"], 1)
            used_through(dve, "w_in", 16)
            for tt in range(TT):
                dve.tensor_copy(tile(v1, tt, 512), ps[:, 6 + tt, :]).then_inc(S["v_ready"], 1)

            def biased(h):
                dve.wait_ge(S["score_done"], h + 1)
                dve.wait_ge(S["toep_loaded"], 32 * HEADS1)
                if h >= 2:
                    dve.wait_ge(S["pt_done"], h - 1)
                n = stat1[:, 6 * h:6 * h + 6]
                p = prob[h % 2]
                link(dve.scalar_tensor_tensor(p, ps[:, h % 2, 0:SPAN], DH ** -0.5, toep[:, h * SPAN:(h + 1) * SPAN],
                                              op0=ALU.mult, op1=ALU.add))
                mark(dve.tensor_reduce(n[:, 4:5], p[:, 0:P], AX_X, ALU.max))
                link(dve.tensor_reduce(n[:, 5:6], p[:, P:SPAN], AX_X, ALU.max))
                dve.tensor_scalar(n[:, 0:2], n[:, 4:6], -1.0, None, ALU.mult).then_inc(S["biased"], 1)

            def normalised(h):
                n = stat1[:, 6 * h:6 * h + 6]
                p = prob[h % 2]
                dve.wait_ge(S["prob_exp"], h + 1)
                link(dve.reciprocal(n[:, 4:6], n[:, 2:4]))
                link(dve.tensor_scalar(p[:, 0:P], p[:, 0:P], n[:, 4:5], None, ALU.mult))
                dve.tensor_scalar(p[:, P:SPAN], p[:, P:SPAN], n[:, 5:6], None, ALU.mult).then_inc(S["prob_ready"], 1)

            for s in range(HEADS1 + 1):
                if s < HEADS1:
                    biased(s)
                if s >= 1:
                    normalised(s - 1)
            add_to_x("w_out", 8)

            norm(1, [("g_ffn", 0)])
            used_through(dve, "w_router", 1)
            dve.wait_ge(bias_loaded, 32)
            i32c = iota[:, 0:EXPERTS]
            for tt in range(TT):
                lg = r_logit[:, tt * 32:(tt + 1) * 32]
                top, idx = r_max[:, tt * 8:tt * 8 + 8], r_idx[:, tt * 8:tt * 8 + 8].bitcast(U32)
                link(dve.tensor_tensor(lg, ps[:, 4, tt * 32:(tt + 1) * 32], r_bias, ALU.add))
                link(dve.max(top, lg))
                dve.tensor_scalar(r_nmax[:, tt:tt + 1], top[:, 0:1], -1.0, None, ALU.mult).then_inc(S["neg_top"], 1)
                link(dve.max_index(idx, top, lg))
                link(dve.tensor_copy(r_idxf[:, tt * 4:tt * 4 + 4], idx[:, 0:4]))
                hots = r_hot[:, tt * 128:(tt + 1) * 128].rearrange("p (k e) -> p k e", k=TOP_K)
                for k in range(TOP_K):
                    mark(dve.tensor_scalar(hots[:, k, :], i32c, r_idxf[:, tt * 4 + k:tt * 4 + k + 1], None, ALU.is_equal))
                step.wait()
                dve.tensor_reduce(r_mask[:, tt * 32:(tt + 1) * 32], hots.rearrange("p k e -> p e k"), AX_X, ALU.add)\
                    .then_inc(S["mask_ready"], 1)
            for tt in range(TT):
                dve.wait_ge(S["gate_exp"], tt + 1)
                gate = r_gate[:, tt * 4:tt * 4 + 4]
                link(dve.reciprocal(r_rec[:, tt:tt + 1], r_sum[:, tt:tt + 1]))
                link(dve.tensor_scalar(gate, r_exp[:, tt * 4:tt * 4 + 4], r_rec[:, tt:tt + 1], None, ALU.mult))
                gm = r_gmat[:, tt * 32:(tt + 1) * 32]
                hot_k = lambda k: r_hot[:, tt * 128 + k * 32:tt * 128 + (k + 1) * 32]
                link(dve.tensor_scalar(gm, hot_k(0), gate[:, 0:1], None, ALU.mult))
                for k in range(1, TOP_K):
                    ins = dve.scalar_tensor_tensor(gm, hot_k(k), gate[:, k:k + 1], gm, op0=ALU.mult, op1=ALU.add)
                    if k < TOP_K - 1:
                        link(ins)
                    else:
                        ins.then_inc(S["gmat_in"], 1)
            dve.wait_ge(S["rank_done"], 1)
            link(dve.tensor_reduce(r_cntf, ps[0:1, 5, 64:96], AX_X, ALU.max))
            dve.tensor_copy(r_cnt, r_cntf).then_inc(S["count_ready"], 1)
            for tt in range(TT):
                rank, mask = ps[:, 5, tt * 32:(tt + 1) * 32], r_mask[:, tt * 32:(tt + 1) * 32]
                link(dve.memset(r_rank1[:, tt * 33 + 32:tt * 33 + 33], 0.0))
                link(dve.scalar_tensor_tensor(r_rank1[:, tt * 33:tt * 33 + 32], rank, 1.0, mask,
                                              op0=ALU.add, op1=ALU.mult))
                hots = r_hot[:, tt * 128:(tt + 1) * 128].rearrange("p (k e) -> p k e", k=TOP_K)
                tmp = r_tmp[:, tt * 128:(tt + 1) * 128].rearrange("p (k e) -> p k e", k=TOP_K)
                link(dve.tensor_tensor(tmp, rank.unsqueeze(1).broadcast_to((P, TOP_K, EXPERTS)), hots, ALU.mult))
                link(dve.tensor_reduce(r_slotf[:, tt * 4:tt * 4 + 4], tmp, AX_X, ALU.add))
            link(dve.tensor_scalar(r_pass, r_slotf, float(CAP), None, ALU.is_ge))
            for level in range(2, PASSES):
                link(dve.tensor_scalar(r_step, r_slotf, float(CAP * level), None, ALU.is_ge))
                link(dve.tensor_tensor(r_pass, r_pass, r_step, ALU.add))
            link(dve.scalar_tensor_tensor(r_slotf, r_pass, -float(CAP), r_slotf, op0=ALU.mult, op1=ALU.add))
            link(dve.scalar_tensor_tensor(r_slotf, r_idxf, float(CAP), r_slotf, op0=ALU.mult, op1=ALU.add))
            dve.tensor_copy(r_slot, r_slotf).then_inc(S["slots_ready"], 1)

            def diagonals(level, link):
                link(dve.scalar_tensor_tensor(r_step, r_pass, float(level), r_gate, op0=ALU.is_equal, op1=ALU.mult))
                for k in range(TT * TOP_K):
                    dve.tensor_scalar(r_diag[:, k * P:(k + 1) * P], ident, r_step[:, k:k + 1], None, ALU.mult)\
                        .then_inc(S["diag_ready"], 1)

            diagonals(0, link)
            dve.wait_ge(S["gmat_done"], 1)
            dve.tensor_copy(r_gmatT, ps[0:32, 6, 0:T]).then_inc(S["gmat_ready"], 1)

            moe = Tally(dve, S["moe_step"])

            def expert_pass(level):
                def select(e):
                    for tt in range(TT):
                        ins = dve.tensor_scalar(m_sel[:, tt * CAP:(tt + 1) * CAP], iota[:, 0:CAP],
                                                float(level * CAP + 1), r_rank1[:, bass.ds(e + tt * 33, 1)],
                                                ALU.add, ALU.is_equal)
                    ins.then_inc(S["sel_ready"], 1)

                select(0)
                with dve.Fori(0, EXPERTS) as e:
                    moe.enter(e, 8)
                    n = e + EXPERTS * level if level else e
                    dve.wait_ge(S["gathered"], e + 33 * level + 1)
                    select(e + 1)
                    dve.wait_ge(S["moe_used"], n * MOE_SLOTS + DT)
                    for b in range(2):
                        g, u, sig, h = (tile(x, b, 512) for x in (m_g, m_u, m_sig, m_h))
                        three = lambda x: x.rearrange("p (f n) -> p f n", n=CAP)
                        bias = lambda k: moe_bias[:, bass.ds(e * 16 + k, 4)].unsqueeze(2).broadcast_to((P, 4, CAP))
                        moe.link(dve.tensor_tensor(three(g), three(ps[:, 2 + b, :]), bias(4 * b), ALU.add))
                        dve.tensor_scalar(g, g, LIMIT, None, ALU.min).then_inc(S["sig_in"], 1)
                        moe.link(dve.tensor_tensor(three(u), three(ps[:, 4 + b, :]), bias(8 + 4 * b), ALU.add))
                        moe.link(dve.tensor_scalar(u, u, LIMIT, -LIMIT, ALU.min, ALU.max))
                        dve.wait_ge(S["sig_ready"], n * 2 + b + 1)
                        moe.link(dve.tensor_tensor(sig, sig, g, ALU.mult))
                        dve.scalar_tensor_tensor(h, u, 1.0, sig, op0=ALU.add, op1=ALU.mult).then_inc(S["hid_ready"], 1)
                moe.leave(EXPERTS)

            expert_pass(0)
            dve.wait_ge(S["count_ready"], 1)
            count = dve.value_load(r_cnt, min_val=0, max_val=T)
            with ExitStack() as nest:
                for level in range(1, PASSES):
                    nest.enter_context(dve.If(count > CAP * level))
                    dve.wait_ge(S["combined"], level)
                    for b in range(4):
                        dve.tensor_tensor(tile(xT, b, 512), ps[:, b, :], tile(xT, b, 512), ALU.add)\
                            .then_inc(S["added"], 1)
                    diagonals(level, moe.link)
                    expert_pass(level)
            dve.wait_ge(S["combined"], 1)
            with ExitStack() as nest:
                for level in range(1, PASSES):
                    nest.enter_context(dve.If(count > CAP * level))
                    dve.wait_ge(S["combined"], level + 1)
            for b in range(4):
                dve.tensor_tensor(tile(xT, b, 512), ps[:, b, :], tile(xT, b, 512), ALU.add).then_inc(x_ready, 1)

            def ple(k, norm_no, gain):
                norm(norm_no, [gain])
                for b in range(4):
                    dve.wait_ge(S["gate_ready"], 4 * k + b + 1)
                    link(dve.tensor_tensor(tile(mT, b, 512), ps[:, b, :], tile(mT, b, 512), ALU.mult))
                    dve.tensor_tensor(tile(xT, b, 512), tile(mT, b, 512), tile(xT, b, 512), ALU.add).then_inc(x_ready, 1)

            ple(0, 2, ("g_ple", 0))
            dve.wait_ge(rms_ready, 4)
            link(dve.reciprocal(rs[:, T:2 * T], rs[:, 0:T]))
            for c in range(DT):
                ins = dve.scalar_tensor_tensor(tile(xT, c), tile(xT, c), col("g_final", c), rs[:, T:2 * T],
                                               op0=ALU.mult, op1=ALU.mult)
                if c % 2:
                    ins.then_inc(x_ready, 1)

            norm(4, [("norm_mix", 0)])
            lam = par[:, PARAMS["lam"][0]:PARAMS["lam"][0] + DT]
            link(dve.tensor_scalar(sp[:, 16:24], lam, -1.0, None, ALU.mult))
            dve.tensor_tensor(sp[:, 0:8], lam, sp[:, 16:24], ALU.max).then_inc(S["lam_in"], 1)
            dve.wait_ge(S["lam_exp"], 1)
            y, z, z2, acc = sp[:, 8:16], sp[:, 24:32], sp[:, 32:40], sp[:, 40:48]
            link(dve.tensor_scalar(z, y, 2.0, None, ALU.add))
            link(dve.reciprocal(z2, z))
            link(dve.tensor_tensor(z, y, z2, ALU.mult))
            link(dve.tensor_tensor(z2, z, z, ALU.mult))
            link(dve.tensor_scalar(acc, z2, 1.0 / 17, 1.0 / 15, ALU.mult, ALU.add))
            for k in (13, 11, 9, 7, 5, 3, 1):
                link(dve.tensor_tensor(acc, acc, z2, ALU.mult))
                link(dve.tensor_scalar(acc, acc, 1.0 / k, None, ALU.add))
            link(dve.tensor_tensor(acc, acc, z, ALU.mult))
            link(dve.tensor_scalar(sp[:, 16:24], sp[:, 16:24], 0.0, None, ALU.max))
            link(dve.scalar_tensor_tensor(acc, acc, 2.0, sp[:, 16:24], op0=ALU.mult, op1=ALU.add))
            link(dve.tensor_scalar(sp[:, 72:80], acc, -8.0, None, ALU.mult))
            dve.tensor_scalar(sp[:, 80:88], acc, 8.0, None, ALU.mult).then_inc(S["lam_in"], 1)
            used_through(dve, "a_in", 8)
            marks = [mark(dve.tensor_scalar(tile(lru[0], c), half(0, c), col("conv_w", 3 * DT + c), col("conv_b", c),
                                            ALU.mult, ALU.add)) for c in range(DT)]
            for back in range(1, CONV):
                for c in range(DT):
                    step.wait(marks[c])
                    dst = tile(lru[0], c)[:, back:T]
                    ins = dve.scalar_tensor_tensor(dst, half(0, c)[:, 0:T - back], col("conv_w", (3 - back) * DT + c), dst,
                                                   op0=ALU.mult, op1=ALU.add)
                    if back < CONV - 1:
                        marks[c] = mark(ins)
                    else:
                        ins.then_inc(S["conv_ready"], 1)
            dve.wait_ge(S["conv_ready"], DT)
            for b in range(4):
                dve.wait_ge(S["lru_exp"], 2 * b + 2)
                a, th = tile(lru[4], b, 512), tile(lru[5], b, 512)
                link(dve.tensor_tensor(tile(lru[6], b, 512), a, a, ALU.mult))
                dve.scalar_tensor_tensor(th, tile(lru[6], b, 512), 1.0, th, op0=ALU.add, op1=ALU.mult)\
                    .then_inc(S["lru_e"], 1)
            for b in range(4):
                dve.wait_ge(S["ri_ready"], 16)
                link(dve.tensor_tensor(tile(lru[3], b, 512), tile(lru[3], b, 512), tile(lru[0], b, 512), ALU.mult))
                dve.wait_ge(S["lru_sqrt"], b + 1)
                link(dve.tensor_tensor(tile(lru[3], b, 512), tile(lru[3], b, 512), tile(lru[6], b, 512), ALU.mult))
                for c in (2 * b, 2 * b + 1):
                    link(dve.tensor_tensor_scan(tile(lru[7], c), tile(lru[4], c), tile(lru[3], c), 0.0,
                                                ALU.mult, ALU.add))
                    dve.tensor_tensor(tile(mT, c), tile(lru[7], c), tile(lru[1], c), ALU.mult)\
                        .then_inc(S["gated_ready"], 1)
            add_to_x("a_out", 8)

            def top16(vals, idx, src, tmp):
                link(dve.max(vals[:, 0:8], src))
                mark(dve.max_index(idx[:, 0:8], vals[:, 0:8], src))
                link(dve.match_replace(tmp, vals[:, 0:8], src, -3e38))
                link(dve.max(vals[:, 8:16], tmp))
                link(dve.max_index(idx[:, 8:16], vals[:, 8:16], tmp))

            def peer(L, norm_no, gain):
                norm(norm_no, [gain])
                for tt in (1, 0):
                    used_through(dve, f"keys{L}", 2)
                    if tt == 0:
                        dve.wait_ge(S["bank_read"], READS * L + 4)
                    for hp in range(16):
                        src = ps[:, 4 + hp // 4, (hp % 4) * P:(hp % 4 + 1) * P] if tt else mT[:, hp * P:(hp + 1) * P]
                        top16(sv[:, hp * 16:hp * 16 + 16], si[:, hp * 16:hp * 16 + 16], src, p_tmp)
                    link(dve.tensor_copy(sif, si))
                    vals = cv[:, tt * P:(tt + 1) * P]
                    for h in range(PH):
                        a = sv[:, 32 * h:32 * h + 16].unsqueeze(2).broadcast_to((P, 16, 16))
                        b = sv[:, 32 * h + 16:32 * h + 32].unsqueeze(1).broadcast_to((P, 16, 16))
                        link(dve.tensor_tensor(cand.rearrange("p (a b) -> p a b", a=16), a, b, ALU.add))
                        top16(vals[:, h * 16:h * 16 + 16], ci[:, h * 16:h * 16 + 16], cand, cand2)
                    for which in range(2):
                        if which == 0:
                            link(dve.tensor_scalar(cc, ci, 4, None, ALU.logical_shift_right))
                        else:
                            link(dve.tensor_scalar(cc, ci, 15, None, ALU.bitwise_and))
                        link(dve.tensor_copy(ccf, cc))
                        place = iota[:, 0:16].unsqueeze(1).broadcast_to((P, P, 16))
                        pk = pick.rearrange("p (k i) -> p k i", i=16)
                        link(dve.tensor_tensor(pk, ccf.unsqueeze(2).broadcast_to((P, P, 16)), place, ALU.is_equal))
                        for h in range(PH):
                            ids = sif[:, 32 * h + 16 * which:32 * h + 16 * which + 16]
                            mark(dve.tensor_tensor(pk[:, h * 16:h * 16 + 16, :], pk[:, h * 16:h * 16 + 16, :],
                                                   ids.unsqueeze(1).broadcast_to((P, 16, 16)), ALU.mult))
                        step.wait()
                        link(dve.tensor_reduce(i12[:, (which * TT + tt) * P:(which * TT + tt + 1) * P], pk, AX_X, ALU.add))
                    v3 = vals.rearrange("p (h k) -> p h k", h=PH)
                    link(dve.tensor_copy(p_sum[:, 0:8], v3[:, :, 0]))
                    ins = dve.tensor_tensor(v3, v3, p_sum[:, 0:8].unsqueeze(2).broadcast_to((P, PH, 16)), ALU.subtract)
                    if tt:
                        link(ins)
                    else:
                        ins.then_inc(S["cv_ready"], 1)
                dve.wait_ge(S["cv_exp"], L + 1)
                c3 = cv.rearrange("p (h k) -> p h k", k=16)
                link(dve.tensor_reduce(p_sum, c3, AX_X, ALU.add))
                link(dve.reciprocal(p_sum, p_sum))
                dve.tensor_tensor(c3, c3, p_sum.unsqueeze(2).broadcast_to((P, 2 * PH, 16)), ALU.mult)\
                    .then_inc(S["sel_done"], 1)
                dve.wait_ge(S["selT_done"], L + 1)
                for k in range(3):
                    dve.tensor_copy(selT[:, k * T:(k + 1) * T], ps[:, 4 + k, 0:T]).then_inc(S["selT_ready"], 1)
                dve.wait_ge(S["selT_ready"], 3 * L + 3)
                dve.wait_ge(S["bank_read"], READS * (L + 1))
                act3 = big[:, :].rearrange("p (j t) -> p j t", t=T)
                with dve.Fori(0, T // BODY) as i:
                    for s in range(BODY):
                        t = i * BODY + s
                        dve.tensor_scalar(mT[:, s * P:(s + 1) * P], iota, selT[:, bass.ds(t, 1)], None, ALU.is_equal)
                        dve.tensor_scalar(mT[:, (BODY + s) * P:(BODY + s + 1) * P], iota, selT[:, bass.ds(t + T, 1)],
                                          selT[:, bass.ds(t + 2 * T, 1)], ALU.is_equal, ALU.mult)\
                            .then_inc(S["oh_ready"], 1)
                    for g in range(BODY // GROUP):
                        dve.wait_ge(S["g_done"], T * L + (g + 1) * GROUP + i * BODY)
                        dst = act3[:, :, bass.ds(i * BODY + g * GROUP, GROUP)]
                        dve.tensor_tensor(dst, ps[:, 4 + g, :].rearrange("p (t j) -> p j t", t=GROUP), dst, ALU.mult)\
                            .then_inc(S["g_used"], 1)
                used_through(dve, f"v{L}", CHUNKS)
                for b in range(4):
                    dve.tensor_copy(tile(xT, b, 512), ps[:, b, :]).then_inc(x_ready, 1)

            peer(0, 5, ("norm_ffn", 0))
            ple(1, 6, ("norm_ple", 0))

            norm(7, [("kv_norm", 0), ("norm_mix", DT)], (hT, mT))
            used_through(dve, "kv", 16)
            for b in range(4):
                dve.tensor_copy(tile(v2, b, 512), ps[:, 4 + b, :]).then_inc(S["v2_ready"], 1)
            mask2 = triu.unsqueeze(1).broadcast_to((P, 2, P))
            diag = lambda x: x.rearrange("p (k t) -> p k t", k=3)[:, 0:3:2, :]
            for g in range(HEADS2 // 4):
                for h in range(4 * g, 4 * g + 4):
                    dve.wait_ge(S["a_exp"], h + 1)
                    if h >= 4:
                        dve.wait_ge(S["rc_done"], h - 3)
                    link(dve.scalar_tensor_tensor(st[4 + h % 4], ps[:, h % 4, 0:SPAN], 0.0, st[16 + h % 4],
                                                  op0=ALU.max, op1=ALU.add))
                    dve.tensor_tensor(diag(st[8 + h % 4]), diag(st[4 + h % 4]), mask2, ALU.mult)\
                        .then_inc(S["spm_ready"], 1)
                for h in range(4 * g, 4 * g + 4):
                    if h >= 4:
                        dve.wait_ge(S["w_exp"], h - 3)
                    link(dve.tensor_tensor(st[20 + h % 4], ps[:, h % 4, 0:SPAN], st[4 + h % 4], ALU.subtract))
                    dve.wait_ge(S["rc_done"], h + 1)
                    dve.tensor_tensor(st[20 + h % 4], ps[:, 4 + h % 2, 0:SPAN], st[20 + h % 4], ALU.add)\
                        .then_inc(S["arg_ready"], 1)
            add_to_x("bo", 8)
            peer(1, 8, ("norm_ffn", DT))
            ple(2, 9, ("norm_ple", DT))
            norm(10, [("final", 0)], (mT,), S["out_ready"])

        @block.gpsimd
        def _(pool):
            for h in range(HEADS1):
                pool.wait_ge(S["row_ready"], h + 1)
                pool.dma_start(toeplitz[h], row[h % 2]).then_inc(row_stored[h % 2], 16)
            for h in range(HEADS1):
                pool.wait_ge(row_stored[h % 2], 16 * (HEADS1 // 2))
                flat = toeplitz[h].rearrange("p x -> (p x)")
                skew = flat[0:P * (SPAN - 1)].rearrange("(p x) -> p x", p=P)
                dst = toep[:, h * SPAN:(h + 1) * SPAN]
                pool.dma_start(dst[:, 0:P], skew[:, P - 1 + P:2 * P - 1 + P]).then_inc(S["toep_loaded"], 16)
                pool.dma_start(dst[:, P:SPAN], skew[:, P - 1:P - 1 + T]).then_inc(S["toep_loaded"], 16)
            def fetch(level):
                pool.wait_ge(S["y_stored"], 16 * EXPERTS * (level + 1))
                for k in range(TT * TOP_K):
                    pool.indirect_dma_start(out=fetched[:, k * D:(k + 1) * D], out_offset=None, in_=expert_out,
                                            in_offset=bass.IndirectOffsetOnAxis(ap=r_slot[:, k:k + 1], axis=0))\
                        .then_inc(S["y_fetched"], 16)

            pool.wait_ge(S["slots_ready"], 1)
            fetch(0)
            count = pool.value_load(r_cnt, min_val=0, max_val=T)
            with ExitStack() as nest:
                for level in range(1, PASSES):
                    nest.enter_context(pool.If(count > CAP * level))
                    fetch(level)
            mask2 = triu.unsqueeze(1).broadcast_to((P, 2, P))
            for h in range(HEADS2):
                pool.wait_ge(S["w_exp"], h + 1)
                a = st[12 + h % 4].rearrange("p (k t) -> p k t", k=3)[:, 0:3:2, :]
                pool.tensor_tensor(a, a, mask2, ALU.mult).then_inc(S["a_ready"], 1)


def kernel(**inputs):
    import concourse.bacc as bacc
    from concourse.bass_utils import run_bass_kernel_spmd

    a = {k: np.asarray(v) for k, v in inputs.items()}

    def cols(v):
        v = v.reshape(-1, v.shape[-1] // P, P)
        return v.transpose(2, 0, 1).reshape(P, -1)

    def t_form(v):
        return v.reshape(T, -1, P).transpose(2, 1, 0).reshape(P, -1)

    named = {
        "g_mix": a["g_mix"], "g_ffn": a["g_ffn"], "g_ple": a["g_ple"], "g_final": a["g_final"],
        "pool_scale": a["pool_scale"], "norm_mix": a["norm_mix_2"], "conv_w": a["a_conv_w_2"][0],
        "conv_b": a["a_conv_b_2"], "b_r": a["a_b_r_2"], "b_i": a["a_b_i_2"], "lam": a["a_lambda_2"],
        "kv_norm": a["kv_norm_2"], "norm_ffn": a["norm_ffn_2"], "norm_ple": a["norm_ple_2"],
        "final": a["final_norm_2"],
    }
    base, reach, hot = constants()
    arrays = {
        "x": t_form(a["x"][0]),
        "consts": base, "reach": reach, "hot": hot,
        "params": np.concatenate([cols(np.atleast_2d(named[n])) for n in PARAMS], axis=1),
        "rel_bias": a["rel_bias"],
        "w_in": a["w_in"][0],
        "w_pool": a["w_pool"][0].transpose(1, 0, 2).reshape(P, -1),
        "w_out": a["w_out"][0],
        "w_router": a["w_router"][0].reshape(DT, P, EXPERTS).transpose(1, 0, 2).reshape(P, -1),
        "b_router": a["b_router"][0],
        "w_gate_up": a["w_gate_up"][0], "w_down": a["w_down"][0], "b_down": a["b_down"][0],
        "b_gate_up": cols(a["b_gate_up"][0]),
        "p0": t_form(a["p"][0, 0]), "w_ple_gate": a["w_ple_gate"][0], "w_ple_proj": a["w_ple_proj"][0],
        "p2": np.stack([t_form(a["p_2"][L, 0]) for L in range(2)]),
        "ple_w_gate": a["ple_w_gate_2"], "ple_w_proj": a["ple_w_proj_2"],
        "a_w_in": np.concatenate([a["a_w_in_2"][0][:, D:], a["a_w_in_2"][0][:, :D]], axis=1),
        "w_r": a["a_w_r_2"][0].transpose(1, 0, 2).reshape(P, -1),
        "w_i": a["a_w_i_2"][0].transpose(1, 0, 2).reshape(P, -1),
        "a_w_out": a["a_w_out_2"][0],
        "w_kv": a["w_kv_2"], "b_w_q": a["b_w_q_2"][0], "b_w_o": a["b_w_o_2"][0],
        "peer_w_q": a["peer_w_q_2"],
        "sub_keys": a["peer_sub_keys_2"].reshape(2, 16, P, P).transpose(0, 3, 1, 2).reshape(2, P, -1),
    }
    for L in range(2):
        arrays[f"u{L}"] = a["peer_u_2"][L].reshape(P, P, DT, P).transpose(1, 3, 2, 0).reshape(P, P, D)
        arrays[f"v{L}"] = a["peer_v_2"][L].reshape(P, P, D).transpose(1, 0, 2)
    arrays = {k: np.ascontiguousarray(v) for k, v in arrays.items()}

    nc = bacc.Bacc("TRN2", target_bir_lowering=False, num_devices=1)
    io = {k: nc.dram_tensor(f"in_{k}", v.shape, mybir.dt.from_np(v.dtype), kind="ExternalInput").ap()
          for k, v in arrays.items()}
    out = nc.dram_tensor("out", (P, W), F32, kind="ExternalOutput").ap()
    program(nc, io, out)
    r = run_bass_kernel_spmd(nc, [{f"in_{k}": v for k, v in arrays.items()}], core_ids=[0])
    y = r.results[0]["out"]
    return y.reshape(P, DT, T).transpose(2, 1, 0).reshape(1, T, D)
```

```python
from contextlib import ExitStack

import numpy as np

import concourse.bass as bass
import concourse.mybir as mybir

F32 = mybir.dt.float32
F32R = mybir.dt.float32r
BF16 = mybir.dt.bfloat16
I32 = mybir.dt.int32
U32 = mybir.dt.uint32
ACT = mybir.ActivationFunctionType
ALU = mybir.AluOpType
AX_X = mybir.AxisListType.X

P = 128
T = 256
D = 1024
DT = D // P
TT = T // P
W = DT * T
BANK = 512
EPS = 1e-6
NEG = -1e30

RING = 8
SLOT = 1024

HEADS1, DH = 8, 64
SPAN = 3 * P
POOL_WINDOWS = (2, 4, 8, 16)
PAD = 16

EXPERTS, TOP_K = 32, 4
CAP = 64
PASSES = T // CAP
LIMIT, ALPHA = 7.0, 1.702
MOE_CHUNKS, MOE_COLS = 12, 2048
MOE_RAW, MOE_SPLIT = 6, 3

HEADS2 = 16
CONV = 4

PH, PTOP, PKEYS = 8, 16, 128
CHUNKS = PKEYS
GROUP = 4
BODY = 8
READS = 4 + CHUNKS // 2

C_IDENT, C_ONES, C_TRIU, C_NTRI, C_NONES, C_IOTA = (P * k for k in range(6))
C_INV = 6 * P
C_COLS = C_INV + 4 * PAD
PARAMS = {}
for _name, _n in (("g_mix", DT), ("g_ffn", DT), ("g_ple", DT), ("g_final", DT), ("pool_scale", 4),
                  ("norm_mix", 2 * DT), ("conv_w", CONV * DT), ("conv_b", DT), ("b_r", DT), ("b_i", DT),
                  ("lam", DT), ("kv_norm", DT), ("norm_ffn", 2 * DT), ("norm_ple", 2 * DT), ("final", DT)):
    PARAMS[_name] = sum(n for _, n in PARAMS.values()), _n
P_COLS = sum(n for _, n in PARAMS.values())


def bucket(d):
    n = np.maximum(d, 1).astype(np.float32)
    large = 16 + (np.log(n / np.float32(16)) / np.float32(np.log(128)) * np.float32(16)).astype(np.int32)
    return np.where(d < 16, d, np.minimum(large, 31))


def constants():
    k, m = np.arange(P)[:, None], np.arange(P)[None, :]
    base = np.concatenate([
        k == m, np.ones((P, P)), k < m, -1.0 * (k > m), -np.ones((P, P)), np.broadcast_to(m, (P, P)),
        np.broadcast_to(np.concatenate([1.0 / np.minimum(np.arange(PAD) + 1, w) for w in POOL_WINDOWS]), (P, 4 * PAD)),
    ], axis=1).astype(np.float32)
    dist = T - 1 - np.arange(SPAN)
    reach = (dist >= 0) * ((dist <= 128).astype(int) + (dist % 4 == 0) + (dist % 16 == 0))
    mask = np.where(reach > 0, np.log(np.maximum(reach, 1)), NEG).astype(np.float32)
    hot = (bucket(np.maximum(dist, 0))[None, :] == np.arange(32)[:, None]).astype(np.float32)
    twice = (k % CAP == m % CAP).astype(np.float32)
    return base, twice, np.ascontiguousarray(np.broadcast_to(mask, (P, SPAN))), hot


def plan():
    first, n = {}, 0
    for name, chunks in (
        ("w_in", 16), ("w_pool", 1), ("w_out", 8), ("w_router", 1), ("b_down", 1), ("proj0", 2), ("ple0", 8),
        ("a_in", 16), ("w_r", 1), ("w_i", 1), ("a_out", 8),
        ("wq0", 16), ("keys0", 2), ("u0", CHUNKS), ("v0", CHUNKS), ("proj1", 2), ("ple1", 8),
        ("kv", 16), ("bq", 8), ("bo", 8),
        ("wq1", 16), ("keys1", 2), ("u1", CHUNKS), ("v1", CHUNKS), ("proj2", 2), ("ple2", 8),
    ):
        first[name] = n
        n += chunks
    return first


class Tally:

    def __init__(self, eng, sem):
        self.eng, self.sem, self.n, self.turns = eng, sem, 0, 0

    def mark(self, ins):
        ins.then_inc(self.sem, 1)
        self.n += 1
        return self.n

    def wait(self, n=None):
        self.eng.wait_ge(self.sem, self.turns + (self.n if n is None else n))

    def link(self, ins):
        self.mark(ins)
        self.wait()

    def enter(self, turn, per, begin=0):
        self.turns, self.start, self.per = turn * per - begin * per, self.n, per

    def leave(self, count):
        assert self.n == self.start + self.per, (self.n - self.start, self.per)
        self.n, self.turns = self.start + self.per * count, 0


def program(nc, io, out):
    first = plan()
    with ExitStack() as ctx:
        def sb(name, shape, dt=F32):
            return ctx.enter_context(nc.sbuf_tensor(name, shape, dt))

        def sem(name):
            return ctx.enter_context(nc.semaphore(name))

        with nc.sbuf_tensor("big", [P, CHUNKS * T], F32) as big:
            pass
        sb("moe_raw_place", [P, MOE_RAW * MOE_COLS])
        moe_hi = sb("moe_hi", [P, MOE_SPLIT * MOE_COLS], F32R)
        moe_lo = sb("moe_lo", [P, MOE_SPLIT * MOE_COLS], F32R)
        m_x = sb("m_x", [P, DT * 2 * CAP], F32R)
        m_h = sb("m_h", [P, DT * 2 * CAP], F32R)
        sb("tail_place", [P, CHUNKS * T - (MOE_RAW + 2 * MOE_SPLIT) * MOE_COLS - 4 * DT * CAP])
        ring = sb("ring", [P, RING, SLOT])
        xT = sb("xT", [P, W])
        hT = sb("hT", [P, W])
        mT = sb("mT", [P, W])
        con = sb("con", [P, C_COLS])
        par = sb("par", [P, P_COLS])
        rs = sb("rs", [P, 2 * T])
        eps = sb("eps", [P, 1])
        small = sb("small", [P, 4064])
        pT = sb("pT", [P, 2 * T])
        ps = ctx.enter_context(nc.psum_tensor("ps", [P, 8, BANK], F32))
        toeplitz = nc.dram_tensor("toeplitz", (HEADS1, P, SPAN), F32, kind="Internal").ap()
        expert_out = nc.dram_tensor("expert_out", (EXPERTS * CAP, D), F32, kind="Internal").ap()

        ident, ones = con[:, C_IDENT:C_IDENT + P], con[:, C_ONES:C_ONES + P]
        triu, ntri = con[:, C_TRIU:C_TRIU + P], con[:, C_NTRI:C_NTRI + P]
        nones, iota = con[:, C_NONES:C_NONES + P], con[:, C_IOTA:C_IOTA + P]

        def col(name, k=0):
            a, n = PARAMS[name]
            return par[:, a + k:a + k + 1]

        def tile(buf, c, n=T):
            return buf[:, c * n:(c + 1) * n]

        def half(bank, e):
            return ps[:, bank + e // 2, (e % 2) * T:(e % 2 + 1) * T]

        w_loaded = [sem(f"w_loaded{k}") for k in range(RING)]
        w_used = sem("w_used")
        x_loaded, con_loaded, par_loaded = sem("x_loaded"), sem("con_loaded"), sem("par_loaded")
        attn_loaded, bias_loaded = sem("attn_loaded"), sem("bias_loaded")
        x_ready, h_ready = sem("x_ready"), sem("h_ready")
        sq_ready, ss_done, rms_ready = sem("sq_ready"), sem("ss_done"), sem("rms_ready")
        eps_ready, p_loaded = sem("eps_ready"), sem("p_loaded")
        dve_step, act_step = sem("dve_step"), sem("act_step")
        names = (
            "rb_ready row_done row_ready toep_loaded u_copied qk_ready v_ready pooled_ready mixed_done "
            "score_done biased prob_exp prob_ready pt_done pt_ready pv_done mix_ready "
            "htok_done htok_ready neg_top gate_exp mask_ready rank_done count_ready gmat_in gmat_done gmat_ready "
            "slots_ready diag_ready sel_ready gathered xg_high xg_ready sig_in sig_ready hid_ready y_done y_ready yt_done "
            "ytok_ready gates_copied ups_copied turned hi_ready split_ready y_stored y_fetched combined added "
            "proj_done gate_ready "
            "conv_ready yg_ready lam_in lam_exp ri_ready lru_exp lru_e lru_sqrt gated_ready "
            "pq_ready s_done bank_read cv_ready cv_exp sel_done selT_done selT_ready oh_ready g_done g_used "
            "q2_ready k2_ready v2_ready z_done spm_ready rc_done arg_ready a_exp w_exp a_ready o_done o_ready "
            "out_ready out_stored moe_step moe_used"
        ).split()
        S = {n: sem(n) for n in names}
        row_stored = [sem(f"row_stored{k}") for k in range(2)]
        moe_loaded = [sem(f"moe_loaded{k}") for k in range(MOE_RAW)]

        def used_through(eng, seg, chunks):
            eng.wait_ge(w_used, first[seg] + chunks)

        TAIL = (MOE_RAW + 2 * MOE_SPLIT) * MOE_COLS
        tail = big[:, TAIL:CHUNKS * T]
        q1, k1, v1 = (tail[:, k * 1024:(k + 1) * 1024] for k in range(3))
        toep = tail[:, 3072:3072 + HEADS1 * SPAN]
        upad = tail[:, 6144:6144 + 4 * (PAD + T)]
        twice = tail[:, 7232:7232 + P]
        moe_bias = tail[:, 7424:7936]
        winsum = small[:, 0:4 * (PAD + T)]
        winsum2 = small[:, 1088:2176]
        cmask, hot = small[:, 2176:2560], small[0:32, 2560:2944]
        relb, rb = small[0:32, 2944:2952], small[0:32, 3040:4064]
        stat1 = small[:, 2952:3000]
        prob = [hT[:, k * SPAN:(k + 1) * SPAN] for k in range(2)]
        probT = [hT[:, (2 + k) * SPAN:(3 + k) * SPAN] for k in range(2)]
        row = [mT[:, k * SPAN:(k + 1) * SPAN] for k in range(2)]

        r_max, r_idx = small[:, 0:16], small[:, 16:32]
        r_idxf, r_nmax = small[:, 32:40], small[:, 40:42]
        r_exp, r_sum, r_rec, r_gate = small[:, 48:56], small[:, 56:58], small[:, 58:60], small[:, 60:68]
        r_bias, r_logit = small[:, 3008:3040], small[:, 160:224]
        r_hot = small[:, 256:512]
        r_mask, r_gmat = small[:, 512:576], small[:, 576:640]
        r_rank1 = small[:, 640:640 + TT * EXPERTS]
        r_tmp = small[:, 768:1024]
        r_slotf, r_slot = small[:, 1024:1032], small[:, 1032:1040].bitcast(U32)
        r_pass, r_step = small[:, 1056:1064], small[:, 1064:1072]
        r_cntf, r_cnt = small[0:1, 4062:4063], small[0:1, 4063:4064].bitcast(I32)
        r_gmatT = small[0:32, 1280:1280 + T]
        r_diag = small[:, 1536:1536 + 8 * P]
        m_sel = small[:, 2560:2560 + TT * P]
        MW = DT * CAP
        m_gu = tail[:, 2048:4096]
        m_y = tail[:, 2048:3072]
        m_tok = tail[0:CAP, 4096:5120]
        m_g, m_u, m_sig, m_hid = (tail[:, 5120 + MW * k:5120 + MW * (k + 1)] for k in range(4))
        fetched = big[:, 0:TT * TOP_K * D]

        lru = [big[:, k * W:(k + 1) * W] for k in range(8)]
        sp = small[:, 0:96]
        k2, q2, v2 = lru[0], lru[1], lru[2]
        st = [big[:, 3 * W + k * SPAN:3 * W + (k + 1) * SPAN] for k in range(24)]

        pq = big[:, CHUNKS * T - 2 * W:CHUNKS * T]
        sv = small[:, 0:256]
        si = small[:, 256:512].bitcast(U32)
        sif = small[:, 512:768]
        cand, cand2 = small[:, 768:1024], small[:, 1024:1280]
        p_tmp = small[:, 1280:1408]
        cv = small[:, 1408:1664]
        ci = small[:, 1664:1792].bitcast(U32)
        cc = small[:, 1792:1920].bitcast(U32)
        ccf = small[:, 1920:2048]
        pick = small[:, 2048:3072].bitcast(BF16)
        i12 = small[:, 3072:3584]
        p_sum = small[:, 3584:3600]
        selT = small[:, 0:3 * T]

        block = ctx.enter_context(nc.Block())

        @block.sync
        def _(sync):
            def free(n):
                if n >= RING:
                    sync.wait_ge(w_used, n - RING + 1)

            def load(n, src, cols=SLOT, rows=P):
                free(n)
                sync.dma_start(ring[0:rows, n % RING, 0:cols], src).then_inc(w_loaded[n % RING], 16)

            def dense(seg, w, halves=1):
                for h in range(halves):
                    for c in range(DT):
                        load(first[seg] + h * DT + c, w[c * P:(c + 1) * P, h * SLOT:(h + 1) * SLOT])

            def ple(k, p, proj, gate):
                if k:
                    sync.wait_ge(w_used, first[f"proj{k - 1}"] + 2)
                sync.dma_start(pT[:, :], p).then_inc(p_loaded, 16)
                for c in range(2):
                    load(first[f"proj{k}"] + c, proj[c * P:(c + 1) * P, :])
                dense(f"ple{k}", gate)

            def table(seg, src):
                n = first[seg]
                with sync.Fori(0, CHUNKS // RING) as i:
                    for k in range(RING):
                        sync.wait_ge(w_used, n + k - RING + 1 + i * RING)
                        sync.dma_start(ring[:, (n + k) % RING, :], src[i * RING + k])\
                            .then_inc(w_loaded[(n + k) % RING], 16)

            def expert_chunk(e, k, count=None):
                if count is not None:
                    sync.wait_ge(S["split_ready"], count)
                dst = big[:, k % MOE_RAW * MOE_COLS:(k % MOE_RAW + 1) * MOE_COLS]
                if k < DT:
                    src = io["w_gate_up"][e, k * P:(k + 1) * P, :]
                else:
                    src = io["w_down"][e, (k - DT) * 2 * P:(k - DT + 1) * 2 * P, :].rearrange("(s p) d -> p s d", p=P)
                    dst = dst.rearrange("p (s d) -> p s d", s=2)
                sync.dma_start(dst, src).then_inc(moe_loaded[k % MOE_RAW], 16)

            def expert_weights(level, start=0):
                if level:
                    sync.wait_ge(S["combined"], level)
                with sync.Fori(start, EXPERTS) as e:
                    for k in range(MOE_CHUNKS):
                        expert_chunk(e, k, e * MOE_CHUNKS + (EXPERTS * level * MOE_CHUNKS + k - MOE_RAW + 1))

            sync.dma_start(xT[:, :], io["x"]).then_inc(x_loaded, 16)
            sync.dma_start(con[:, :], io["consts"]).then_inc(con_loaded, 16)
            sync.dma_start(par[:, :], io["params"]).then_inc(par_loaded, 16)
            sync.dma_start(cmask, io["reach"]).then_inc(attn_loaded, 16)
            sync.dma_start(hot, io["hot"]).then_inc(attn_loaded, 16)
            sync.dma_start(relb, io["rel_bias"]).then_inc(attn_loaded, 16)
            sync.dma_start(moe_bias, io["b_gate_up"]).then_inc(bias_loaded, 16)
            sync.dma_start(twice, io["twice"]).then_inc(bias_loaded, 16)
            sync.dma_start(r_bias, io["b_router"].partition_broadcast(P)).then_inc(bias_loaded, 16)
            dense("w_in", io["w_in"], 2)
            load(first["w_pool"], io["w_pool"], 4 * P)
            dense("w_out", io["w_out"])
            load(first["w_router"], io["w_router"], DT * EXPERTS)
            load(first["b_down"], io["b_down"], rows=EXPERTS)
            for k in range(MOE_CHUNKS):
                expert_chunk(0, k, k - MOE_RAW + 1 if k >= MOE_RAW else None)
            expert_weights(0, 1)
            sync.wait_ge(S["count_ready"], 1)
            count = sync.value_load(r_cnt, min_val=0, max_val=T)
            with ExitStack() as nest:
                for level in range(1, PASSES):
                    nest.enter_context(sync.If(count > CAP * level))
                    expert_weights(level)
            ple(0, io["p0"], io["w_ple_proj"], io["w_ple_gate"])
            dense("a_in", io["a_w_in"], 2)
            load(first["w_r"], io["w_r"])
            load(first["w_i"], io["w_i"])
            dense("a_out", io["a_w_out"])
            for L in range(2):
                dense(f"wq{L}", io["peer_w_q"][L], 2)
                for k in range(2):
                    load(first[f"keys{L}"] + k, io["sub_keys"][L, :, k * SLOT:(k + 1) * SLOT])
                table(f"u{L}", io[f"u{L}"])
                table(f"v{L}", io[f"v{L}"])
                ple(L + 1, io["p2"][L], io["ple_w_proj"][L], io["ple_w_gate"][L])
                if L == 0:
                    dense("kv", io["w_kv"], 2)
                    dense("bq", io["b_w_q"])
                    dense("bo", io["b_w_o"])
            sync.wait_ge(S["out_ready"], 8)
            sync.dma_start(out, mT[:, :]).then_inc(S["out_stored"], 16)
            sync.wait_ge(S["out_stored"], 16)

        @block.tensor
        def _(pe):
            def chunk(n):
                pe.wait_ge(w_loaded[n % RING], 16 * (n // RING + 1))
                return ring[:, n % RING, :]

            def sum_squares(k):
                for j in range(4):
                    pe.wait_ge(sq_ready, 4 * k + j + 1)
                    for c in (2 * j, 2 * j + 1):
                        last = pe.matmul(ps[:, 7, 0:T], ones, tile(mT, c), start=(c == 0), stop=(c == DT - 1))
                last.then_inc(ss_done, 1)

            def dense(n, src, bank, ready=None, at=0, between=None):
                for c in range(DT):
                    if ready is not None:
                        pe.wait_ge(ready, at + c + 1)
                    w = chunk(n + c)
                    for e in range(DT):
                        last = pe.matmul(half(bank, e), w[:, e * P:(e + 1) * P], src(c),
                                         start=(c == 0 and e % 2 == 0), stop=(c == DT - 1), skip_group_check=True)
                    last.then_inc(w_used, 1)
                    if between:
                        between(c)

            def token_major(n, src, ready, at, cols, outs):
                for c in range(DT):
                    pe.wait_ge(ready, at + c + 1)
                    w = chunk(n + c)
                    for tt in range(TT):
                        for k, o in enumerate(outs[tt]):
                            last = pe.matmul(o, tile(src, c)[:, tt * P:(tt + 1) * P],
                                             w[:, cols + k * BANK:cols + (k + 1) * BANK],
                                             start=(c == 0), stop=(c == DT - 1), skip_group_check=True)
                    last.then_inc(w_used, 1)

            hsrc = lambda c: tile(hT, c)
            msrc = lambda c: tile(mT, c)

            pe.wait_ge(con_loaded, 16)
            sum_squares(0)
            pe.wait_ge(attn_loaded, 48)

            def bias_row(h):
                pe.wait_ge(S["rb_ready"], h + 1)
                if h >= 2:
                    pe.wait_ge(S["row_ready"], h - 1)
                pe.matmul(ps[:, 4 + h % 2, 0:SPAN], rb[:, h * P:(h + 1) * P], hot, start=True, stop=True)\
                    .then_inc(S["row_done"], 1)

            dense(first["w_in"], hsrc, 0, h_ready, 0, between=bias_row)
            pe.wait_ge(S["row_ready"], HEADS1)
            pe.wait_ge(rms_ready, 1)
            for c in range(DT):
                w = chunk(first["w_in"] + DT + c)
                for e in range(4):
                    pe.matmul(half(4, e), w[:, e * P:(e + 1) * P], hsrc(c),
                              start=(c == 0 and e % 2 == 0), stop=(c == DT - 1), skip_group_check=True)
                for tt in range(TT):
                    last = pe.matmul(ps[:, 6 + tt, :], hsrc(c)[:, tt * P:(tt + 1) * P], w[:, BANK:2 * BANK],
                                     start=(c == 0), stop=(c == DT - 1), skip_group_check=True)
                last.then_inc(w_used, 1)

            def scores(h):
                lo = 64 * (h % 2)
                q, k = tile(q1, h // 2), tile(k1, h // 2)
                if h == 0:
                    pe.wait_ge(S["qk_ready"], 4)
                    pe.wait_ge(S["u_copied"], 4)
                if h >= 2:
                    pe.wait_ge(S["prob_ready"], h - 1)
                pe.matmul(ps[:, h % 2, 0:P], q[lo:lo + DH, 0:P], k[lo:lo + DH, 0:P], start=True, stop=True)
                pe.matmul(ps[:, h % 2, P:SPAN], q[lo:lo + DH, P:T], k[lo:lo + DH, 0:T], start=True, stop=True)\
                    .then_inc(S["score_done"], 1)

            def turn(h):
                pe.wait_ge(S["prob_ready"], h + 1)
                if h >= 2:
                    pe.wait_ge(S["pt_ready"], h - 1)
                for b in range(3):
                    last = pe.transpose(ps[:, 2 + h % 2, b * P:(b + 1) * P], prob[h % 2][:, b * P:(b + 1) * P], ident)
                last.then_inc(S["pt_done"], 1)

            def values(h):
                lo = 64 * (h % 2)
                if h == 0:
                    pe.wait_ge(S["v_ready"], 2)
                pe.wait_ge(S["pt_ready"], h + 1)
                if h >= 4:
                    pe.wait_ge(S["mix_ready"], h - 3)
                o = ps[lo:lo + DH, 4 + (h // 2) % 2, 0:T]
                v = [v1[:, tt * BANK + h * DH:tt * BANK + (h + 1) * DH] for tt in range(TT)]
                pt = probT[h % 2]
                pe.matmul(o[:, 0:P], v[0], pt[:, 0:P], start=True, stop=True)
                pe.matmul(o[:, P:T], v[0], pt[:, P:2 * P], start=True, stop=False)
                pe.matmul(o[:, P:T], v[1], pt[:, 2 * P:SPAN], start=False, stop=True).then_inc(S["pv_done"], 1)

            for s in range(HEADS1 + 2):
                if s < HEADS1:
                    scores(s)
                if 1 <= s <= HEADS1:
                    turn(s - 1)
                if s >= 2:
                    values(s - 2)
            w = chunk(first["w_pool"])
            pe.wait_ge(S["v_ready"], 2)
            for g in range(4):
                pe.wait_ge(S["pooled_ready"], g + 1)
                last = pe.matmul(half(6, g), w[:, g * P:(g + 1) * P], upad[:, g * (PAD + T) + PAD:(g + 1) * (PAD + T)],
                                 start=True, stop=True)
            last.then_inc(w_used, 1)
            pe.wait_ge(S["mix_ready"], HEADS1 + 4)
            dense(first["w_out"], msrc, 0)

            sum_squares(1)
            pe.wait_ge(h_ready, 2 * DT)
            w = chunk(first["w_router"])
            for tt in range(TT):
                for c in range(DT):
                    last = pe.matmul(ps[:, 4, tt * EXPERTS:(tt + 1) * EXPERTS], tile(hT, c)[:, tt * P:(tt + 1) * P],
                                     w[:, c * EXPERTS:(c + 1) * EXPERTS], start=(c == 0), stop=(c == DT - 1))
            last.then_inc(w_used, 1)
            for tt in range(TT):
                for c in range(DT):
                    last = pe.transpose(ps[:, 2 * tt + c // 4, (c % 4) * P:(c % 4 + 1) * P],
                                        tile(hT, c)[:, tt * P:(tt + 1) * P], ident)
                last.then_inc(S["htok_done"], 1)
            pe.wait_ge(S["mask_ready"], 2)
            pe.matmul(ps[:, 5, 0:32], triu, r_mask[:, 0:32], start=True, stop=True)
            pe.matmul(ps[:, 5, 32:64], triu, r_mask[:, 32:64], start=True, stop=False)
            pe.matmul(ps[:, 5, 32:64], ones, r_mask[:, 0:32], start=False, stop=True)
            pe.matmul(ps[:, 5, 64:96], ones, r_mask[:, 0:32], start=True, stop=False)
            pe.matmul(ps[:, 5, 64:96], ones, r_mask[:, 32:64], start=False, stop=True).then_inc(S["rank_done"], 1)
            pe.wait_ge(S["gmat_in"], 2)
            for tt in range(TT):
                last = pe.transpose(ps[0:32, 6, tt * P:(tt + 1) * P], r_gmat[:, tt * 32:(tt + 1) * 32], ident)
            last.then_inc(S["gmat_done"], 1)

            def expert_pass(level):
                base = EXPERTS * level

                def gather(e):
                    pe.wait_ge(S["sel_ready"], e + base + 1)
                    for c in range(DT):
                        for tt in range(TT):
                            last = pe.matmul(ps[:, c // 4, (c % 4) * P:(c % 4 + 1) * P],
                                             mT[:, tt * D + c * P:tt * D + (c + 1) * P],
                                             m_sel[:, tt * P:(tt + 1) * P], start=(tt == 0), stop=(tt == TT - 1))
                    last.then_inc(S["gathered"], 1)

                def products(e, k, operand, bank, blocks, start, stop):
                    for s, o in enumerate(operand):
                        for part in (moe_hi, moe_lo):
                            for b in range(blocks):
                                a = k % MOE_SPLIT * MOE_COLS + (s * blocks + b) * BANK
                                last = pe.matmul(ps[:, bank + b, :], o, part[:, a:a + BANK],
                                                 start=(start and s == 0 and part is moe_hi),
                                                 stop=(stop and s == len(operand) - 1 and part is moe_lo),
                                                 skip_group_check=True)
                    last.then_inc(S["moe_used"], 1)

                def sum_halves(n):
                    for b in range(2):
                        pe.wait_ge(S["y_ready"], n * 2 + b + 1)
                        pe.matmul(ps[0:CAP, b, :], twice[:, 0:CAP], tile(m_y, b, 512), start=True, stop=True)\
                            .then_inc(S["yt_done"], 1)

                def expert(e, first=False, last=False):
                    n = e + base
                    pe.wait_ge(S["xg_ready"], n * 2 + 2)
                    for c in range(DT):
                        pe.wait_ge(S["split_ready"], n * MOE_CHUNKS + c + 1)
                        products(e, c, [m_x[:, c * P:(c + 1) * P]], 2, 4, c == 0, c == DT - 1)
                        if c == 0 and not first:
                            sum_halves(n - 1)
                    if not first:
                        pe.wait_ge(S["ytok_ready"], n * 2)
                    if not last:
                        gather(e + 1)
                    for b in range(2):
                        pe.wait_ge(S["gates_copied"], n * 2 + b + 1)
                        pe.wait_ge(S["ups_copied"], n * 2 + b + 1)
                        for bank in (b, 2 + b):
                            for f in range(4):
                                a = bank * BANK + f * P
                                ins = pe.matmul(ps[:, 2 + bank, f * P:(f + 1) * P], m_gu[:, a:a + P], twice,
                                                start=True, stop=True)
                        ins.then_inc(S["turned"], 1)
                    for k in range(DT, MOE_CHUNKS):
                        f = 2 * (k - DT)
                        pe.wait_ge(S["hid_ready"], n * 2 + 1 + f // 4)
                        pe.wait_ge(S["split_ready"], n * MOE_CHUNKS + k + 1)
                        products(e, k, [m_h[:, (f + s) * P:(f + s + 1) * P] for s in range(2)], 6, 2,
                                 k == DT, k == MOE_CHUNKS - 1)
                    if last:
                        sum_halves(n)

                if level == 0:
                    pe.wait_ge(S["htok_ready"], 4)
                    pe.wait_ge(S["gmat_ready"], 1)
                gather(0)
                expert(0, first=True)
                with pe.Fori(1, EXPERTS - 1) as e:
                    expert(e)
                expert(EXPERTS - 1, last=True)

            def combine(level):
                pe.wait_ge(S["diag_ready"], 8 * (level + 1))
                pe.wait_ge(S["y_fetched"], 16 * 8 * (level + 1))
                if level == 0:
                    w = chunk(first["b_down"])
                    for c in range(DT):
                        last = pe.matmul(half(0, c), w[0:EXPERTS, c * P:(c + 1) * P], r_gmatT, start=(c % 2 == 0),
                                         stop=False, skip_group_check=True)
                    last.then_inc(w_used, 1)
                for c in range(DT):
                    for tt in range(TT):
                        for k in range(TOP_K):
                            a = (tt * TOP_K + k) * D + c * P
                            last = pe.matmul(half(0, c)[:, tt * P:(tt + 1) * P], fetched[:, a:a + P],
                                             r_diag[:, (tt * TOP_K + k) * P:(tt * TOP_K + k + 1) * P],
                                             start=(level > 0 and c % 2 == 0 and tt == 0 and k == 0),
                                             stop=(k == TOP_K - 1), skip_group_check=True)
                last.then_inc(S["combined"], 1)

            expert_pass(0)
            combine(0)
            count = pe.value_load(r_cnt, min_val=0, max_val=T)
            with ExitStack() as nest:
                for level in range(1, PASSES):
                    nest.enter_context(pe.If(count > CAP * level))
                    pe.wait_ge(S["added"], 4 * level)
                    expert_pass(level)
                    combine(level)

            def ple(k, norm, reads):
                pe.wait_ge(x_ready, 4 * (norm - 1) + 4)
                n = first[f"proj{k}"]
                pe.wait_ge(p_loaded, 16 * (k + 1))
                for c in range(2):
                    w = chunk(n + c)
                    for e in range(DT):
                        last = pe.matmul(half(0, e), w[:, e * P:(e + 1) * P], tile(pT, c),
                                         start=(c == 0 and e % 2 == 0), stop=(c == 1), skip_group_check=True)
                    last.then_inc(w_used, 1)
                sum_squares(norm)
                dense(first[f"ple{k}"], hsrc, 4, h_ready, DT * reads)

            ple(0, 2, 2)
            sum_squares(3)

            sum_squares(4)
            dense(first["a_in"], hsrc, 0, h_ready, 3 * DT)
            dense(first["a_in"] + DT, hsrc, 4)
            for k, seg in enumerate(("w_r", "w_i")):
                w = chunk(first[seg])
                if k == 1:
                    pe.wait_ge(S["yg_ready"], 4)
                for h in range(DT):
                    if k == 0:
                        pe.wait_ge(S["conv_ready"], DT)
                    last = pe.matmul(half(4 * k, h), w[:, h * P:(h + 1) * P], tile(lru[0], h), start=True, stop=True)
                last.then_inc(w_used, 1)
            for c in range(4):
                pe.wait_ge(S["ri_ready"], 16)
            dense(first["a_out"], msrc, 0, S["gated_ready"], 0)

            def peer(L, norm, at):
                sum_squares(norm)
                dense(first[f"wq{L}"], hsrc, 0, h_ready, at)
                dense(first[f"wq{L}"] + DT, hsrc, 4)
                keys = [chunk(first[f"keys{L}"] + k) for k in range(2)]
                pe.wait_ge(S["pq_ready"], 8 * L + 8)
                for tt in range(TT):
                    for hp in range(16):
                        last = pe.matmul(ps[:, 4 * tt + hp // 4, (hp % 4) * P:(hp % 4 + 1) * P],
                                         tile(pq, hp)[:, tt * P:(tt + 1) * P],
                                         keys[hp // 8][:, (hp % 8) * P:(hp % 8 + 1) * P], start=True, stop=True)
                        if tt and hp % 8 == 7:
                            last.then_inc(w_used, 1)
                    if tt == 0:
                        last.then_inc(S["s_done"], 1)
                n = first[f"u{L}"]
                with pe.Fori(0, CHUNKS // RING) as i:
                    for k in range(RING):
                        m = n + k
                        pe.wait_ge(w_loaded[m % RING], 16 * (m // RING + 1) + i * 16)
                        if k % 2 == 0:
                            pe.wait_ge(S["bank_read"], READS * L + k // 2 + 1 + i * 4)
                        for c in range(DT):
                            last = pe.matmul(half(0, k), ring[:, m % RING, c * P:(c + 1) * P], hsrc(c),
                                             start=(c == 0), stop=(c == DT - 1))
                        last.then_inc(w_used, 1)
                pe.wait_ge(S["sel_done"], L + 1)
                for k in range(3):
                    for tt in range(TT):
                        src = (i12[:, (k * TT + tt) * P:(k * TT + tt + 1) * P] if k < 2 else cv[:, tt * P:(tt + 1) * P])
                        last = pe.transpose(ps[:, 4 + k, tt * P:(tt + 1) * P], src, ident)
                last.then_inc(S["selT_done"], 1)
                with pe.Fori(0, T // BODY) as i:
                    for s in range(BODY):
                        pe.wait_ge(S["oh_ready"], T * L + s + 1 + i * BODY)
                        pe.matmul(ps[:, 4 + s // GROUP, (s % GROUP) * P:(s % GROUP + 1) * P],
                                  mT[:, s * P:(s + 1) * P], mT[:, (BODY + s) * P:(BODY + s + 1) * P],
                                  start=True, stop=True).then_inc(S["g_done"], 1)
                pe.wait_ge(S["g_used"], 64 * L + 64)
                for e in range(DT):
                    pe.matmul(half(0, e), ident, tile(xT, e), start=(e % 2 == 0), stop=False, skip_group_check=True)
                n = first[f"v{L}"]
                with pe.Fori(0, CHUNKS // RING) as i:
                    for k in range(RING):
                        m = n + k
                        pe.wait_ge(w_loaded[m % RING], 16 * (m // RING + 1) + i * 16)
                        for e in range(DT):
                            last = pe.matmul(half(0, e), ring[:, m % RING, e * P:(e + 1) * P],
                                             big[:, bass.ds(i * (RING * T) + k * T, T)],
                                             start=False, stop=True, skip_group_check=True)
                        last.then_inc(w_used, 1)

            peer(0, 5, 4 * DT)
            ple(1, 6, 5)

            sum_squares(7)
            dense(first["kv"], hsrc, 0, h_ready, 6 * DT)
            token_major(first["kv"] + DT, hT, h_ready, 6 * DT, 0, [[ps[:, 4 + 2 * tt + k, :] for k in range(2)] for tt in range(TT)])
            pe.wait_ge(S["k2_ready"], 4)
            dense(first["bq"], msrc, 0, h_ready, 7 * DT)

            def logits(h):
                lo = 64 * (h % 2)
                q, k = tile(q2, h // 2), tile(k2, h // 2)
                if h == 0:
                    pe.wait_ge(S["q2_ready"], 4)
                    pe.wait_ge(S["v2_ready"], 4)
                if h >= 4:
                    pe.wait_ge(S["arg_ready"], h - 3)
                z = ps[:, h % 4, 0:SPAN]
                pe.matmul(z[:, 0:T], k[lo:lo + DH, 0:P], q[lo:lo + DH, 0:T], start=True, stop=True)
                pe.matmul(z[:, T:SPAN], k[lo:lo + DH, P:T], q[lo:lo + DH, P:T], start=True, stop=True)\
                    .then_inc(S["z_done"], 1)

            def suffix(h):
                g = h % 4
                pe.wait_ge(S["spm_ready"], h + 1)
                if h >= 2:
                    pe.wait_ge(S["arg_ready"], h - 1)
                r = ps[:, 4 + h % 2, 0:SPAN]
                pe.matmul(r[:, 0:P], ntri, st[8 + g][:, 0:P], start=True, stop=True)
                pe.matmul(r[:, P:T], ntri, st[4 + g][:, P:T], start=True, stop=False)
                pe.matmul(r[:, P:T], nones, st[8 + g][:, T:SPAN], start=False, stop=True)
                pe.matmul(r[:, T:SPAN], ntri, st[8 + g][:, T:SPAN], start=True, stop=True).then_inc(S["rc_done"], 1)

            def heads_out(h):
                lo, g = 64 * (h % 2), h % 4
                pe.wait_ge(S["a_ready"], h + 1)
                if h >= 4:
                    pe.wait_ge(S["o_ready"], h - 3)
                o = ps[lo:lo + DH, 6 + (h // 2) % 2, 0:T]
                v = [v2[:, tt * D + h * DH:tt * D + (h + 1) * DH] for tt in range(TT)]
                a = st[12 + g]
                pe.matmul(o[:, 0:P], v[0], a[:, 0:P], start=True, stop=True)
                pe.matmul(o[:, P:T], v[0], a[:, P:T], start=True, stop=False)
                pe.matmul(o[:, P:T], v[1], a[:, T:SPAN], start=False, stop=True).then_inc(S["o_done"], 1)

            for g in range(HEADS2 // 4 + 1):
                for h in range(4 * g, 4 * g + 4):
                    if g < HEADS2 // 4:
                        logits(h)
                    if g >= 1:
                        heads_out(h - 4)
                if g < HEADS2 // 4:
                    for h in range(4 * g, 4 * g + 4):
                        suffix(h)
            pe.wait_ge(S["o_ready"], HEADS2)
            dense(first["bo"], msrc, 0)
            peer(1, 8, 8 * DT)
            ple(2, 9, 9)
            sum_squares(10)

        @block.scalar
        def _(act):
            step = Tally(act, act_step)

            def squares(k):
                if k == 0:
                    act.wait_ge(x_loaded, 16)
                for j in range(4):
                    if k:
                        act.wait_ge(x_ready, 4 * (k - 1) + j + 1)
                    act.activation(tile(mT, j, 512), tile(xT, j, 512), ACT.Square).then_inc(sq_ready, 1)
                act.wait_ge(ss_done, k + 1)
                act.activation(rs[:, 0:T], ps[:, 7, 0:T], ACT.Sqrt, scale=1.0 / D, bias=eps[:, :])\
                    .then_inc(rms_ready, 1)

            act.wait_ge(eps_ready, 1)
            squares(0)
            used_through(act, "w_in", 8)
            for g in range(4):
                act.copy(upad[:, g * (PAD + T) + PAD:(g + 1) * (PAD + T)], half(0, g)).then_inc(S["u_copied"], 1)
            for b in range(2):
                act.copy(tile(q1, b, 512), ps[:, 2 + b, :]).then_inc(S["qk_ready"], 1)
            used_through(act, "w_in", 16)
            for b in range(2):
                act.copy(tile(k1, b, 512), ps[:, 4 + b, :]).then_inc(S["qk_ready"], 1)

            def exps(h):
                act.wait_ge(S["biased"], h + 1)
                n = stat1[:, 6 * (h % 8):6 * (h % 8) + 6]
                p = prob[h % 2]
                act.activation(p[:, 0:P], p[:, 0:P], ACT.Exp, bias=n[:, 0:1], accum_out=n[:, 2:3])
                act.activation(p[:, P:SPAN], p[:, P:SPAN], ACT.Exp, bias=n[:, 1:2], accum_out=n[:, 3:4])\
                    .then_inc(S["prob_exp"], 1)

            def copy_pt(h):
                act.wait_ge(S["pt_done"], h + 1)
                if h >= 2:
                    act.wait_ge(S["pv_done"], h - 1)
                act.copy(probT[h % 2], ps[:, 2 + h % 2, 0:SPAN]).then_inc(S["pt_ready"], 1)

            def copy_o(h):
                lo = 64 * (h % 2)
                act.wait_ge(S["pv_done"], h + 1)
                if h == 0:
                    for k in range(2):
                        act.wait_ge(row_stored[k], 16 * (HEADS1 // 2))
                act.copy(tile(mT, 4 + h // 2)[lo:lo + DH, :], ps[lo:lo + DH, 4 + (h // 2) % 2, 0:T])\
                    .then_inc(S["mix_ready"], 1)

            for s in range(HEADS1 + 2):
                if s < HEADS1:
                    exps(s)
                if 1 <= s <= HEADS1:
                    copy_pt(s - 1)
                if s >= 2:
                    copy_o(s - 2)
            used_through(act, "w_pool", 1)
            for g in range(4):
                act.activation(tile(mT, g), half(6, g), ACT.Copy, scale=col("pool_scale", g)).then_inc(S["mix_ready"], 1)

            squares(1)
            for tt in range(TT):
                act.wait_ge(S["htok_done"], tt + 1)
                for b in range(2):
                    act.copy(mT[:, tt * D + b * BANK:tt * D + (b + 1) * BANK], ps[:, 2 * tt + b, :])\
                        .then_inc(S["htok_ready"], 1)
            for tt in range(TT):
                act.wait_ge(S["neg_top"], tt + 1)
                act.activation(r_exp[:, tt * 4:tt * 4 + 4], r_max[:, tt * 8:tt * 8 + 4], ACT.Exp,
                               bias=r_nmax[:, tt:tt + 1], accum_out=r_sum[:, tt:tt + 1]).then_inc(S["gate_exp"], 1)

            def expert_pass(level):
                base = EXPERTS * level

                def split(n, k):
                    act.wait_ge(moe_loaded[k % MOE_RAW], n * 32 + 16 * (k // MOE_RAW + 1))
                    used = n * MOE_CHUNKS + (k - MOE_SPLIT + 1)
                    if not isinstance(used, int) or used > 0:
                        act.wait_ge(S["moe_used"], used)
                    act.copy(moe_hi[:, k % MOE_SPLIT * MOE_COLS:(k % MOE_SPLIT + 1) * MOE_COLS],
                             big[:, k % MOE_RAW * MOE_COLS:(k % MOE_RAW + 1) * MOE_COLS]).then_inc(S["hi_ready"], 1)

                def gathered(n):
                    act.wait_ge(S["gathered"], n + 1)
                    for b in range(2):
                        act.copy(m_x[:, b * BANK:(b + 1) * BANK].rearrange("p (c n) -> p c n", n=P)[:, :, 0:CAP],
                                 ps[:, b, :].rearrange("p (c n) -> p c n", n=P)[:, :, 0:CAP])\
                            .then_inc(S["xg_high"], 1)

                def store(e):
                    n = e + base
                    if level or not isinstance(e, int) or e > 0:
                        act.wait_ge(S["y_stored"], n * 16)
                    for b in range(2):
                        act.wait_ge(S["yt_done"], n * 2 + b + 1)
                        act.copy(tile(m_tok, b, 512), ps[0:CAP, b, :]).then_inc(S["ytok_ready"], 1)
                    act.wait_ge(S["ytok_ready"], n * 2 + 2)
                    act.dma_start(expert_out[bass.ds(e * CAP, CAP), :], m_tok).then_inc(S["y_stored"], 16)

                def expert(e, first=False, last=False):
                    n = e + base
                    split(n, 3)
                    if not first:
                        store(e - 1)
                    for k in range(4, 10):
                        split(n, k)
                    act.wait_ge(S["moe_used"], n * MOE_CHUNKS + DT)
                    for b in range(2):
                        act.copy(tile(m_gu, b, 512), ps[:, 2 + b, :]).then_inc(S["gates_copied"], 1)
                    for b in range(2):
                        act.wait_ge(S["sig_in"], n * 2 + b + 1)
                        act.activation(tile(m_sig, b, 256), tile(m_g, b, 256), ACT.Sigmoid, scale=ALPHA)\
                            .then_inc(S["sig_ready"], 1)
                    split(n, 10)
                    if not last:
                        gathered(n + 1)
                    split(n, 11)
                    for k in range(12, 14):
                        if not last:
                            split(n, k)
                    act.wait_ge(S["moe_used"], n * MOE_CHUNKS + MOE_CHUNKS)
                    for b in range(2):
                        act.copy(tile(m_y, b, 512), ps[:, 6 + b, :]).then_inc(S["y_ready"], 1)
                    if last:
                        store(e)
                    else:
                        split(n, 14)

                for k in range(MOE_SPLIT):
                    split(base, k)
                gathered(base)
                expert(0, first=True)
                with act.Fori(1, EXPERTS - 1) as e:
                    expert(e)
                expert(EXPERTS - 1, last=True)

            expert_pass(0)
            act.wait_ge(S["count_ready"], 1)
            count = act.value_load(r_cnt, min_val=0, max_val=T)
            with ExitStack() as nest:
                for level in range(1, PASSES):
                    nest.enter_context(act.If(count > CAP * level))
                    expert_pass(level)

            def ple(k, norm):
                squares(norm)
                used_through(act, f"ple{k}", 8)
                for b in range(4):
                    act.activation(tile(mT, b, 512), ps[:, 4 + b, :], ACT.Sigmoid).then_inc(S["gate_ready"], 1)

            ple(0, 2)
            squares(3)

            squares(4)
            act.wait_ge(S["lam_in"], 1)
            act.activation(sp[:, 8:16], sp[:, 0:8], ACT.Exp, scale=-1.0).then_inc(S["lam_exp"], 1)
            used_through(act, "a_in", 16)
            for b in range(4):
                act.activation(tile(lru[1], b, 512), ps[:, 4 + b, :], ACT.Gelu_apprx_tanh).then_inc(S["yg_ready"], 1)
            for k, name in enumerate(("b_r", "b_i")):
                used_through(act, ("w_r", "w_i")[k], 1)
                for h in range(DT):
                    act.activation(tile(lru[2 + k], h), half(4 * k, h), ACT.Sigmoid, bias=col(name, h))\
                        .then_inc(S["ri_ready"], 1)
            act.wait_ge(S["ri_ready"], 16)
            act.wait_ge(S["lam_in"], 2)
            for h in range(DT):
                act.activation(tile(lru[4], h), tile(lru[2], h), ACT.Exp, scale=sp[:, 72 + h:73 + h])
                act.activation(tile(lru[5], h), tile(lru[2], h), ACT.Tanh, scale=sp[:, 80 + h:81 + h])\
                    .then_inc(S["lru_exp"], 1)
            for b in range(4):
                act.wait_ge(S["lru_e"], b + 1)
                act.activation(tile(lru[6], b, 512), tile(lru[5], b, 512), ACT.Sqrt).then_inc(S["lru_sqrt"], 1)

            def peer(L, norm):
                squares(norm)
                for k in range(2):
                    used_through(act, f"wq{L}", 8 * (k + 1))
                    for b in range(4):
                        act.copy(pq[:, (4 * k + b) * 512:(4 * k + b + 1) * 512], ps[:, 4 * k + b, :])\
                            .then_inc(S["pq_ready"], 1)
                act.wait_ge(S["s_done"], L + 1)
                for b in range(4):
                    act.copy(tile(mT, b, 512), ps[:, b, :]).then_inc(S["bank_read"], 1)
                n = first[f"u{L}"]
                with act.Fori(0, CHUNKS // RING) as i:
                    for k in range(RING // 2):
                        act.wait_ge(w_used, n + 2 * k + 2 + i * RING)
                        act.activation(big[:, bass.ds(i * (RING * T) + k * BANK, BANK)], ps[:, k, :],
                                       ACT.Gelu_apprx_tanh).then_inc(S["bank_read"], 1)
                act.wait_ge(S["cv_ready"], L + 1)
                act.activation(cv, cv, ACT.Exp).then_inc(S["cv_exp"], 1)

            peer(0, 5)
            ple(1, 6)

            squares(7)
            used_through(act, "kv", 8)
            for b in range(4):
                act.copy(tile(k2, b, 512), ps[:, b, :]).then_inc(S["k2_ready"], 1)
            used_through(act, "bq", 8)
            for b in range(4):
                act.activation(tile(q2, b, 512), ps[:, b, :], ACT.Copy, scale=DH ** -0.5).then_inc(S["q2_ready"], 1)
            for g in range(HEADS2 // 4 + 1):
                if g < HEADS2 // 4:
                    for h in range(4 * g, 4 * g + 4):
                        a = st[h % 4]
                        act.wait_ge(S["z_done"], h + 1)
                        step.link(act.activation(a, ps[:, h % 4, 0:SPAN], ACT.Abs))
                        step.link(act.activation(a, a, ACT.Exp, scale=-1.0))
                        if h >= 4:
                            act.wait_ge(S["spm_ready"], h - 3)
                        act.activation(st[16 + h % 4], a, ACT.Ln, bias=1.0).then_inc(S["a_exp"], 1)
                    for h in range(4 * g, 4 * g + 4):
                        act.wait_ge(S["arg_ready"], h + 1)
                        if h >= 4:
                            act.wait_ge(S["o_done"], h - 3)
                        act.activation(st[12 + h % 4], st[20 + h % 4], ACT.Exp).then_inc(S["w_exp"], 1)
                if g < HEADS2 // 4:
                    for h in range(4 * g, 4 * g + 4):
                        lo = 64 * (h % 2)
                        act.wait_ge(S["o_done"], h + 1)
                        act.copy(tile(mT, h // 2)[lo:lo + DH, :], ps[lo:lo + DH, 6 + (h // 2) % 2, 0:T])\
                            .then_inc(S["o_ready"], 1)
            peer(1, 8)
            ple(2, 9)
            squares(10)

        @block.vector
        def _(dve):
            step = Tally(dve, dve_step)
            link, mark = step.link, step.mark

            def norm(k, gains, dsts=(hT,), sem_=h_ready):
                dve.wait_ge(rms_ready, k + 1)
                link(dve.reciprocal(rs[:, T:2 * T], rs[:, 0:T]))
                for dst, (name, at) in zip(dsts, gains):
                    for c in range(DT):
                        dve.scalar_tensor_tensor(tile(dst, c), tile(xT, c), col(name, at + c), rs[:, T:2 * T],
                                                 op0=ALU.mult, op1=ALU.mult).then_inc(sem_, 1)

            def add_to_x(seg, chunks):
                used_through(dve, seg, chunks)
                for b in range(4):
                    dve.tensor_tensor(tile(xT, b, 512), ps[:, b, :], tile(xT, b, 512), ALU.add).then_inc(x_ready, 1)

            dve.memset(eps[:, :], EPS).then_inc(eps_ready, 1)
            dve.wait_ge(attn_loaded, 48)
            dve.wait_ge(con_loaded, 16)
            for h in range(HEADS1):
                dve.tensor_scalar(rb[:, h * P:(h + 1) * P], ones[0:32, :], relb[:, h:h + 1], None, ALU.mult)\
                    .then_inc(S["rb_ready"], 1)
            dve.memset(upad, 0.0).then_inc(dve_step, 1)
            step.n += 1
            dve.wait_ge(x_loaded, 16)
            dve.wait_ge(par_loaded, 16)
            norm(0, [("g_mix", 0)])
            dve.wait_ge(h_ready, DT)
            for h in range(HEADS1):
                dve.wait_ge(S["row_done"], h + 1)
                if h >= 2:
                    dve.wait_ge(row_stored[h % 2], 16 * (h // 2))
                dve.tensor_tensor(row[h % 2], ps[:, 4 + h % 2, 0:SPAN], cmask, ALU.add).then_inc(S["row_ready"], 1)
            dve.wait_ge(S["u_copied"], 4)
            up = upad.rearrange("p (g t) -> p g t", g=4)
            s0 = winsum.rearrange("p (g t) -> p g t", g=4)
            s1 = winsum2.rearrange("p (g t) -> p g t", g=4)
            E = PAD + T
            link(dve.tensor_tensor(s0[:, :, 1:E], up[:, :, 1:E], up[:, :, 0:E - 1], ALU.add))
            link(dve.tensor_tensor(s1[:, 1:4, 3:E], s0[:, 1:4, 3:E], s0[:, 1:4, 1:E - 2], ALU.add))
            link(dve.tensor_tensor(s0[:, 2:4, 7:E], s1[:, 2:4, 7:E], s1[:, 2:4, 3:E - 4], ALU.add))
            link(dve.tensor_tensor(s1[:, 3, 15:E], s0[:, 3, 15:E], s0[:, 3, 7:E - 8], ALU.add))
            for g, w in enumerate(POOL_WINDOWS):
                s = (s0, s1)[g % 2][:, g, PAD:E]
                link(dve.tensor_scalar(s[:, PAD:T], s[:, PAD:T], 1.0 / w, None, ALU.mult))
                link(dve.tensor_tensor(s[:, 0:PAD], s[:, 0:PAD], con[:, C_INV + g * PAD:C_INV + (g + 1) * PAD], ALU.mult))
                dve.tensor_tensor(up[:, g, PAD:E], s, up[:, g, PAD:E], ALU.subtract).then_inc(S["pooled_ready"], 1)
            used_through(dve, "w_in", 16)
            for tt in range(TT):
                dve.tensor_copy(tile(v1, tt, 512), ps[:, 6 + tt, :]).then_inc(S["v_ready"], 1)

            def biased(h):
                dve.wait_ge(S["score_done"], h + 1)
                dve.wait_ge(S["toep_loaded"], 32 * HEADS1)
                if h >= 2:
                    dve.wait_ge(S["pt_done"], h - 1)
                n = stat1[:, 6 * h:6 * h + 6]
                p = prob[h % 2]
                link(dve.scalar_tensor_tensor(p, ps[:, h % 2, 0:SPAN], DH ** -0.5, toep[:, h * SPAN:(h + 1) * SPAN],
                                              op0=ALU.mult, op1=ALU.add))
                mark(dve.tensor_reduce(n[:, 4:5], p[:, 0:P], AX_X, ALU.max))
                link(dve.tensor_reduce(n[:, 5:6], p[:, P:SPAN], AX_X, ALU.max))
                dve.tensor_scalar(n[:, 0:2], n[:, 4:6], -1.0, None, ALU.mult).then_inc(S["biased"], 1)

            def normalised(h):
                n = stat1[:, 6 * h:6 * h + 6]
                p = prob[h % 2]
                dve.wait_ge(S["prob_exp"], h + 1)
                link(dve.reciprocal(n[:, 4:6], n[:, 2:4]))
                link(dve.tensor_scalar(p[:, 0:P], p[:, 0:P], n[:, 4:5], None, ALU.mult))
                dve.tensor_scalar(p[:, P:SPAN], p[:, P:SPAN], n[:, 5:6], None, ALU.mult).then_inc(S["prob_ready"], 1)

            for s in range(HEADS1 + 1):
                if s < HEADS1:
                    biased(s)
                if s >= 1:
                    normalised(s - 1)
            add_to_x("w_out", 8)

            norm(1, [("g_ffn", 0)])
            used_through(dve, "w_router", 1)
            dve.wait_ge(bias_loaded, 48)
            i32c = iota[:, 0:EXPERTS]
            for tt in range(TT):
                lg = r_logit[:, tt * 32:(tt + 1) * 32]
                top, idx = r_max[:, tt * 8:tt * 8 + 8], r_idx[:, tt * 8:tt * 8 + 8].bitcast(U32)
                link(dve.tensor_tensor(lg, ps[:, 4, tt * 32:(tt + 1) * 32], r_bias, ALU.add))
                link(dve.max(top, lg))
                dve.tensor_scalar(r_nmax[:, tt:tt + 1], top[:, 0:1], -1.0, None, ALU.mult).then_inc(S["neg_top"], 1)
                link(dve.max_index(idx, top, lg))
                link(dve.tensor_copy(r_idxf[:, tt * 4:tt * 4 + 4], idx[:, 0:4]))
                hots = r_hot[:, tt * 128:(tt + 1) * 128].rearrange("p (k e) -> p k e", k=TOP_K)
                for k in range(TOP_K):
                    mark(dve.tensor_scalar(hots[:, k, :], i32c, r_idxf[:, tt * 4 + k:tt * 4 + k + 1], None, ALU.is_equal))
                step.wait()
                dve.tensor_reduce(r_mask[:, tt * 32:(tt + 1) * 32], hots.rearrange("p k e -> p e k"), AX_X, ALU.add)\
                    .then_inc(S["mask_ready"], 1)
            for tt in range(TT):
                dve.wait_ge(S["gate_exp"], tt + 1)
                gate = r_gate[:, tt * 4:tt * 4 + 4]
                link(dve.reciprocal(r_rec[:, tt:tt + 1], r_sum[:, tt:tt + 1]))
                link(dve.tensor_scalar(gate, r_exp[:, tt * 4:tt * 4 + 4], r_rec[:, tt:tt + 1], None, ALU.mult))
                gm = r_gmat[:, tt * 32:(tt + 1) * 32]
                hot_k = lambda k: r_hot[:, tt * 128 + k * 32:tt * 128 + (k + 1) * 32]
                link(dve.tensor_scalar(gm, hot_k(0), gate[:, 0:1], None, ALU.mult))
                for k in range(1, TOP_K):
                    ins = dve.scalar_tensor_tensor(gm, hot_k(k), gate[:, k:k + 1], gm, op0=ALU.mult, op1=ALU.add)
                    if k < TOP_K - 1:
                        link(ins)
                    else:
                        ins.then_inc(S["gmat_in"], 1)
            dve.wait_ge(S["rank_done"], 1)
            link(dve.tensor_reduce(r_cntf, ps[0:1, 5, 64:96], AX_X, ALU.max))
            dve.tensor_copy(r_cnt, r_cntf).then_inc(S["count_ready"], 1)
            for tt in range(TT):
                rank, mask = ps[:, 5, tt * 32:(tt + 1) * 32], r_mask[:, tt * 32:(tt + 1) * 32]
                link(dve.scalar_tensor_tensor(r_rank1[:, tt * 32:(tt + 1) * 32], rank, 1.0, mask,
                                              op0=ALU.add, op1=ALU.mult))
                hots = r_hot[:, tt * 128:(tt + 1) * 128].rearrange("p (k e) -> p k e", k=TOP_K)
                tmp = r_tmp[:, tt * 128:(tt + 1) * 128].rearrange("p (k e) -> p k e", k=TOP_K)
                link(dve.tensor_tensor(tmp, rank.unsqueeze(1).broadcast_to((P, TOP_K, EXPERTS)), hots, ALU.mult))
                link(dve.tensor_reduce(r_slotf[:, tt * 4:tt * 4 + 4], tmp, AX_X, ALU.add))
            link(dve.tensor_scalar(r_pass, r_slotf, float(CAP), None, ALU.is_ge))
            for level in range(2, PASSES):
                link(dve.tensor_scalar(r_step, r_slotf, float(CAP * level), None, ALU.is_ge))
                link(dve.tensor_tensor(r_pass, r_pass, r_step, ALU.add))
            link(dve.scalar_tensor_tensor(r_slotf, r_pass, -float(CAP), r_slotf, op0=ALU.mult, op1=ALU.add))
            link(dve.scalar_tensor_tensor(r_slotf, r_idxf, float(CAP), r_slotf, op0=ALU.mult, op1=ALU.add))
            dve.tensor_copy(r_slot, r_slotf).then_inc(S["slots_ready"], 1)

            def diagonals(level, link):
                link(dve.scalar_tensor_tensor(r_step, r_pass, float(level), r_gate, op0=ALU.is_equal, op1=ALU.mult))
                for k in range(TT * TOP_K):
                    dve.tensor_scalar(r_diag[:, k * P:(k + 1) * P], ident, r_step[:, k:k + 1], None, ALU.mult)\
                        .then_inc(S["diag_ready"], 1)

            diagonals(0, link)
            dve.wait_ge(S["gmat_done"], 1)
            dve.tensor_copy(r_gmatT, ps[0:32, 6, 0:T]).then_inc(S["gmat_ready"], 1)

            moe = Tally(dve, S["moe_step"])

            def expert_pass(level):
                base = EXPERTS * level

                def select(e):
                    for tt in range(TT):
                        ins = dve.tensor_scalar(m_sel[:, tt * P:(tt + 1) * P], iota,
                                                float(level * CAP + 1), r_rank1[:, bass.ds(e + tt * EXPERTS, 1)],
                                                ALU.add, ALU.is_equal)
                    ins.then_inc(S["sel_ready"], 1)

                def split(n, k):
                    dve.wait_ge(S["hi_ready"], n * MOE_CHUNKS + k + 1)
                    at = slice(k % MOE_SPLIT * MOE_COLS, (k % MOE_SPLIT + 1) * MOE_COLS)
                    dve.tensor_tensor(moe_lo[:, at], big[:, k % MOE_RAW * MOE_COLS:(k % MOE_RAW + 1) * MOE_COLS],
                                      moe_hi[:, at], ALU.subtract).then_inc(S["split_ready"], 1)

                def gathered(n):
                    for b in range(2):
                        dve.wait_ge(S["xg_high"], n * 2 + b + 1)
                        x = m_x[:, b * BANK:(b + 1) * BANK].rearrange("p (c n) -> p c n", n=P)
                        dve.tensor_tensor(x[:, :, CAP:P], ps[:, b, :].rearrange("p (c n) -> p c n", n=P)[:, :, 0:CAP],
                                          x[:, :, 0:CAP], ALU.subtract).then_inc(S["xg_ready"], 1)

                def expert(e, last=False):
                    n = e + base
                    split(n, 3)
                    if not last:
                        select(e + 1)
                    for k in range(4, 10):
                        split(n, k)
                    dve.wait_ge(S["moe_used"], n * MOE_CHUNKS + DT)
                    for b in range(2):
                        dve.tensor_copy(tile(m_gu, 2 + b, 512), ps[:, 4 + b, :]).then_inc(S["ups_copied"], 1)
                    for b in range(2):
                        dve.wait_ge(S["turned"], n * 2 + b + 1)
                        three = lambda x: x[:, b * 256:(b + 1) * 256].rearrange("p (f n) -> p f n", n=CAP)
                        bank = lambda k: ps[:, k, :].rearrange("p (f n) -> p f n", n=P)[:, :, 0:CAP]
                        bias = lambda k: moe_bias[:, bass.ds(e * 16 + k, 4)].unsqueeze(2).broadcast_to((P, 4, CAP))
                        g, u, sig, h = (three(x) for x in (m_g, m_u, m_sig, m_hid))
                        hh = m_h[:, b * BANK:(b + 1) * BANK].rearrange("p (f n) -> p f n", n=P)
                        moe.link(dve.tensor_tensor(g, bank(2 + b), bias(4 * b), ALU.add))
                        dve.tensor_scalar(g, g, LIMIT, None, ALU.min).then_inc(S["sig_in"], 1)
                        moe.link(dve.tensor_tensor(u, bank(4 + b), bias(8 + 4 * b), ALU.add))
                        moe.link(dve.tensor_scalar(u, u, LIMIT, -LIMIT, ALU.min, ALU.max))
                        dve.wait_ge(S["sig_ready"], n * 2 + b + 1)
                        moe.link(dve.tensor_tensor(sig, sig, g, ALU.mult))
                        moe.link(dve.scalar_tensor_tensor(h, u, 1.0, sig, op0=ALU.add, op1=ALU.mult))
                        moe.link(dve.tensor_copy(hh[:, :, 0:CAP], h))
                        dve.tensor_tensor(hh[:, :, CAP:P], h, hh[:, :, 0:CAP], ALU.subtract)\
                            .then_inc(S["hid_ready"], 1)
                    split(n, 10)
                    if not last:
                        gathered(n + 1)
                    split(n, 11)
                    if not last:
                        for k in range(12, 15):
                            split(n, k)

                select(0)
                for k in range(MOE_SPLIT):
                    split(base, k)
                gathered(base)
                expert(0)
                with dve.Fori(1, EXPERTS - 1) as e:
                    moe.enter(e, 12, 1)
                    expert(e)
                moe.leave(EXPERTS - 2)
                expert(EXPERTS - 1, last=True)

            expert_pass(0)
            dve.wait_ge(S["count_ready"], 1)
            count = dve.value_load(r_cnt, min_val=0, max_val=T)
            with ExitStack() as nest:
                for level in range(1, PASSES):
                    nest.enter_context(dve.If(count > CAP * level))
                    dve.wait_ge(S["combined"], level)
                    for b in range(4):
                        dve.tensor_tensor(tile(xT, b, 512), ps[:, b, :], tile(xT, b, 512), ALU.add)\
                            .then_inc(S["added"], 1)
                    diagonals(level, moe.link)
                    expert_pass(level)
            dve.wait_ge(S["combined"], 1)
            with ExitStack() as nest:
                for level in range(1, PASSES):
                    nest.enter_context(dve.If(count > CAP * level))
                    dve.wait_ge(S["combined"], level + 1)
            for b in range(4):
                dve.tensor_tensor(tile(xT, b, 512), ps[:, b, :], tile(xT, b, 512), ALU.add).then_inc(x_ready, 1)

            def ple(k, norm_no, gain):
                norm(norm_no, [gain])
                for b in range(4):
                    dve.wait_ge(S["gate_ready"], 4 * k + b + 1)
                    link(dve.tensor_tensor(tile(mT, b, 512), ps[:, b, :], tile(mT, b, 512), ALU.mult))
                    dve.tensor_tensor(tile(xT, b, 512), tile(mT, b, 512), tile(xT, b, 512), ALU.add).then_inc(x_ready, 1)

            ple(0, 2, ("g_ple", 0))
            dve.wait_ge(rms_ready, 4)
            link(dve.reciprocal(rs[:, T:2 * T], rs[:, 0:T]))
            for c in range(DT):
                ins = dve.scalar_tensor_tensor(tile(xT, c), tile(xT, c), col("g_final", c), rs[:, T:2 * T],
                                               op0=ALU.mult, op1=ALU.mult)
                if c % 2:
                    ins.then_inc(x_ready, 1)

            norm(4, [("norm_mix", 0)])
            lam = par[:, PARAMS["lam"][0]:PARAMS["lam"][0] + DT]
            link(dve.tensor_scalar(sp[:, 16:24], lam, -1.0, None, ALU.mult))
            dve.tensor_tensor(sp[:, 0:8], lam, sp[:, 16:24], ALU.max).then_inc(S["lam_in"], 1)
            dve.wait_ge(S["lam_exp"], 1)
            y, z, z2, acc = sp[:, 8:16], sp[:, 24:32], sp[:, 32:40], sp[:, 40:48]
            link(dve.tensor_scalar(z, y, 2.0, None, ALU.add))
            link(dve.reciprocal(z2, z))
            link(dve.tensor_tensor(z, y, z2, ALU.mult))
            link(dve.tensor_tensor(z2, z, z, ALU.mult))
            link(dve.tensor_scalar(acc, z2, 1.0 / 17, 1.0 / 15, ALU.mult, ALU.add))
            for k in (13, 11, 9, 7, 5, 3, 1):
                link(dve.tensor_tensor(acc, acc, z2, ALU.mult))
                link(dve.tensor_scalar(acc, acc, 1.0 / k, None, ALU.add))
            link(dve.tensor_tensor(acc, acc, z, ALU.mult))
            link(dve.tensor_scalar(sp[:, 16:24], sp[:, 16:24], 0.0, None, ALU.max))
            link(dve.scalar_tensor_tensor(acc, acc, 2.0, sp[:, 16:24], op0=ALU.mult, op1=ALU.add))
            link(dve.tensor_scalar(sp[:, 72:80], acc, -8.0, None, ALU.mult))
            dve.tensor_scalar(sp[:, 80:88], acc, 8.0, None, ALU.mult).then_inc(S["lam_in"], 1)
            used_through(dve, "a_in", 8)
            marks = [mark(dve.tensor_scalar(tile(lru[0], c), half(0, c), col("conv_w", 3 * DT + c), col("conv_b", c),
                                            ALU.mult, ALU.add)) for c in range(DT)]
            for back in range(1, CONV):
                for c in range(DT):
                    step.wait(marks[c])
                    dst = tile(lru[0], c)[:, back:T]
                    ins = dve.scalar_tensor_tensor(dst, half(0, c)[:, 0:T - back], col("conv_w", (3 - back) * DT + c), dst,
                                                   op0=ALU.mult, op1=ALU.add)
                    if back < CONV - 1:
                        marks[c] = mark(ins)
                    else:
                        ins.then_inc(S["conv_ready"], 1)
            dve.wait_ge(S["conv_ready"], DT)
            for b in range(4):
                dve.wait_ge(S["lru_exp"], 2 * b + 2)
                a, th = tile(lru[4], b, 512), tile(lru[5], b, 512)
                link(dve.tensor_tensor(tile(lru[6], b, 512), a, a, ALU.mult))
                dve.scalar_tensor_tensor(th, tile(lru[6], b, 512), 1.0, th, op0=ALU.add, op1=ALU.mult)\
                    .then_inc(S["lru_e"], 1)
            for b in range(4):
                dve.wait_ge(S["ri_ready"], 16)
                link(dve.tensor_tensor(tile(lru[3], b, 512), tile(lru[3], b, 512), tile(lru[0], b, 512), ALU.mult))
                dve.wait_ge(S["lru_sqrt"], b + 1)
                link(dve.tensor_tensor(tile(lru[3], b, 512), tile(lru[3], b, 512), tile(lru[6], b, 512), ALU.mult))
                for c in (2 * b, 2 * b + 1):
                    link(dve.tensor_tensor_scan(tile(lru[7], c), tile(lru[4], c), tile(lru[3], c), 0.0,
                                                ALU.mult, ALU.add))
                    dve.tensor_tensor(tile(mT, c), tile(lru[7], c), tile(lru[1], c), ALU.mult)\
                        .then_inc(S["gated_ready"], 1)
            add_to_x("a_out", 8)

            def top16(vals, idx, src, tmp):
                link(dve.max(vals[:, 0:8], src))
                mark(dve.max_index(idx[:, 0:8], vals[:, 0:8], src))
                link(dve.match_replace(tmp, vals[:, 0:8], src, -3e38))
                link(dve.max(vals[:, 8:16], tmp))
                link(dve.max_index(idx[:, 8:16], vals[:, 8:16], tmp))

            def peer(L, norm_no, gain):
                norm(norm_no, [gain])
                for tt in (1, 0):
                    used_through(dve, f"keys{L}", 2)
                    if tt == 0:
                        dve.wait_ge(S["bank_read"], READS * L + 4)
                    for hp in range(16):
                        src = ps[:, 4 + hp // 4, (hp % 4) * P:(hp % 4 + 1) * P] if tt else mT[:, hp * P:(hp + 1) * P]
                        top16(sv[:, hp * 16:hp * 16 + 16], si[:, hp * 16:hp * 16 + 16], src, p_tmp)
                    link(dve.tensor_copy(sif, si))
                    vals = cv[:, tt * P:(tt + 1) * P]
                    for h in range(PH):
                        a = sv[:, 32 * h:32 * h + 16].unsqueeze(2).broadcast_to((P, 16, 16))
                        b = sv[:, 32 * h + 16:32 * h + 32].unsqueeze(1).broadcast_to((P, 16, 16))
                        link(dve.tensor_tensor(cand.rearrange("p (a b) -> p a b", a=16), a, b, ALU.add))
                        top16(vals[:, h * 16:h * 16 + 16], ci[:, h * 16:h * 16 + 16], cand, cand2)
                    for which in range(2):
                        if which == 0:
                            link(dve.tensor_scalar(cc, ci, 4, None, ALU.logical_shift_right))
                        else:
                            link(dve.tensor_scalar(cc, ci, 15, None, ALU.bitwise_and))
                        link(dve.tensor_copy(ccf, cc))
                        place = iota[:, 0:16].unsqueeze(1).broadcast_to((P, P, 16))
                        pk = pick.rearrange("p (k i) -> p k i", i=16)
                        link(dve.tensor_tensor(pk, ccf.unsqueeze(2).broadcast_to((P, P, 16)), place, ALU.is_equal))
                        for h in range(PH):
                            ids = sif[:, 32 * h + 16 * which:32 * h + 16 * which + 16]
                            mark(dve.tensor_tensor(pk[:, h * 16:h * 16 + 16, :], pk[:, h * 16:h * 16 + 16, :],
                                                   ids.unsqueeze(1).broadcast_to((P, 16, 16)), ALU.mult))
                        step.wait()
                        link(dve.tensor_reduce(i12[:, (which * TT + tt) * P:(which * TT + tt + 1) * P], pk, AX_X, ALU.add))
                    v3 = vals.rearrange("p (h k) -> p h k", h=PH)
                    link(dve.tensor_copy(p_sum[:, 0:8], v3[:, :, 0]))
                    ins = dve.tensor_tensor(v3, v3, p_sum[:, 0:8].unsqueeze(2).broadcast_to((P, PH, 16)), ALU.subtract)
                    if tt:
                        link(ins)
                    else:
                        ins.then_inc(S["cv_ready"], 1)
                dve.wait_ge(S["cv_exp"], L + 1)
                c3 = cv.rearrange("p (h k) -> p h k", k=16)
                link(dve.tensor_reduce(p_sum, c3, AX_X, ALU.add))
                link(dve.reciprocal(p_sum, p_sum))
                dve.tensor_tensor(c3, c3, p_sum.unsqueeze(2).broadcast_to((P, 2 * PH, 16)), ALU.mult)\
                    .then_inc(S["sel_done"], 1)
                dve.wait_ge(S["selT_done"], L + 1)
                for k in range(3):
                    dve.tensor_copy(selT[:, k * T:(k + 1) * T], ps[:, 4 + k, 0:T]).then_inc(S["selT_ready"], 1)
                dve.wait_ge(S["selT_ready"], 3 * L + 3)
                dve.wait_ge(S["bank_read"], READS * (L + 1))
                act3 = big[:, :].rearrange("p (j t) -> p j t", t=T)
                with dve.Fori(0, T // BODY) as i:
                    for s in range(BODY):
                        t = i * BODY + s
                        dve.tensor_scalar(mT[:, s * P:(s + 1) * P], iota, selT[:, bass.ds(t, 1)], None, ALU.is_equal)
                        dve.tensor_scalar(mT[:, (BODY + s) * P:(BODY + s + 1) * P], iota, selT[:, bass.ds(t + T, 1)],
                                          selT[:, bass.ds(t + 2 * T, 1)], ALU.is_equal, ALU.mult)\
                            .then_inc(S["oh_ready"], 1)
                    for g in range(BODY // GROUP):
                        dve.wait_ge(S["g_done"], T * L + (g + 1) * GROUP + i * BODY)
                        dst = act3[:, :, bass.ds(i * BODY + g * GROUP, GROUP)]
                        dve.tensor_tensor(dst, ps[:, 4 + g, :].rearrange("p (t j) -> p j t", t=GROUP), dst, ALU.mult)\
                            .then_inc(S["g_used"], 1)
                used_through(dve, f"v{L}", CHUNKS)
                for b in range(4):
                    dve.tensor_copy(tile(xT, b, 512), ps[:, b, :]).then_inc(x_ready, 1)

            peer(0, 5, ("norm_ffn", 0))
            ple(1, 6, ("norm_ple", 0))

            norm(7, [("kv_norm", 0), ("norm_mix", DT)], (hT, mT))
            used_through(dve, "kv", 16)
            for b in range(4):
                dve.tensor_copy(tile(v2, b, 512), ps[:, 4 + b, :]).then_inc(S["v2_ready"], 1)
            mask2 = triu.unsqueeze(1).broadcast_to((P, 2, P))
            diag = lambda x: x.rearrange("p (k t) -> p k t", k=3)[:, 0:3:2, :]
            for g in range(HEADS2 // 4):
                for h in range(4 * g, 4 * g + 4):
                    dve.wait_ge(S["a_exp"], h + 1)
                    if h >= 4:
                        dve.wait_ge(S["rc_done"], h - 3)
                    link(dve.scalar_tensor_tensor(st[4 + h % 4], ps[:, h % 4, 0:SPAN], 0.0, st[16 + h % 4],
                                                  op0=ALU.max, op1=ALU.add))
                    dve.tensor_tensor(diag(st[8 + h % 4]), diag(st[4 + h % 4]), mask2, ALU.mult)\
                        .then_inc(S["spm_ready"], 1)
                for h in range(4 * g, 4 * g + 4):
                    if h >= 4:
                        dve.wait_ge(S["w_exp"], h - 3)
                    link(dve.tensor_tensor(st[20 + h % 4], ps[:, h % 4, 0:SPAN], st[4 + h % 4], ALU.subtract))
                    dve.wait_ge(S["rc_done"], h + 1)
                    dve.tensor_tensor(st[20 + h % 4], ps[:, 4 + h % 2, 0:SPAN], st[20 + h % 4], ALU.add)\
                        .then_inc(S["arg_ready"], 1)
            add_to_x("bo", 8)
            peer(1, 8, ("norm_ffn", DT))
            ple(2, 9, ("norm_ple", DT))
            norm(10, [("final", 0)], (mT,), S["out_ready"])

        @block.gpsimd
        def _(pool):
            for h in range(HEADS1):
                pool.wait_ge(S["row_ready"], h + 1)
                pool.dma_start(toeplitz[h], row[h % 2]).then_inc(row_stored[h % 2], 16)
            for h in range(HEADS1):
                pool.wait_ge(row_stored[h % 2], 16 * (HEADS1 // 2))
                flat = toeplitz[h].rearrange("p x -> (p x)")
                skew = flat[0:P * (SPAN - 1)].rearrange("(p x) -> p x", p=P)
                dst = toep[:, h * SPAN:(h + 1) * SPAN]
                pool.dma_start(dst[:, 0:P], skew[:, P - 1 + P:2 * P - 1 + P]).then_inc(S["toep_loaded"], 16)
                pool.dma_start(dst[:, P:SPAN], skew[:, P - 1:P - 1 + T]).then_inc(S["toep_loaded"], 16)
            def fetch(level):
                pool.wait_ge(S["y_stored"], 16 * EXPERTS * (level + 1))
                for k in range(TT * TOP_K):
                    pool.indirect_dma_start(out=fetched[:, k * D:(k + 1) * D], out_offset=None, in_=expert_out,
                                            in_offset=bass.IndirectOffsetOnAxis(ap=r_slot[:, k:k + 1], axis=0))\
                        .then_inc(S["y_fetched"], 16)

            pool.wait_ge(S["slots_ready"], 1)
            fetch(0)
            count = pool.value_load(r_cnt, min_val=0, max_val=T)
            with ExitStack() as nest:
                for level in range(1, PASSES):
                    nest.enter_context(pool.If(count > CAP * level))
                    fetch(level)
            mask2 = triu.unsqueeze(1).broadcast_to((P, 2, P))
            for h in range(HEADS2):
                pool.wait_ge(S["w_exp"], h + 1)
                a = st[12 + h % 4].rearrange("p (k t) -> p k t", k=3)[:, 0:3:2, :]
                pool.tensor_tensor(a, a, mask2, ALU.mult).then_inc(S["a_ready"], 1)


def kernel(**inputs):
    import concourse.bacc as bacc
    from concourse.bass_utils import run_bass_kernel_spmd

    a = {k: np.asarray(v) for k, v in inputs.items()}

    def cols(v):
        v = v.reshape(-1, v.shape[-1] // P, P)
        return v.transpose(2, 0, 1).reshape(P, -1)

    def t_form(v):
        return v.reshape(T, -1, P).transpose(2, 1, 0).reshape(P, -1)

    named = {
        "g_mix": a["g_mix"], "g_ffn": a["g_ffn"], "g_ple": a["g_ple"], "g_final": a["g_final"],
        "pool_scale": a["pool_scale"], "norm_mix": a["norm_mix_2"], "conv_w": a["a_conv_w_2"][0],
        "conv_b": a["a_conv_b_2"], "b_r": a["a_b_r_2"], "b_i": a["a_b_i_2"], "lam": a["a_lambda_2"],
        "kv_norm": a["kv_norm_2"], "norm_ffn": a["norm_ffn_2"], "norm_ple": a["norm_ple_2"],
        "final": a["final_norm_2"],
    }
    base, twice, reach, hot = constants()
    arrays = {
        "x": t_form(a["x"][0]),
        "consts": base, "twice": twice, "reach": reach, "hot": hot,
        "params": np.concatenate([cols(np.atleast_2d(named[n])) for n in PARAMS], axis=1),
        "rel_bias": a["rel_bias"],
        "w_in": a["w_in"][0],
        "w_pool": a["w_pool"][0].transpose(1, 0, 2).reshape(P, -1),
        "w_out": a["w_out"][0],
        "w_router": a["w_router"][0].reshape(DT, P, EXPERTS).transpose(1, 0, 2).reshape(P, -1),
        "b_router": a["b_router"][0],
        "w_gate_up": a["w_gate_up"][0], "w_down": a["w_down"][0], "b_down": a["b_down"][0],
        "b_gate_up": cols(a["b_gate_up"][0]),
        "p0": t_form(a["p"][0, 0]), "w_ple_gate": a["w_ple_gate"][0], "w_ple_proj": a["w_ple_proj"][0],
        "p2": np.stack([t_form(a["p_2"][L, 0]) for L in range(2)]),
        "ple_w_gate": a["ple_w_gate_2"], "ple_w_proj": a["ple_w_proj_2"],
        "a_w_in": np.concatenate([a["a_w_in_2"][0][:, D:], a["a_w_in_2"][0][:, :D]], axis=1),
        "w_r": a["a_w_r_2"][0].transpose(1, 0, 2).reshape(P, -1),
        "w_i": a["a_w_i_2"][0].transpose(1, 0, 2).reshape(P, -1),
        "a_w_out": a["a_w_out_2"][0],
        "w_kv": a["w_kv_2"], "b_w_q": a["b_w_q_2"][0], "b_w_o": a["b_w_o_2"][0],
        "peer_w_q": a["peer_w_q_2"],
        "sub_keys": a["peer_sub_keys_2"].reshape(2, 16, P, P).transpose(0, 3, 1, 2).reshape(2, P, -1),
    }
    for L in range(2):
        arrays[f"u{L}"] = a["peer_u_2"][L].reshape(P, P, DT, P).transpose(1, 3, 2, 0).reshape(P, P, D)
        arrays[f"v{L}"] = a["peer_v_2"][L].reshape(P, P, D).transpose(1, 0, 2)
    arrays = {k: np.ascontiguousarray(v) for k, v in arrays.items()}

    nc = bacc.Bacc("TRN2", target_bir_lowering=False, num_devices=1)
    io = {k: nc.dram_tensor(f"in_{k}", v.shape, mybir.dt.from_np(v.dtype), kind="ExternalInput").ap()
          for k, v in arrays.items()}
    out = nc.dram_tensor("out", (P, W), F32, kind="ExternalOutput").ap()
    program(nc, io, out)
    r = run_bass_kernel_spmd(nc, [{f"in_{k}": v for k, v in arrays.items()}], core_ids=[0])
    y = r.results[0]["out"]
    return y.reshape(P, DT, T).transpose(2, 1, 0).reshape(1, T, D)
```

```python
from contextlib import ExitStack

import numpy as np

import concourse.bass as bass
import concourse.mybir as mybir

F32 = mybir.dt.float32
F32R = mybir.dt.float32r
BF16 = mybir.dt.bfloat16
I32 = mybir.dt.int32
U32 = mybir.dt.uint32
ACT = mybir.ActivationFunctionType
ALU = mybir.AluOpType
AX_X = mybir.AxisListType.X

P = 128
T = 256
D = 1024
DT = D // P
TT = T // P
W = DT * T
BANK = 512
EPS = 1e-6
NEG = -1e30

RING = 8
SLOT = 1024

HEADS1, DH = 8, 64
SPAN = 3 * P
POOL_WINDOWS = (2, 4, 8, 16)
PAD = 16

EXPERTS, TOP_K = 32, 4
CAP = 64
PASSES = T // CAP
LIMIT, ALPHA = 7.0, 1.702
MOE_CHUNKS, MOE_COLS = 12, 2048
MOE_RAW, MOE_SPLIT = 6, 3
MOE_DVE = 1536

HEADS2 = 16
CONV = 4

PH, PTOP, PKEYS = 8, 16, 128
CHUNKS = PKEYS
GROUP = 4
TOKENS = 16
GROUPS = TOKENS // GROUP
BODY = 8
EXP_BODY, TURN_BODY, COPY_BODY = 10, 12, 13
POOL_BODIES = 6
RAW, SPLIT = 4, 2
READS = 4 + CHUNKS // 2

C_IDENT, C_ONES, C_TRIU, C_NTRI, C_NONES, C_IOTA = (P * k for k in range(6))
C_INV = 6 * P
C_COLS = C_INV + 4 * PAD
PARAMS = {}
for _name, _n in (("g_mix", DT), ("g_ffn", DT), ("g_ple", DT), ("g_final", DT), ("pool_scale", 4),
                  ("norm_mix", 2 * DT), ("conv_w", CONV * DT), ("conv_b", DT), ("b_r", DT), ("b_i", DT),
                  ("lam", DT), ("kv_norm", DT), ("norm_ffn", 2 * DT), ("norm_ple", 2 * DT), ("final", DT)):
    PARAMS[_name] = sum(n for _, n in PARAMS.values()), _n
P_COLS = sum(n for _, n in PARAMS.values())


def bucket(d):
    n = np.maximum(d, 1).astype(np.float32)
    large = 16 + (np.log(n / np.float32(16)) / np.float32(np.log(128)) * np.float32(16)).astype(np.int32)
    return np.where(d < 16, d, np.minimum(large, 31))


def constants():
    k, m = np.arange(P)[:, None], np.arange(P)[None, :]
    base = np.concatenate([
        k == m, np.ones((P, P)), k < m, -1.0 * (k > m), -np.ones((P, P)), np.broadcast_to(m, (P, P)),
        np.broadcast_to(np.concatenate([1.0 / np.minimum(np.arange(PAD) + 1, w) for w in POOL_WINDOWS]), (P, 4 * PAD)),
    ], axis=1).astype(np.float32)
    dist = T - 1 - np.arange(SPAN)
    reach = (dist >= 0) * ((dist <= 128).astype(int) + (dist % 4 == 0) + (dist % 16 == 0))
    mask = np.where(reach > 0, np.log(np.maximum(reach, 1)), NEG).astype(np.float32)
    hot = (bucket(np.maximum(dist, 0))[None, :] == np.arange(32)[:, None]).astype(np.float32)
    twice = (k % CAP == m % CAP).astype(np.float32)
    return base, twice, np.ascontiguousarray(np.broadcast_to(mask, (P, SPAN))), hot


Y_PARTS = (("a_y0", range(0, 3)), ("a_y1", range(3, 4)), ("a_y2", range(4, 8)))


def plan():
    first, n = {}, 0
    for name, chunks in (
        ("w_in", 16), ("w_pool", 1), ("w_out", 8), ("w_router", 1), ("b_down", 1), ("proj0", 2), ("ple0", 8),
        ("a_x", 8), ("a_y0", 3), ("w_r", 1), ("a_y1", 1), ("w_i", 1), ("a_y2", 4), ("a_out", 8),
        ("wq0", 16), ("keys0", 2), ("u0", CHUNKS), ("v0", CHUNKS), ("proj1", 2), ("ple1", 8),
        ("kv", 16), ("bq", 8), ("bo", 8),
        ("wq1", 16), ("keys1", 2), ("u1", CHUNKS), ("v1", CHUNKS), ("proj2", 2), ("ple2", 8),
    ):
        first[name] = n
        n += chunks
    return first


class Tally:

    def __init__(self, eng, sem):
        self.eng, self.sem, self.n, self.turns = eng, sem, 0, 0

    def mark(self, ins):
        ins.then_inc(self.sem, 1)
        self.n += 1
        return self.n

    def wait(self, n=None):
        self.eng.wait_ge(self.sem, self.turns + (self.n if n is None else n))

    def link(self, ins):
        self.mark(ins)
        self.wait()

    def enter(self, turn, per, begin=0):
        self.turns, self.start, self.per = turn * per - begin * per, self.n, per

    def leave(self, count):
        assert self.n == self.start + self.per, (self.n - self.start, self.per)
        self.n, self.turns = self.start + self.per * count, 0


def program(nc, io, out):
    first = plan()
    with ExitStack() as ctx:
        def sb(name, shape, dt=F32):
            return ctx.enter_context(nc.sbuf_tensor(name, shape, dt))

        def sem(name):
            return ctx.enter_context(nc.semaphore(name))

        with nc.sbuf_tensor("big", [P, CHUNKS * T], F32) as big:
            pass
        sb("moe_raw_place", [P, MOE_RAW * MOE_COLS])
        moe_hi = sb("moe_hi", [P, MOE_SPLIT * MOE_COLS], F32R)
        moe_lo = sb("moe_lo", [P, MOE_SPLIT * MOE_COLS], F32R)
        m_x = sb("m_x", [P, DT * 2 * CAP], F32R)
        m_h = sb("m_h", [P, DT * 2 * CAP], F32R)
        sb("tail_place", [P, CHUNKS * T - (MOE_RAW + 2 * MOE_SPLIT) * MOE_COLS - 4 * DT * CAP])
        with nc.sbuf_tensor("ring", [P, RING, SLOT], F32) as ring:
            pass
        sb("ring_raw_place", [P, RAW * SLOT])
        w_hi = sb("w_hi", [P, SPLIT, SLOT], F32R)
        w_lo = sb("w_lo", [P, SPLIT, SLOT], F32R)
        with nc.sbuf_tensor("xT", [P, W], F32) as xT:
            pass
        h_hi = sb("h_hi", [P, W], F32R)
        with nc.sbuf_tensor("hT", [P, W], F32) as hT:
            pass
        h_lo = sb("h_lo", [P, W], F32R)
        mT = sb("mT", [P, W])
        con = sb("con", [P, C_COLS])
        par = sb("par", [P, P_COLS])
        rs = sb("rs", [P, 2 * T])
        eps = sb("eps", [P, 1])
        small = sb("small", [P, 4064])
        pT = sb("pT", [P, 2 * T])
        ps = ctx.enter_context(nc.psum_tensor("ps", [P, 8, BANK], F32))
        toeplitz = nc.dram_tensor("toeplitz", (HEADS1, P, SPAN), F32, kind="Internal").ap()
        expert_out = nc.dram_tensor("expert_out", (EXPERTS * CAP, D), F32, kind="Internal").ap()

        x_aside = nc.dram_tensor("x_aside", (P, W), F32, kind="Internal").ap()

        ident, ones = con[:, C_IDENT:C_IDENT + P], con[:, C_ONES:C_ONES + P]
        triu, ntri = con[:, C_TRIU:C_TRIU + P], con[:, C_NTRI:C_NTRI + P]
        nones, iota = con[:, C_NONES:C_NONES + P], con[:, C_IOTA:C_IOTA + P]

        def col(name, k=0):
            a, n = PARAMS[name]
            return par[:, a + k:a + k + 1]

        def tile(buf, c, n=T):
            return buf[:, c * n:(c + 1) * n]

        def half(bank, e):
            return ps[:, bank + e // 2, (e % 2) * T:(e % 2 + 1) * T]

        w_loaded = [sem(f"w_loaded{k}") for k in range(RING)]
        w_used = sem("w_used")
        x_loaded, con_loaded, par_loaded = sem("x_loaded"), sem("con_loaded"), sem("par_loaded")
        attn_loaded, bias_loaded = sem("attn_loaded"), sem("bias_loaded")
        x_ready, h_ready = sem("x_ready"), sem("h_ready")
        sq_ready, ss_done, rms_ready = sem("sq_ready"), sem("ss_done"), sem("rms_ready")
        eps_ready, p_loaded = sem("eps_ready"), sem("p_loaded")
        dve_step, act_step = sem("dve_step"), sem("act_step")
        names = (
            "rb_ready row_done row_ready toep_loaded u_copied qk_ready v_ready pooled_ready "
            "score_done biased prob_exp prob_ready pt_done pt_ready pv_done mix_ready "
            "htok_done htok_ready neg_top gate_exp mask_ready rank_done count_ready gmat_in gmat_done gmat_ready "
            "slots_ready diag_ready sel_ready gathered xg_high xg_ready sig_in sig_ready hid_ready y_ready yt_done "
            "ytok_ready gates_copied ups_copied turned hi_ready split_ready split_rest y_stored y_fetched combined added "
            "gate_ready conv_ready yg_ready lam_in lam_exp ri_ready lru_exp lru_e lru_sqrt gated_ready "
            "pq_ready s_done bank_read cv_ready cv_exp sel_done selT_done selT_ready "
            "offsets_ready hots_ready oh_ready g_done g_used x_spilled x_back "
            "h_high h_split u_high u_split_pool u_split_dve v_high v_split half_used "
            "q2_ready k2_ready v2_ready z_done z_used spm_ready rc_done arg_ready a_exp w_exp a_ready o_done o_ready "
            "out_ready out_stored moe_step moe_used"
        ).split()
        S = {n: sem(n) for n in names}
        row_stored = [sem(f"row_stored{k}") for k in range(2)]
        moe_loaded = [sem(f"moe_loaded{k}") for k in range(MOE_RAW)]

        def used_through(eng, seg, chunks):
            eng.wait_ge(w_used, first[seg] + chunks)

        TAIL = (MOE_RAW + 2 * MOE_SPLIT) * MOE_COLS
        tail = big[:, TAIL:CHUNKS * T]
        q1, k1, v1 = (tail[:, k * 1024:(k + 1) * 1024] for k in range(3))
        toep = tail[:, 3072:3072 + HEADS1 * SPAN]
        upad = tail[:, 6144:6144 + 4 * (PAD + T)]
        twice = tail[:, 7232:7232 + P]
        moe_bias = tail[:, 7424:7936]
        winsum = small[:, 0:4 * (PAD + T)]
        winsum2 = small[:, 1088:2176]
        cmask, hot = small[:, 2176:2560], small[0:32, 2560:2944]
        relb, rb = small[0:32, 2944:2952], small[0:32, 3040:4064]
        stat1 = small[:, 2952:3000]
        prob = [hT[:, k * SPAN:(k + 1) * SPAN] for k in range(2)]
        probT = [hT[:, (2 + k) * SPAN:(3 + k) * SPAN] for k in range(2)]
        row = [mT[:, k * SPAN:(k + 1) * SPAN] for k in range(2)]

        r_max, r_idx = small[:, 0:16], small[:, 16:32]
        r_idxf, r_nmax = small[:, 32:40], small[:, 40:42]
        r_exp, r_sum, r_rec, r_gate = small[:, 48:56], small[:, 56:58], small[:, 58:60], small[:, 60:68]
        r_bias, r_logit = small[:, 3008:3040], small[:, 160:224]
        r_hot = small[:, 256:512]
        r_mask, r_gmat = small[:, 512:576], small[:, 576:640]
        r_rank1 = small[:, 640:640 + TT * EXPERTS]
        r_tmp = small[:, 768:1024]
        r_slotf, r_slot = small[:, 1024:1032], small[:, 1032:1040].bitcast(U32)
        r_pass, r_step = small[:, 1056:1064], small[:, 1064:1072]
        r_cntf, r_cnt = small[0:1, 4062:4063], small[0:1, 4063:4064].bitcast(I32)
        r_gmatT = small[0:32, 1280:1280 + T]
        r_diag = small[:, 1536:1536 + 8 * P]
        m_sel = small[:, 2560:2560 + TT * P]
        MW = DT * CAP
        m_gu = tail[:, 2048:4096]
        m_y = tail[:, 2048:3072]
        m_tok = tail[0:CAP, 4096:5120]
        m_g, m_u, m_sig, m_hid = (tail[:, 5120 + MW * k:5120 + MW * (k + 1)] for k in range(4))
        fetched = big[:, 0:TT * TOP_K * D]

        lru = [big[:, k * W:(k + 1) * W] for k in range(8)]
        sp = small[:, 0:96]
        k2, q2, v2 = lru[0], lru[1], lru[2]
        st = [big[:, 3 * W + k * SPAN:3 * W + (k + 1) * SPAN] for k in range(28)]

        pq = big[:, CHUNKS * T - 2 * W:CHUNKS * T]
        sv = small[:, 0:256]
        si = small[:, 256:512].bitcast(U32)
        sif = small[:, 512:768]
        cand, cand2 = small[:, 768:1024], small[:, 1024:1280]
        p_tmp = small[:, 1280:1408]
        cv = small[:, 1408:1664]
        ci = small[:, 1664:1792].bitcast(U32)
        cc = small[:, 1792:1920].bitcast(U32)
        ccf = small[:, 1920:2048]
        pick = small[:, 2048:3072].bitcast(BF16)
        i12 = small[:, 3072:3584]
        p_sum = small[:, 3584:3600]
        selT = small[:, 0:3 * T]


        def group_hot(g):
            return (mT, mT, hT, hT)[g][:, g % 2 * 2 * BANK:(g % 2 + 1) * 2 * BANK]

        places = iota.unsqueeze(1).broadcast_to((P, GROUP, P))
        by_token = lambda x: x.rearrange("p (s m) -> p s m", s=GROUP)

        def parts(k):
            return [h_lo[:, (k % 4 * 2 + z) * T:(k % 4 * 2 + z + 1) * T] for z in range(2)]

        def moe_low(eng, k, start, end):
            raw, split = k % MOE_RAW * MOE_COLS, k % MOE_SPLIT * MOE_COLS
            return eng.tensor_tensor(moe_lo[:, split + start:split + end], big[:, raw + start:raw + end],
                                     moe_hi[:, split + start:split + end], ALU.subtract)

        def low(eng, k, z):
            at = slice(z * BANK, (z + 1) * BANK)
            return eng.tensor_tensor(w_lo[:, k % SPLIT, at], ring[:, k % RAW, at], w_hi[:, k % SPLIT, at], ALU.subtract)

        block = ctx.enter_context(nc.Block())

        @block.sync
        def _(sync):
            def free(n):
                for L in range(2):
                    end = first[f"v{L}"] + CHUNKS
                    if end <= n < end + RING:
                        if n % RING < RAW:
                            sync.wait_ge(S["v_split"], 2 * CHUNKS * (L + 1))
                        else:
                            sync.wait_ge(w_used, end)
                        return
                if n >= RING:
                    sync.wait_ge(w_used, n - RING + 1)

            def load(n, src, cols=SLOT, rows=P):
                free(n)
                sync.dma_start(ring[0:rows, n % RING, 0:cols], src).then_inc(w_loaded[n % RING], 16)

            def dense(seg, w, halves=1):
                for h in range(halves):
                    for c in range(DT):
                        load(first[seg] + h * DT + c, w[c * P:(c + 1) * P, h * SLOT:(h + 1) * SLOT])

            def ple(k, p, proj, gate):
                if k:
                    sync.wait_ge(w_used, first[f"proj{k - 1}"] + 2)
                sync.dma_start(pT[:, :], p).then_inc(p_loaded, 16)
                for c in range(2):
                    load(first[f"proj{k}"] + c, proj[c * P:(c + 1) * P, :])
                dense(f"ple{k}", gate)

            def table(L, which, src):
                n = first[f"{which}{L}"]

                def load_raw(i, k):
                    j = i * BODY + k
                    sync.dma_start(ring[:, k % RAW, :], src[j]).then_inc(w_loaded[(n + k) % RING], 16)

                def body(i, pool, dve):
                    for k in range(BODY):
                        last = (i * BODY + (k - RAW + 1)) * 2
                        if which == "v":
                            sync.wait_ge(S["v_split"], last + 2 * CHUNKS * L)
                        elif pool and (k < RAW or not dve):
                            sync.wait_ge(S["u_split_pool"], last + 2 * BODY * POOL_BODIES * L)
                        else:
                            sync.wait_ge(S["u_split_dve"], last + 2 * (CHUNKS * L - BODY * POOL_BODIES * (L + 1)))
                        load_raw(i, k)

                for k in range(BODY):
                    if k >= RAW:
                        if which == "u":
                            sync.wait_ge(S["u_split_pool"], 2 * (BODY * POOL_BODIES * L + k - RAW + 1))
                        else:
                            sync.wait_ge(S["v_split"], 2 * (CHUNKS * L + k - RAW + 1))
                    elif which == "u":
                        sync.wait_ge(w_used, max(m for m in range(n - RING, n) if m % RING == k) + 1)
                    else:
                        sync.wait_ge(S["u_split_dve"], 2 * ((CHUNKS - BODY * POOL_BODIES) * (L + 1) - RAW + k + 1))
                    load_raw(0, k)
                if which == "u":
                    with sync.Fori(1, POOL_BODIES) as i:
                        body(i, True, False)
                    body(POOL_BODIES, True, True)
                    with sync.Fori(POOL_BODIES + 1, CHUNKS // BODY) as i:
                        body(i, False, True)
                else:
                    with sync.Fori(1, CHUNKS // BODY) as i:
                        body(i, False, True)

            def expert_chunk(e, k, count=None):
                if count is not None:
                    for done in ("split_ready", "split_rest"):
                        sync.wait_ge(S[done], count)
                dst = big[:, k % MOE_RAW * MOE_COLS:(k % MOE_RAW + 1) * MOE_COLS]
                if k < DT:
                    src = io["w_gate_up"][e, k * P:(k + 1) * P, :]
                else:
                    src = io["w_down"][e, (k - DT) * 2 * P:(k - DT + 1) * 2 * P, :].rearrange("(s p) d -> p s d", p=P)
                    dst = dst.rearrange("p (s d) -> p s d", s=2)
                sync.dma_start(dst, src).then_inc(moe_loaded[k % MOE_RAW], 16)

            def expert_weights(level, start=0):
                if level:
                    sync.wait_ge(S["combined"], level)
                with sync.Fori(start, EXPERTS) as e:
                    for k in range(MOE_CHUNKS):
                        expert_chunk(e, k, e * MOE_CHUNKS + (EXPERTS * level * MOE_CHUNKS + k - MOE_RAW + 1))

            sync.dma_start(xT[:, :], io["x"]).then_inc(x_loaded, 16)
            sync.dma_start(con[:, :], io["consts"]).then_inc(con_loaded, 16)
            sync.dma_start(par[:, :], io["params"]).then_inc(par_loaded, 16)
            sync.dma_start(cmask, io["reach"]).then_inc(attn_loaded, 16)
            sync.dma_start(hot, io["hot"]).then_inc(attn_loaded, 16)
            sync.dma_start(relb, io["rel_bias"]).then_inc(attn_loaded, 16)
            sync.dma_start(moe_bias, io["b_gate_up"]).then_inc(bias_loaded, 16)
            sync.dma_start(twice, io["twice"]).then_inc(bias_loaded, 16)
            sync.dma_start(r_bias, io["b_router"].partition_broadcast(P)).then_inc(bias_loaded, 16)
            dense("w_in", io["w_in"], 2)
            load(first["w_pool"], io["w_pool"], 4 * P)
            dense("w_out", io["w_out"])
            load(first["w_router"], io["w_router"], DT * EXPERTS)
            load(first["b_down"], io["b_down"], rows=EXPERTS)
            for k in range(MOE_CHUNKS):
                expert_chunk(0, k, k - MOE_RAW + 1 if k >= MOE_RAW else None)
            expert_weights(0, 1)
            sync.wait_ge(S["count_ready"], 1)
            count = sync.value_load(r_cnt, min_val=0, max_val=T)
            with ExitStack() as nest:
                for level in range(1, PASSES):
                    nest.enter_context(sync.If(count > CAP * level))
                    expert_weights(level)
            ple(0, io["p0"], io["w_ple_proj"], io["w_ple_gate"])
            dense("a_x", io["a_w_in"])
            for (seg, cs), gate in zip(Y_PARTS, ("w_r", "w_i", None)):
                for c in cs:
                    load(first[seg] + c - cs[0], io["a_w_in"][c * P:(c + 1) * P, SLOT:2 * SLOT])
                if gate:
                    load(first[gate], io[gate])
            dense("a_out", io["a_w_out"])
            for L in range(2):
                dense(f"wq{L}", io["peer_w_q"][L], 2)
                for k in range(2):
                    load(first[f"keys{L}"] + k, io["sub_keys"][L, :, k * SLOT:(k + 1) * SLOT])
                table(L, "u", io[f"u{L}"])
                table(L, "v", io[f"v{L}"])
                ple(L + 1, io["p2"][L], io["ple_w_proj"][L], io["ple_w_gate"][L])
                if L == 0:
                    dense("kv", io["w_kv"], 2)
                    dense("bq", io["b_w_q"])
                    dense("bo", io["b_w_o"])
            sync.wait_ge(S["out_ready"], 8)
            sync.dma_start(out, mT[:, :]).then_inc(S["out_stored"], 16)
            sync.wait_ge(S["out_stored"], 16)

        @block.tensor
        def _(pe):
            def chunk(n):
                pe.wait_ge(w_loaded[n % RING], 16 * (n // RING + 1))
                return ring[:, n % RING, :]

            def sum_squares(k):
                for j in range(4):
                    pe.wait_ge(sq_ready, 4 * k + j + 1)
                    for c in (2 * j, 2 * j + 1):
                        last = pe.matmul(ps[:, 7, 0:T], ones, tile(mT, c), start=(c == 0), stop=(c == DT - 1))
                last.then_inc(ss_done, 1)

            def dense(n, src, bank, ready=None, at=0, between=None, cs=range(DT)):
                for c in cs:
                    if ready is not None:
                        pe.wait_ge(ready, at + c + 1)
                    w = chunk(n + c - cs[0])
                    for e in range(DT):
                        last = pe.matmul(half(bank, e), w[:, e * P:(e + 1) * P], src(c),
                                         start=(c == 0 and e % 2 == 0), stop=(c == DT - 1), skip_group_check=True)
                    last.then_inc(w_used, 1)
                    if between:
                        between(c)

            def token_major(n, src, ready, at, cols, outs):
                for c in range(DT):
                    pe.wait_ge(ready, at + c + 1)
                    w = chunk(n + c)
                    for tt in range(TT):
                        for k, o in enumerate(outs[tt]):
                            last = pe.matmul(o, tile(src, c)[:, tt * P:(tt + 1) * P],
                                             w[:, cols + k * BANK:cols + (k + 1) * BANK],
                                             start=(c == 0), stop=(c == DT - 1), skip_group_check=True)
                    last.then_inc(w_used, 1)

            hsrc = lambda c: tile(hT, c)
            msrc = lambda c: tile(mT, c)

            pe.wait_ge(con_loaded, 16)
            sum_squares(0)
            pe.wait_ge(attn_loaded, 48)

            def bias_row(h):
                pe.wait_ge(S["rb_ready"], h + 1)
                if h >= 2:
                    pe.wait_ge(S["row_ready"], h - 1)
                pe.matmul(ps[:, 4 + h % 2, 0:SPAN], rb[:, h * P:(h + 1) * P], hot, start=True, stop=True)\
                    .then_inc(S["row_done"], 1)

            dense(first["w_in"], hsrc, 0, h_ready, 0, between=bias_row)
            pe.wait_ge(S["row_ready"], HEADS1)
            pe.wait_ge(rms_ready, 1)
            for c in range(DT):
                w = chunk(first["w_in"] + DT + c)
                for e in range(4):
                    pe.matmul(half(4, e), w[:, e * P:(e + 1) * P], hsrc(c),
                              start=(c == 0 and e % 2 == 0), stop=(c == DT - 1), skip_group_check=True)
                for tt in range(TT):
                    last = pe.matmul(ps[:, 6 + tt, :], hsrc(c)[:, tt * P:(tt + 1) * P], w[:, BANK:2 * BANK],
                                     start=(c == 0), stop=(c == DT - 1), skip_group_check=True)
                last.then_inc(w_used, 1)

            def scores(h):
                lo = 64 * (h % 2)
                q, k = tile(q1, h // 2), tile(k1, h // 2)
                if h == 0:
                    pe.wait_ge(S["qk_ready"], 4)
                    pe.wait_ge(S["u_copied"], 4)
                if h >= 2:
                    pe.wait_ge(S["prob_ready"], h - 1)
                pe.matmul(ps[:, h % 2, 0:P], q[lo:lo + DH, 0:P], k[lo:lo + DH, 0:P], start=True, stop=True)
                pe.matmul(ps[:, h % 2, P:SPAN], q[lo:lo + DH, P:T], k[lo:lo + DH, 0:T], start=True, stop=True)\
                    .then_inc(S["score_done"], 1)

            def turn(h):
                pe.wait_ge(S["prob_ready"], h + 1)
                if h >= 2:
                    pe.wait_ge(S["pt_ready"], h - 1)
                for b in range(3):
                    last = pe.transpose(ps[:, 2 + h % 2, b * P:(b + 1) * P], prob[h % 2][:, b * P:(b + 1) * P], ident)
                last.then_inc(S["pt_done"], 1)

            def values(h):
                lo = 64 * (h % 2)
                if h == 0:
                    pe.wait_ge(S["v_ready"], 2)
                pe.wait_ge(S["pt_ready"], h + 1)
                if h >= 4:
                    pe.wait_ge(S["mix_ready"], h - 3)
                o = ps[lo:lo + DH, 4 + (h // 2) % 2, 0:T]
                v = [v1[:, tt * BANK + h * DH:tt * BANK + (h + 1) * DH] for tt in range(TT)]
                pt = probT[h % 2]
                pe.matmul(o[:, 0:P], v[0], pt[:, 0:P], start=True, stop=True)
                pe.matmul(o[:, P:T], v[0], pt[:, P:2 * P], start=True, stop=False)
                pe.matmul(o[:, P:T], v[1], pt[:, 2 * P:SPAN], start=False, stop=True).then_inc(S["pv_done"], 1)

            for s in range(HEADS1 + 2):
                if s < HEADS1:
                    scores(s)
                if 1 <= s <= HEADS1:
                    turn(s - 1)
                if s >= 2:
                    values(s - 2)
            w = chunk(first["w_pool"])
            pe.wait_ge(S["v_ready"], 2)
            for g in range(4):
                pe.wait_ge(S["pooled_ready"], g + 1)
                last = pe.matmul(half(6, g), w[:, g * P:(g + 1) * P], upad[:, g * (PAD + T) + PAD:(g + 1) * (PAD + T)],
                                 start=True, stop=True)
            last.then_inc(w_used, 1)
            pe.wait_ge(S["mix_ready"], HEADS1 + 4)
            dense(first["w_out"], msrc, 0)

            sum_squares(1)
            pe.wait_ge(h_ready, 2 * DT)
            w = chunk(first["w_router"])
            for tt in range(TT):
                for c in range(DT):
                    last = pe.matmul(ps[:, 4, tt * EXPERTS:(tt + 1) * EXPERTS], tile(hT, c)[:, tt * P:(tt + 1) * P],
                                     w[:, c * EXPERTS:(c + 1) * EXPERTS], start=(c == 0), stop=(c == DT - 1))
            last.then_inc(w_used, 1)
            for tt in range(TT):
                for c in range(DT):
                    last = pe.transpose(ps[:, 2 * tt + c // 4, (c % 4) * P:(c % 4 + 1) * P],
                                        tile(hT, c)[:, tt * P:(tt + 1) * P], ident)
                last.then_inc(S["htok_done"], 1)
            pe.wait_ge(S["mask_ready"], 2)
            pe.matmul(ps[:, 5, 0:32], triu, r_mask[:, 0:32], start=True, stop=True)
            pe.matmul(ps[:, 5, 32:64], triu, r_mask[:, 32:64], start=True, stop=False)
            pe.matmul(ps[:, 5, 32:64], ones, r_mask[:, 0:32], start=False, stop=True)
            pe.matmul(ps[:, 5, 64:96], ones, r_mask[:, 0:32], start=True, stop=False)
            pe.matmul(ps[:, 5, 64:96], ones, r_mask[:, 32:64], start=False, stop=True).then_inc(S["rank_done"], 1)
            pe.wait_ge(S["gmat_in"], 2)
            for tt in range(TT):
                last = pe.transpose(ps[0:32, 6, tt * P:(tt + 1) * P], r_gmat[:, tt * 32:(tt + 1) * 32], ident)
            last.then_inc(S["gmat_done"], 1)

            def expert_pass(level):
                base = EXPERTS * level

                def gather(e):
                    pe.wait_ge(S["sel_ready"], e + base + 1)
                    for c in range(DT):
                        for tt in range(TT):
                            last = pe.matmul(ps[:, c // 4, (c % 4) * P:(c % 4 + 1) * P],
                                             mT[:, tt * D + c * P:tt * D + (c + 1) * P],
                                             m_sel[:, tt * P:(tt + 1) * P], start=(tt == 0), stop=(tt == TT - 1))
                    last.then_inc(S["gathered"], 1)

                def split(n, k):
                    for done in ("split_ready", "split_rest"):
                        pe.wait_ge(S[done], n * MOE_CHUNKS + k + 1)

                def products(k, operand, bank, blocks, start, stop):
                    for s, o in enumerate(operand):
                        for part in (moe_hi, moe_lo):
                            for b in range(blocks):
                                a = k % MOE_SPLIT * MOE_COLS + (s * blocks + b) * BANK
                                last = pe.matmul(ps[:, bank + b, :], o, part[:, a:a + BANK],
                                                 start=(start and s == 0 and part is moe_hi),
                                                 stop=(stop and s == len(operand) - 1 and part is moe_lo),
                                                 skip_group_check=True)
                    last.then_inc(S["moe_used"], 1)

                def sum_halves(n):
                    for b in range(2):
                        pe.wait_ge(S["y_ready"], n * 2 + b + 1)
                        pe.matmul(ps[0:CAP, b, :], twice[:, 0:CAP], tile(m_y, b, 512), start=True, stop=True)\
                            .then_inc(S["yt_done"], 1)

                def expert(e, first=False, last=False):
                    n = e + base
                    pe.wait_ge(S["xg_ready"], n * 2 + 2)
                    for c in range(DT):
                        split(n, c)
                        products(c, [m_x[:, c * P:(c + 1) * P]], 2, 4, c == 0, c == DT - 1)
                        if c == 0 and not first:
                            sum_halves(n - 1)
                    if not first:
                        pe.wait_ge(S["ytok_ready"], n * 2)
                    if not last:
                        gather(e + 1)
                    for b in range(2):
                        pe.wait_ge(S["gates_copied"], n * 2 + b + 1)
                        pe.wait_ge(S["ups_copied"], n * 2 + b + 1)
                        for bank in (b, 2 + b):
                            for f in range(4):
                                a = bank * BANK + f * P
                                ins = pe.matmul(ps[:, 2 + bank, f * P:(f + 1) * P], m_gu[:, a:a + P], twice,
                                                start=True, stop=True)
                        ins.then_inc(S["turned"], 1)
                    for k in range(DT, MOE_CHUNKS):
                        f = 2 * (k - DT)
                        pe.wait_ge(S["hid_ready"], n * 2 + 1 + f // 4)
                        split(n, k)
                        products(k, [m_h[:, (f + s) * P:(f + s + 1) * P] for s in range(2)], 6, 2,
                                 k == DT, k == MOE_CHUNKS - 1)
                    if last:
                        sum_halves(n)

                if level == 0:
                    pe.wait_ge(S["htok_ready"], 4)
                    pe.wait_ge(S["gmat_ready"], 1)
                gather(0)
                expert(0, first=True)
                with pe.Fori(1, EXPERTS - 1) as e:
                    expert(e)
                expert(EXPERTS - 1, last=True)

            def combine(level):
                pe.wait_ge(S["ytok_ready"], 2 * EXPERTS * (level + 1))
                if level == 0:
                    w = chunk(first["b_down"])
                    for c in range(DT):
                        last = pe.matmul(half(0, c), w[0:EXPERTS, c * P:(c + 1) * P], r_gmatT, start=(c % 2 == 0),
                                         stop=False, skip_group_check=True)
                    last.then_inc(w_used, 1)
                pe.wait_ge(S["diag_ready"], 8 * (level + 1))
                pe.wait_ge(S["y_fetched"], 16 * 8 * (level + 1))
                for c in range(DT):
                    for tt in range(TT):
                        for k in range(TOP_K):
                            a = (tt * TOP_K + k) * D + c * P
                            last = pe.matmul(half(0, c)[:, tt * P:(tt + 1) * P], fetched[:, a:a + P],
                                             r_diag[:, (tt * TOP_K + k) * P:(tt * TOP_K + k + 1) * P],
                                             start=(level > 0 and c % 2 == 0 and tt == 0 and k == 0),
                                             stop=(k == TOP_K - 1), skip_group_check=True)
                last.then_inc(S["combined"], 1)

            expert_pass(0)
            combine(0)
            count = pe.value_load(r_cnt, min_val=0, max_val=T)
            with ExitStack() as nest:
                for level in range(1, PASSES):
                    nest.enter_context(pe.If(count > CAP * level))
                    pe.wait_ge(S["added"], 4 * level)
                    expert_pass(level)
                    combine(level)

            def ple(k, norm, reads):
                pe.wait_ge(x_ready, 4 * (norm - 1) + 4)
                n = first[f"proj{k}"]
                pe.wait_ge(p_loaded, 16 * (k + 1))
                for c in range(2):
                    w = chunk(n + c)
                    for e in range(DT):
                        last = pe.matmul(half(0, e), w[:, e * P:(e + 1) * P], tile(pT, c),
                                         start=(c == 0 and e % 2 == 0), stop=(c == 1), skip_group_check=True)
                    last.then_inc(w_used, 1)
                    if c == 0:
                        sum_squares(norm)
                dense(first[f"ple{k}"], hsrc, 4, h_ready, DT * reads)

            ple(0, 2, 2)
            sum_squares(3)

            sum_squares(4)
            dense(first["a_x"], hsrc, 0, h_ready, 3 * DT)
            for k, (seg, cs) in enumerate(Y_PARTS):
                dense(first[seg], hsrc, 4, cs=cs)
                if k < 2:
                    w = chunk(first[("w_r", "w_i")[k]])
                    if k == 0:
                        pe.wait_ge(S["conv_ready"], DT)
                    else:
                        pe.wait_ge(S["ri_ready"], DT)
                    for h in range(DT):
                        last = pe.matmul(half(0, h), w[:, h * P:(h + 1) * P], tile(lru[0], h), start=True, stop=True)
                    last.then_inc(w_used, 1)
            pe.wait_ge(S["ri_ready"], 2 * DT)
            dense(first["a_out"], msrc, 0, S["gated_ready"], 0)

            def peer(L, norm, at):
                sum_squares(norm)
                dense(first[f"wq{L}"], hsrc, 0, h_ready, at)
                dense(first[f"wq{L}"] + DT, hsrc, 4)
                keys = [chunk(first[f"keys{L}"] + k) for k in range(2)]
                pe.wait_ge(S["pq_ready"], 8 * L + 8)
                for tt in range(TT):
                    for hp in range(16):
                        last = pe.matmul(ps[:, 4 * tt + hp // 4, (hp % 4) * P:(hp % 4 + 1) * P],
                                         tile(pq, hp)[:, tt * P:(tt + 1) * P],
                                         keys[hp // 8][:, (hp % 8) * P:(hp % 8 + 1) * P], start=True, stop=True)
                        if tt and hp % 8 == 7:
                            last.then_inc(w_used, 1)
                    if tt == 0:
                        last.then_inc(S["s_done"], 1)
                pe.wait_ge(S["h_split"], 4 * L + 4)

                def u_body(i, sem_, offset):
                    for k in range(BODY):
                        if k % 2 == 0:
                            pe.wait_ge(S["bank_read"], READS * L + k // 2 + 1 + i * 4)
                        for c in range(DT):
                            if c % 4 == 0:
                                pe.wait_ge(sem_, i * (2 * BODY) + (offset + 2 * k + c // 4 + 1))
                            hi, lo = (x[:, k % SPLIT, c * P:(c + 1) * P] for x in (w_hi, w_lo))
                            pe.matmul(half(0, k), hi, tile(h_hi, c), start=(c == 0), stop=False)
                            pe.matmul(half(0, k), hi, tile(h_lo, c), start=False, stop=False)
                            last = pe.matmul(half(0, k), lo, tile(h_hi, c), start=False, stop=(c == DT - 1))
                            if c % 4 == 3:
                                last.then_inc(w_used if c == DT - 1 else S["half_used"], 1)

                with pe.Fori(0, POOL_BODIES) as i:
                    u_body(i, S["u_split_pool"], 2 * BODY * POOL_BODIES * L)
                dve_offset = 2 * (CHUNKS * L - BODY * POOL_BODIES * (L + 1))
                with pe.Fori(POOL_BODIES, TURN_BODY) as i:
                    u_body(i, S["u_split_dve"], dve_offset)
                pe.wait_ge(S["sel_done"], L + 1)
                for k in range(3):
                    for tt in range(TT):
                        src = (i12[:, (k * TT + tt) * P:(k * TT + tt + 1) * P] if k < 2 else cv[:, tt * P:(tt + 1) * P])
                        last = pe.transpose(ps[:, 4 + k, tt * P:(tt + 1) * P], src, ident)
                last.then_inc(S["selT_done"], 1)
                with pe.Fori(TURN_BODY, CHUNKS // BODY) as i:
                    u_body(i, S["u_split_dve"], dve_offset)
                with pe.Fori(0, T // TOKENS) as i:
                    for g in range(GROUPS):
                        pe.wait_ge(S["oh_ready"], i * GROUPS + (T // GROUP * L + g + 1))
                        h = group_hot(g)
                        for s in range(GROUP):
                            last = pe.matmul(ps[:, 4 + g, s * P:(s + 1) * P], h[:, s * P:(s + 1) * P],
                                             h[:, BANK + s * P:BANK + (s + 1) * P], start=True, stop=True)
                        last.then_inc(S["g_done"], 1)
                pe.wait_ge(S["x_back"], 16 * (L + 1))
                for e in range(DT):
                    pe.matmul(half(0, e), ident, tile(xT, e), start=(e % 2 == 0), stop=False, skip_group_check=True)
                with pe.Fori(0, CHUNKS // BODY) as i:
                    for k in range(BODY):
                        a_hi, a_lo = parts(k)
                        for e in range(DT):
                            if e % 4 == 0:
                                pe.wait_ge(S["v_split"], i * (2 * BODY) + (2 * CHUNKS * L + 2 * k + e // 4 + 1))
                            hi, lo = (x[:, k % SPLIT, e * P:(e + 1) * P] for x in (w_hi, w_lo))
                            pe.matmul(half(0, e), hi, a_hi, start=False, stop=False, skip_group_check=True)
                            pe.matmul(half(0, e), hi, a_lo, start=False, stop=False, skip_group_check=True)
                            last = pe.matmul(half(0, e), lo, a_hi, start=False, stop=True, skip_group_check=True)
                            if e % 4 == 3:
                                last.then_inc(w_used if e == DT - 1 else S["half_used"], 1)

            peer(0, 5, 4 * DT)
            ple(1, 6, 5)

            sum_squares(7)
            dense(first["kv"], hsrc, 0, h_ready, 6 * DT)
            token_major(first["kv"] + DT, hT, h_ready, 6 * DT, 0,
                        [[ps[:, 4 + 2 * tt + k, :] for k in range(2)] for tt in range(TT)])
            pe.wait_ge(S["k2_ready"], 4)
            dense(first["bq"], msrc, 0, h_ready, 7 * DT)

            def logits(h):
                lo = 64 * (h % 2)
                q, k = tile(q2, h // 2), tile(k2, h // 2)
                if h == 0:
                    pe.wait_ge(S["q2_ready"], 4)
                    pe.wait_ge(S["v2_ready"], 4)
                if h >= 4:
                    pe.wait_ge(S["z_used"], h - 3)
                z = ps[:, h % 4, 0:SPAN]
                pe.matmul(z[:, 0:T], k[lo:lo + DH, 0:P], q[lo:lo + DH, 0:T], start=True, stop=True)
                pe.matmul(z[:, T:SPAN], k[lo:lo + DH, P:T], q[lo:lo + DH, P:T], start=True, stop=True)\
                    .then_inc(S["z_done"], 1)

            def suffix(h):
                g = h % 4
                pe.wait_ge(S["spm_ready"], h + 1)
                if h >= 2:
                    pe.wait_ge(S["arg_ready"], h - 1)
                r = ps[:, 4 + h % 2, 0:SPAN]
                pe.matmul(r[:, 0:P], ntri, st[8 + g][:, 0:P], start=True, stop=True)
                pe.matmul(r[:, P:T], ntri, st[4 + g][:, P:T], start=True, stop=False)
                pe.matmul(r[:, P:T], nones, st[8 + g][:, T:SPAN], start=False, stop=True)
                pe.matmul(r[:, T:SPAN], ntri, st[8 + g][:, T:SPAN], start=True, stop=True).then_inc(S["rc_done"], 1)

            def heads_out(h):
                lo, g = 64 * (h % 2), h % 4
                pe.wait_ge(S["a_ready"], h + 1)
                if h >= 4:
                    pe.wait_ge(S["o_ready"], h - 3)
                o = ps[lo:lo + DH, 6 + (h // 2) % 2, 0:T]
                v = [v2[:, tt * D + h * DH:tt * D + (h + 1) * DH] for tt in range(TT)]
                a = st[12 + g]
                pe.matmul(o[:, 0:P], v[0], a[:, 0:P], start=True, stop=True)
                pe.matmul(o[:, P:T], v[0], a[:, P:T], start=True, stop=False)
                pe.matmul(o[:, P:T], v[1], a[:, T:SPAN], start=False, stop=True).then_inc(S["o_done"], 1)

            for h in range(4):
                logits(h)
            for g in range(HEADS2 // 4):
                for h in range(4 * g, 4 * g + 4):
                    if g < HEADS2 // 4 - 1:
                        logits(h + 4)
                    if g >= 1:
                        heads_out(h - 4)
                for h in range(4 * g, 4 * g + 4):
                    suffix(h)
            for h in range(HEADS2 - 4, HEADS2):
                heads_out(h)
            pe.wait_ge(S["o_ready"], HEADS2)
            dense(first["bo"], msrc, 0)
            peer(1, 8, 8 * DT)
            ple(2, 9, 9)
            sum_squares(10)

        @block.scalar
        def _(act):
            step = Tally(act, act_step)

            def squares(k):
                if k == 0:
                    act.wait_ge(x_loaded, 16)
                for j in range(4):
                    if k:
                        act.wait_ge(x_ready, 4 * (k - 1) + j + 1)
                    act.activation(tile(mT, j, 512), tile(xT, j, 512), ACT.Square).then_inc(sq_ready, 1)
                act.wait_ge(ss_done, k + 1)
                act.activation(rs[:, 0:T], ps[:, 7, 0:T], ACT.Sqrt, scale=1.0 / D, bias=eps[:, :])\
                    .then_inc(rms_ready, 1)

            act.wait_ge(eps_ready, 1)
            squares(0)
            used_through(act, "w_in", 8)
            for g in range(4):
                act.copy(upad[:, g * (PAD + T) + PAD:(g + 1) * (PAD + T)], half(0, g)).then_inc(S["u_copied"], 1)
            for b in range(2):
                act.copy(tile(q1, b, 512), ps[:, 2 + b, :]).then_inc(S["qk_ready"], 1)
            used_through(act, "w_in", 16)
            for b in range(2):
                act.copy(tile(k1, b, 512), ps[:, 4 + b, :]).then_inc(S["qk_ready"], 1)

            def exps(h):
                act.wait_ge(S["biased"], h + 1)
                n = stat1[:, 6 * (h % 8):6 * (h % 8) + 6]
                p = prob[h % 2]
                act.activation(p[:, 0:P], p[:, 0:P], ACT.Exp, bias=n[:, 0:1], accum_out=n[:, 2:3])
                act.activation(p[:, P:SPAN], p[:, P:SPAN], ACT.Exp, bias=n[:, 1:2], accum_out=n[:, 3:4])\
                    .then_inc(S["prob_exp"], 1)

            def copy_pt(h):
                act.wait_ge(S["pt_done"], h + 1)
                if h >= 2:
                    act.wait_ge(S["pv_done"], h - 1)
                act.copy(probT[h % 2], ps[:, 2 + h % 2, 0:SPAN]).then_inc(S["pt_ready"], 1)

            def copy_o(h):
                lo = 64 * (h % 2)
                act.wait_ge(S["pv_done"], h + 1)
                if h == 0:
                    for k in range(2):
                        act.wait_ge(row_stored[k], 16 * (HEADS1 // 2))
                act.copy(tile(mT, 4 + h // 2)[lo:lo + DH, :], ps[lo:lo + DH, 4 + (h // 2) % 2, 0:T])\
                    .then_inc(S["mix_ready"], 1)

            for s in range(HEADS1 + 2):
                if s < HEADS1:
                    exps(s)
                if 1 <= s <= HEADS1:
                    copy_pt(s - 1)
                if s >= 2:
                    copy_o(s - 2)
            used_through(act, "w_pool", 1)
            for g in range(4):
                act.activation(tile(mT, g), half(6, g), ACT.Copy, scale=col("pool_scale", g)).then_inc(S["mix_ready"], 1)

            squares(1)
            for tt in range(TT):
                act.wait_ge(S["htok_done"], tt + 1)
                for b in range(2):
                    act.copy(mT[:, tt * D + b * BANK:tt * D + (b + 1) * BANK], ps[:, 2 * tt + b, :])\
                        .then_inc(S["htok_ready"], 1)
            for tt in range(TT):
                act.wait_ge(S["neg_top"], tt + 1)
                act.activation(r_exp[:, tt * 4:tt * 4 + 4], r_max[:, tt * 8:tt * 8 + 4], ACT.Exp,
                               bias=r_nmax[:, tt:tt + 1], accum_out=r_sum[:, tt:tt + 1]).then_inc(S["gate_exp"], 1)

            def expert_pass(level):
                base = EXPERTS * level

                def split(n, k):
                    act.wait_ge(moe_loaded[k % MOE_RAW], n * 32 + 16 * (k // MOE_RAW + 1))
                    used = n * MOE_CHUNKS + (k - MOE_SPLIT + 1)
                    if not isinstance(used, int) or used > 0:
                        act.wait_ge(S["moe_used"], used)
                    act.copy(moe_hi[:, k % MOE_SPLIT * MOE_COLS:(k % MOE_SPLIT + 1) * MOE_COLS],
                             big[:, k % MOE_RAW * MOE_COLS:(k % MOE_RAW + 1) * MOE_COLS]).then_inc(S["hi_ready"], 1)

                def gathered(n):
                    act.wait_ge(S["gathered"], n + 1)
                    for b in range(2):
                        act.copy(m_x[:, b * BANK:(b + 1) * BANK].rearrange("p (c n) -> p c n", n=P)[:, :, 0:CAP],
                                 ps[:, b, :].rearrange("p (c n) -> p c n", n=P)[:, :, 0:CAP])\
                            .then_inc(S["xg_high"], 1)

                def store(e):
                    n = e + base
                    if level or not isinstance(e, int) or e > 0:
                        act.wait_ge(S["y_stored"], n * 16)
                    for b in range(2):
                        act.wait_ge(S["yt_done"], n * 2 + b + 1)
                        act.copy(tile(m_tok, b, 512), ps[0:CAP, b, :]).then_inc(S["ytok_ready"], 1)
                    act.wait_ge(S["ytok_ready"], n * 2 + 2)
                    act.dma_start(expert_out[bass.ds(e * CAP, CAP), :], m_tok).then_inc(S["y_stored"], 16)

                def expert(e, first=False, last=False):
                    n = e + base
                    split(n, 3)
                    if not first:
                        store(e - 1)
                    for k in range(4, 10):
                        split(n, k)
                    act.wait_ge(S["moe_used"], n * MOE_CHUNKS + DT)
                    for b in range(2):
                        act.copy(tile(m_gu, b, 512), ps[:, 2 + b, :]).then_inc(S["gates_copied"], 1)
                    split(n, 10)
                    for b in range(2):
                        act.wait_ge(S["sig_in"], n * 2 + b + 1)
                        act.activation(tile(m_sig, b, 256), tile(m_g, b, 256), ACT.Sigmoid, scale=ALPHA)\
                            .then_inc(S["sig_ready"], 1)
                    if not last:
                        gathered(n + 1)
                    split(n, 11)
                    for k in range(12, 14):
                        if not last:
                            split(n, k)
                    act.wait_ge(S["moe_used"], n * MOE_CHUNKS + MOE_CHUNKS)
                    for b in range(2):
                        act.copy(tile(m_y, b, 512), ps[:, 6 + b, :]).then_inc(S["y_ready"], 1)
                    if last:
                        store(e)
                    else:
                        split(n, 14)

                for k in range(MOE_SPLIT):
                    split(base, k)
                gathered(base)
                expert(0, first=True)
                with act.Fori(1, EXPERTS - 1) as e:
                    expert(e)
                expert(EXPERTS - 1, last=True)

            expert_pass(0)
            act.wait_ge(S["count_ready"], 1)
            count = act.value_load(r_cnt, min_val=0, max_val=T)
            with ExitStack() as nest:
                for level in range(1, PASSES):
                    nest.enter_context(act.If(count > CAP * level))
                    expert_pass(level)

            def ple(k, norm):
                squares(norm)
                used_through(act, f"ple{k}", 8)
                for b in range(4):
                    act.activation(tile(mT, b, 512), ps[:, 4 + b, :], ACT.Sigmoid).then_inc(S["gate_ready"], 1)

            ple(0, 2)
            squares(3)

            squares(4)
            act.wait_ge(S["lam_in"], 1)
            act.activation(sp[:, 8:16], sp[:, 0:8], ACT.Exp, scale=-1.0).then_inc(S["lam_exp"], 1)
            for k, name in enumerate(("b_r", "b_i")):
                used_through(act, ("w_r", "w_i")[k], 1)
                for h in range(DT):
                    act.activation(tile(lru[2 + k], h), half(0, h), ACT.Sigmoid, bias=col(name, h))\
                        .then_inc(S["ri_ready"], 1)
            act.wait_ge(S["ri_ready"], 16)
            act.wait_ge(S["lam_in"], 2)
            for h in range(DT):
                act.activation(tile(lru[4], h), tile(lru[2], h), ACT.Exp, scale=sp[:, 72 + h:73 + h])
                act.activation(tile(lru[5], h), tile(lru[2], h), ACT.Tanh, scale=sp[:, 80 + h:81 + h])\
                    .then_inc(S["lru_exp"], 1)
            for b in range(4):
                act.wait_ge(S["lru_e"], b + 1)
                act.activation(tile(lru[6], b, 512), tile(lru[5], b, 512), ACT.Sqrt).then_inc(S["lru_sqrt"], 1)
            used_through(act, "a_y2", 4)
            for b in range(4):
                act.activation(tile(lru[1], b, 512), ps[:, 4 + b, :], ACT.Gelu_apprx_tanh).then_inc(S["yg_ready"], 1)

            def peer(L, norm):
                squares(norm)
                for k in range(2):
                    used_through(act, f"wq{L}", 8 * (k + 1))
                    for b in range(4):
                        act.copy(pq[:, (4 * k + b) * 512:(4 * k + b + 1) * 512], ps[:, 4 * k + b, :])\
                            .then_inc(S["pq_ready"], 1)
                act.wait_ge(S["x_spilled"], 16 * (L + 1))
                for b in range(4):
                    act.copy(tile(h_hi, b, 512), tile(hT, b, 512)).then_inc(S["h_high"], 1)
                act.wait_ge(S["s_done"], L + 1)
                for b in range(4):
                    act.copy(tile(mT, b, 512), ps[:, b, :]).then_inc(S["bank_read"], 1)

                def high(which, i, k, z):
                    m = first[f"{which}{L}"] + k
                    if z == 0:
                        act.wait_ge(w_loaded[m % RING], 16 * (m // RING + 1) + i * 16)
                        if which == "u" and k == 0:
                            used_through(act, f"keys{L}", 2)
                        used = i * BODY + (CHUNKS * (2 * L + (which == "v")) + k - SPLIT + 1)
                        if not isinstance(used, int) or used > 0:
                            act.wait_ge(S["half_used"], used)
                    else:
                        act.wait_ge(w_used, i * BODY + (m - SPLIT + 1))
                    at = slice(z * BANK, (z + 1) * BANK)
                    return act.copy(w_hi[:, k % SPLIT, at], ring[:, k % RAW, at])

                def gelu(i, k):
                    act.activation(big[:, bass.ds(i * (BODY * T) + k * T, BANK)], ps[:, (k // 2) % 4, :],
                                   ACT.Gelu_apprx_tanh).then_inc(S["bank_read"], 1)

                def body(i, start=False):
                    for k in range(BODY):
                        for z in range(2):
                            high("u", i, k, z).then_inc(S["u_high"], 1)
                        if k % 2 and not (start and k == 1):
                            gelu(i, k - 3)

                body(0, True)
                with act.Fori(1, EXP_BODY) as i:
                    body(i)
                act.wait_ge(S["cv_ready"], L + 1)
                act.activation(cv, cv, ACT.Exp).then_inc(S["cv_exp"], 1)
                with act.Fori(EXP_BODY, CHUNKS // BODY) as i:
                    body(i)
                used_through(act, f"u{L}", CHUNKS)
                gelu(CHUNKS // BODY, -2)
                act.wait_ge(S["selT_ready"], 3 * L + 3)
                with act.Fori(0, T // TOKENS) as i:
                    for g in range(GROUPS):
                        act.wait_ge(S["hots_ready"], i * GROUPS + (T // GROUP * L + g + 1))
                        for s in range(GROUP):
                            dst = group_hot(g)[:, BANK + s * P:BANK + (s + 1) * P]
                            ins = act.activation(dst, dst, ACT.Copy,
                                                 scale=selT[:, bass.ds(i * TOKENS + (2 * T + g * GROUP + s), 1)])
                        ins.then_inc(S["oh_ready"], 1)
                act.wait_ge(S["g_used"], T // GROUP * (L + 1))
                with act.Fori(0, CHUNKS // BODY) as i:
                    for k in range(BODY):
                        high("v", i, k, 0)
                        act.copy(parts(k)[0], big[:, bass.ds(i * (BODY * T) + k * T, T)]).then_inc(S["v_high"], 1)
                        high("v", i, k, 1).then_inc(S["v_high"], 1)

            peer(0, 5)
            ple(1, 6)

            squares(7)
            used_through(act, "kv", 8)
            for b in range(4):
                act.copy(tile(k2, b, 512), ps[:, b, :]).then_inc(S["k2_ready"], 1)
            used_through(act, "bq", 8)
            for b in range(4):
                act.activation(tile(q2, b, 512), ps[:, b, :], ACT.Copy, scale=DH ** -0.5).then_inc(S["q2_ready"], 1)

            def softplus_in(g):
                for h in range(4 * g, 4 * g + 4):
                    a = st[h % 4]
                    act.wait_ge(S["z_done"], h + 1)
                    step.link(act.activation(a, ps[:, h % 4, 0:SPAN], ACT.Abs))
                    step.mark(act.activation(a, a, ACT.Exp, scale=-1.0))
                step.wait()
                for h in range(4 * g, 4 * g + 4):
                    if h >= 4:
                        act.wait_ge(S["spm_ready"], h - 3)
                    act.activation(st[16 + h % 4], st[h % 4], ACT.Ln, bias=1.0).then_inc(S["a_exp"], 1)

            def outputs(g):
                for h in range(4 * g, 4 * g + 4):
                    lo = 64 * (h % 2)
                    act.wait_ge(S["o_done"], h + 1)
                    act.copy(tile(mT, h // 2)[lo:lo + DH, :], ps[lo:lo + DH, 6 + (h // 2) % 2, 0:T])\
                        .then_inc(S["o_ready"], 1)

            softplus_in(0)
            for g in range(HEADS2 // 4):
                if g < HEADS2 // 4 - 1:
                    softplus_in(g + 1)
                if g >= 1:
                    outputs(g - 1)
                for h in range(4 * g, 4 * g + 4):
                    act.wait_ge(S["arg_ready"], h + 1)
                    if h >= 4:
                        act.wait_ge(S["o_done"], h - 3)
                    act.activation(st[12 + h % 4], st[20 + h % 8], ACT.Exp).then_inc(S["w_exp"], 1)
            outputs(HEADS2 // 4 - 1)
            peer(1, 8)
            ple(2, 9)
            squares(10)

        @block.vector
        def _(dve):
            step = Tally(dve, dve_step)
            link, mark = step.link, step.mark

            def norm(k, gains, dsts=(hT,), sem_=h_ready):
                dve.wait_ge(rms_ready, k + 1)
                link(dve.reciprocal(rs[:, T:2 * T], rs[:, 0:T]))
                for dst, (name, at) in zip(dsts, gains):
                    for c in range(DT):
                        dve.scalar_tensor_tensor(tile(dst, c), tile(xT, c), col(name, at + c), rs[:, T:2 * T],
                                                 op0=ALU.mult, op1=ALU.mult).then_inc(sem_, 1)

            def add_to_x(seg, chunks):
                used_through(dve, seg, chunks)
                for b in range(4):
                    dve.tensor_tensor(tile(xT, b, 512), ps[:, b, :], tile(xT, b, 512), ALU.add).then_inc(x_ready, 1)

            dve.memset(eps[:, :], EPS).then_inc(eps_ready, 1)
            dve.wait_ge(attn_loaded, 48)
            dve.wait_ge(con_loaded, 16)
            for h in range(HEADS1):
                dve.tensor_scalar(rb[:, h * P:(h + 1) * P], ones[0:32, :], relb[:, h:h + 1], None, ALU.mult)\
                    .then_inc(S["rb_ready"], 1)
            dve.memset(upad, 0.0).then_inc(dve_step, 1)
            step.n += 1
            dve.wait_ge(x_loaded, 16)
            dve.wait_ge(par_loaded, 16)
            norm(0, [("g_mix", 0)])
            dve.wait_ge(h_ready, DT)
            for h in range(HEADS1):
                dve.wait_ge(S["row_done"], h + 1)
                if h >= 2:
                    dve.wait_ge(row_stored[h % 2], 16 * (h // 2))
                dve.tensor_tensor(row[h % 2], ps[:, 4 + h % 2, 0:SPAN], cmask, ALU.add).then_inc(S["row_ready"], 1)
            dve.wait_ge(S["u_copied"], 4)
            up = upad.rearrange("p (g t) -> p g t", g=4)
            s0 = winsum.rearrange("p (g t) -> p g t", g=4)
            s1 = winsum2.rearrange("p (g t) -> p g t", g=4)
            E = PAD + T
            link(dve.tensor_tensor(s0[:, :, 1:E], up[:, :, 1:E], up[:, :, 0:E - 1], ALU.add))
            link(dve.tensor_tensor(s1[:, 1:4, 3:E], s0[:, 1:4, 3:E], s0[:, 1:4, 1:E - 2], ALU.add))
            link(dve.tensor_tensor(s0[:, 2:4, 7:E], s1[:, 2:4, 7:E], s1[:, 2:4, 3:E - 4], ALU.add))
            link(dve.tensor_tensor(s1[:, 3, 15:E], s0[:, 3, 15:E], s0[:, 3, 7:E - 8], ALU.add))
            for g, w in enumerate(POOL_WINDOWS):
                s = (s0, s1)[g % 2][:, g, PAD:E]
                link(dve.tensor_scalar(s[:, PAD:T], s[:, PAD:T], 1.0 / w, None, ALU.mult))
                link(dve.tensor_tensor(s[:, 0:PAD], s[:, 0:PAD], con[:, C_INV + g * PAD:C_INV + (g + 1) * PAD], ALU.mult))
                dve.tensor_tensor(up[:, g, PAD:E], s, up[:, g, PAD:E], ALU.subtract).then_inc(S["pooled_ready"], 1)
            used_through(dve, "w_in", 16)
            for tt in range(TT):
                dve.tensor_copy(tile(v1, tt, 512), ps[:, 6 + tt, :]).then_inc(S["v_ready"], 1)

            def biased(h):
                dve.wait_ge(S["score_done"], h + 1)
                dve.wait_ge(S["toep_loaded"], 32 * HEADS1)
                if h >= 2:
                    dve.wait_ge(S["pt_done"], h - 1)
                n = stat1[:, 6 * h:6 * h + 6]
                p = prob[h % 2]
                link(dve.scalar_tensor_tensor(p, ps[:, h % 2, 0:SPAN], DH ** -0.5, toep[:, h * SPAN:(h + 1) * SPAN],
                                              op0=ALU.mult, op1=ALU.add))
                mark(dve.tensor_reduce(n[:, 4:5], p[:, 0:P], AX_X, ALU.max))
                link(dve.tensor_reduce(n[:, 5:6], p[:, P:SPAN], AX_X, ALU.max))
                dve.tensor_scalar(n[:, 0:2], n[:, 4:6], -1.0, None, ALU.mult).then_inc(S["biased"], 1)

            def normalised(h):
                n = stat1[:, 6 * h:6 * h + 6]
                p = prob[h % 2]
                dve.wait_ge(S["prob_exp"], h + 1)
                link(dve.reciprocal(n[:, 4:6], n[:, 2:4]))
                link(dve.tensor_scalar(p[:, 0:P], p[:, 0:P], n[:, 4:5], None, ALU.mult))
                dve.tensor_scalar(p[:, P:SPAN], p[:, P:SPAN], n[:, 5:6], None, ALU.mult).then_inc(S["prob_ready"], 1)

            for s in range(HEADS1 + 1):
                if s < HEADS1:
                    biased(s)
                if s >= 1:
                    normalised(s - 1)
            add_to_x("w_out", 8)

            norm(1, [("g_ffn", 0)])
            used_through(dve, "w_router", 1)
            dve.wait_ge(bias_loaded, 48)
            i32c = iota[:, 0:EXPERTS]
            for tt in range(TT):
                lg = r_logit[:, tt * 32:(tt + 1) * 32]
                top, idx = r_max[:, tt * 8:tt * 8 + 8], r_idx[:, tt * 8:tt * 8 + 8].bitcast(U32)
                link(dve.tensor_tensor(lg, ps[:, 4, tt * 32:(tt + 1) * 32], r_bias, ALU.add))
                link(dve.max(top, lg))
                dve.tensor_scalar(r_nmax[:, tt:tt + 1], top[:, 0:1], -1.0, None, ALU.mult).then_inc(S["neg_top"], 1)
                link(dve.max_index(idx, top, lg))
                link(dve.tensor_copy(r_idxf[:, tt * 4:tt * 4 + 4], idx[:, 0:4]))
                hots = r_hot[:, tt * 128:(tt + 1) * 128].rearrange("p (k e) -> p k e", k=TOP_K)
                for k in range(TOP_K):
                    mark(dve.tensor_scalar(hots[:, k, :], i32c, r_idxf[:, tt * 4 + k:tt * 4 + k + 1], None, ALU.is_equal))
                step.wait()
                dve.tensor_reduce(r_mask[:, tt * 32:(tt + 1) * 32], hots.rearrange("p k e -> p e k"), AX_X, ALU.add)\
                    .then_inc(S["mask_ready"], 1)
            for tt in range(TT):
                dve.wait_ge(S["gate_exp"], tt + 1)
                gate = r_gate[:, tt * 4:tt * 4 + 4]
                link(dve.reciprocal(r_rec[:, tt:tt + 1], r_sum[:, tt:tt + 1]))
                link(dve.tensor_scalar(gate, r_exp[:, tt * 4:tt * 4 + 4], r_rec[:, tt:tt + 1], None, ALU.mult))
                gm = r_gmat[:, tt * 32:(tt + 1) * 32]
                hot_k = lambda k: r_hot[:, tt * 128 + k * 32:tt * 128 + (k + 1) * 32]
                link(dve.tensor_scalar(gm, hot_k(0), gate[:, 0:1], None, ALU.mult))
                for k in range(1, TOP_K):
                    ins = dve.scalar_tensor_tensor(gm, hot_k(k), gate[:, k:k + 1], gm, op0=ALU.mult, op1=ALU.add)
                    if k < TOP_K - 1:
                        link(ins)
                    else:
                        ins.then_inc(S["gmat_in"], 1)
            dve.wait_ge(S["rank_done"], 1)
            link(dve.tensor_reduce(r_cntf, ps[0:1, 5, 64:96], AX_X, ALU.max))
            dve.tensor_copy(r_cnt, r_cntf).then_inc(S["count_ready"], 1)
            for tt in range(TT):
                rank, mask = ps[:, 5, tt * 32:(tt + 1) * 32], r_mask[:, tt * 32:(tt + 1) * 32]
                link(dve.scalar_tensor_tensor(r_rank1[:, tt * 32:(tt + 1) * 32], rank, 1.0, mask,
                                              op0=ALU.add, op1=ALU.mult))
                hots = r_hot[:, tt * 128:(tt + 1) * 128].rearrange("p (k e) -> p k e", k=TOP_K)
                tmp = r_tmp[:, tt * 128:(tt + 1) * 128].rearrange("p (k e) -> p k e", k=TOP_K)
                link(dve.tensor_tensor(tmp, rank.unsqueeze(1).broadcast_to((P, TOP_K, EXPERTS)), hots, ALU.mult))
                link(dve.tensor_reduce(r_slotf[:, tt * 4:tt * 4 + 4], tmp, AX_X, ALU.add))
            link(dve.tensor_scalar(r_pass, r_slotf, float(CAP), None, ALU.is_ge))
            for level in range(2, PASSES):
                link(dve.tensor_scalar(r_step, r_slotf, float(CAP * level), None, ALU.is_ge))
                link(dve.tensor_tensor(r_pass, r_pass, r_step, ALU.add))
            link(dve.scalar_tensor_tensor(r_slotf, r_pass, -float(CAP), r_slotf, op0=ALU.mult, op1=ALU.add))
            link(dve.scalar_tensor_tensor(r_slotf, r_idxf, float(CAP), r_slotf, op0=ALU.mult, op1=ALU.add))
            dve.tensor_copy(r_slot, r_slotf).then_inc(S["slots_ready"], 1)

            def diagonals(level, link):
                link(dve.scalar_tensor_tensor(r_step, r_pass, float(level), r_gate, op0=ALU.is_equal, op1=ALU.mult))
                for k in range(TT * TOP_K):
                    dve.tensor_scalar(r_diag[:, k * P:(k + 1) * P], ident, r_step[:, k:k + 1], None, ALU.mult)\
                        .then_inc(S["diag_ready"], 1)

            diagonals(0, link)
            dve.wait_ge(S["gmat_done"], 1)
            dve.tensor_copy(r_gmatT, ps[0:32, 6, 0:T]).then_inc(S["gmat_ready"], 1)

            moe = Tally(dve, S["moe_step"])

            def expert_pass(level):
                base = EXPERTS * level

                def select(e):
                    for tt in range(TT):
                        ins = dve.tensor_scalar(m_sel[:, tt * P:(tt + 1) * P], iota,
                                                float(level * CAP + 1), r_rank1[:, bass.ds(e + tt * EXPERTS, 1)],
                                                ALU.add, ALU.is_equal)
                    ins.then_inc(S["sel_ready"], 1)

                def split(n, k):
                    dve.wait_ge(S["hi_ready"], n * MOE_CHUNKS + k + 1)
                    moe_low(dve, k, 0, MOE_DVE).then_inc(S["split_ready"], 1)

                def gathered(n):
                    for b in range(2):
                        dve.wait_ge(S["xg_high"], n * 2 + b + 1)
                        x = m_x[:, b * BANK:(b + 1) * BANK].rearrange("p (c n) -> p c n", n=P)
                        dve.tensor_tensor(x[:, :, CAP:P], ps[:, b, :].rearrange("p (c n) -> p c n", n=P)[:, :, 0:CAP],
                                          x[:, :, 0:CAP], ALU.subtract).then_inc(S["xg_ready"], 1)

                def expert(e, last=False):
                    n = e + base
                    split(n, 3)
                    if not last:
                        select(e + 1)
                    for k in range(4, 10):
                        split(n, k)
                    dve.wait_ge(S["moe_used"], n * MOE_CHUNKS + DT)
                    for b in range(2):
                        dve.tensor_copy(tile(m_gu, 2 + b, 512), ps[:, 4 + b, :]).then_inc(S["ups_copied"], 1)
                    split(n, 10)
                    for b in range(2):
                        dve.wait_ge(S["turned"], n * 2 + b + 1)
                        three = lambda x: x[:, b * 256:(b + 1) * 256].rearrange("p (f n) -> p f n", n=CAP)
                        bank = lambda k: ps[:, k, :].rearrange("p (f n) -> p f n", n=P)[:, :, 0:CAP]
                        bias = lambda k: moe_bias[:, bass.ds(e * 16 + k, 4)].unsqueeze(2).broadcast_to((P, 4, CAP))
                        g, u, sig, h = (three(x) for x in (m_g, m_u, m_sig, m_hid))
                        hh = m_h[:, b * BANK:(b + 1) * BANK].rearrange("p (f n) -> p f n", n=P)
                        moe.link(dve.tensor_tensor(g, bank(2 + b), bias(4 * b), ALU.add))
                        dve.tensor_scalar(g, g, LIMIT, None, ALU.min).then_inc(S["sig_in"], 1)
                        moe.link(dve.tensor_tensor(u, bank(4 + b), bias(8 + 4 * b), ALU.add))
                        moe.link(dve.tensor_scalar(u, u, LIMIT, -LIMIT, ALU.min, ALU.max))
                        dve.wait_ge(S["sig_ready"], n * 2 + b + 1)
                        moe.link(dve.tensor_tensor(sig, sig, g, ALU.mult))
                        moe.link(dve.scalar_tensor_tensor(h, u, 1.0, sig, op0=ALU.add, op1=ALU.mult))
                        moe.link(dve.tensor_copy(hh[:, :, 0:CAP], h))
                        dve.tensor_tensor(hh[:, :, CAP:P], h, hh[:, :, 0:CAP], ALU.subtract)\
                            .then_inc(S["hid_ready"], 1)
                    if not last:
                        gathered(n + 1)
                    split(n, 11)
                    if not last:
                        for k in range(12, 15):
                            split(n, k)

                select(0)
                for k in range(MOE_SPLIT):
                    split(base, k)
                gathered(base)
                expert(0)
                with dve.Fori(1, EXPERTS - 1) as e:
                    moe.enter(e, 12, 1)
                    expert(e)
                moe.leave(EXPERTS - 2)
                expert(EXPERTS - 1, last=True)

            expert_pass(0)
            dve.wait_ge(S["count_ready"], 1)
            count = dve.value_load(r_cnt, min_val=0, max_val=T)
            with ExitStack() as nest:
                for level in range(1, PASSES):
                    nest.enter_context(dve.If(count > CAP * level))
                    dve.wait_ge(S["combined"], level)
                    for b in range(4):
                        dve.tensor_tensor(tile(xT, b, 512), ps[:, b, :], tile(xT, b, 512), ALU.add)\
                            .then_inc(S["added"], 1)
                    diagonals(level, moe.link)
                    expert_pass(level)
            dve.wait_ge(S["combined"], 1)
            with ExitStack() as nest:
                for level in range(1, PASSES):
                    nest.enter_context(dve.If(count > CAP * level))
                    dve.wait_ge(S["combined"], level + 1)
            for b in range(4):
                dve.tensor_tensor(tile(xT, b, 512), ps[:, b, :], tile(xT, b, 512), ALU.add).then_inc(x_ready, 1)

            def ple(k, norm_no, gain):
                norm(norm_no, [gain])
                for b in range(4):
                    dve.wait_ge(S["gate_ready"], 4 * k + b + 1)
                    link(dve.tensor_tensor(tile(mT, b, 512), ps[:, b, :], tile(mT, b, 512), ALU.mult))
                    dve.tensor_tensor(tile(xT, b, 512), tile(mT, b, 512), tile(xT, b, 512), ALU.add).then_inc(x_ready, 1)

            ple(0, 2, ("g_ple", 0))
            dve.wait_ge(rms_ready, 4)
            link(dve.reciprocal(rs[:, T:2 * T], rs[:, 0:T]))
            for c in range(DT):
                ins = dve.scalar_tensor_tensor(tile(xT, c), tile(xT, c), col("g_final", c), rs[:, T:2 * T],
                                               op0=ALU.mult, op1=ALU.mult)
                if c % 2:
                    ins.then_inc(x_ready, 1)

            norm(4, [("norm_mix", 0)])
            lam = par[:, PARAMS["lam"][0]:PARAMS["lam"][0] + DT]
            link(dve.tensor_scalar(sp[:, 16:24], lam, -1.0, None, ALU.mult))
            dve.tensor_tensor(sp[:, 0:8], lam, sp[:, 16:24], ALU.max).then_inc(S["lam_in"], 1)
            dve.wait_ge(S["lam_exp"], 1)
            y, z, z2, acc = sp[:, 8:16], sp[:, 24:32], sp[:, 32:40], sp[:, 40:48]
            link(dve.tensor_scalar(z, y, 2.0, None, ALU.add))
            link(dve.reciprocal(z2, z))
            link(dve.tensor_tensor(z, y, z2, ALU.mult))
            link(dve.tensor_tensor(z2, z, z, ALU.mult))
            link(dve.tensor_scalar(acc, z2, 1.0 / 17, 1.0 / 15, ALU.mult, ALU.add))
            for k in (13, 11, 9, 7, 5, 3, 1):
                link(dve.tensor_tensor(acc, acc, z2, ALU.mult))
                link(dve.tensor_scalar(acc, acc, 1.0 / k, None, ALU.add))
            link(dve.tensor_tensor(acc, acc, z, ALU.mult))
            link(dve.tensor_scalar(sp[:, 16:24], sp[:, 16:24], 0.0, None, ALU.max))
            link(dve.scalar_tensor_tensor(acc, acc, 2.0, sp[:, 16:24], op0=ALU.mult, op1=ALU.add))
            link(dve.tensor_scalar(sp[:, 72:80], acc, -8.0, None, ALU.mult))
            dve.tensor_scalar(sp[:, 80:88], acc, 8.0, None, ALU.mult).then_inc(S["lam_in"], 1)
            used_through(dve, "a_x", 8)
            marks = [mark(dve.tensor_scalar(tile(lru[0], c), half(0, c), col("conv_w", 3 * DT + c), col("conv_b", c),
                                            ALU.mult, ALU.add)) for c in range(DT)]
            for back in range(1, CONV):
                for c in range(DT):
                    step.wait(marks[c])
                    dst = tile(lru[0], c)[:, back:T]
                    ins = dve.scalar_tensor_tensor(dst, half(0, c)[:, 0:T - back], col("conv_w", (3 - back) * DT + c), dst,
                                                   op0=ALU.mult, op1=ALU.add)
                    if back < CONV - 1:
                        marks[c] = mark(ins)
                    else:
                        ins.then_inc(S["conv_ready"], 1)
            dve.wait_ge(S["conv_ready"], DT)
            for b in range(4):
                dve.wait_ge(S["ri_ready"], DT + 2 * b + 2)
                mark(dve.tensor_tensor(tile(lru[3], b, 512), tile(lru[3], b, 512), tile(lru[0], b, 512), ALU.mult))
            for b in range(4):
                dve.wait_ge(S["lru_exp"], 2 * b + 2)
                a, th = tile(lru[4], b, 512), tile(lru[5], b, 512)
                link(dve.tensor_tensor(tile(lru[6], b, 512), a, a, ALU.mult))
                dve.scalar_tensor_tensor(th, tile(lru[6], b, 512), 1.0, th, op0=ALU.add, op1=ALU.mult)\
                    .then_inc(S["lru_e"], 1)
            for b in range(4):
                dve.wait_ge(S["lru_sqrt"], b + 1)
                link(dve.tensor_tensor(tile(lru[3], b, 512), tile(lru[3], b, 512), tile(lru[6], b, 512), ALU.mult))
                for c in (2 * b, 2 * b + 1):
                    mark(dve.tensor_tensor_scan(tile(lru[7], c), tile(lru[4], c), tile(lru[3], c), 0.0,
                                                ALU.mult, ALU.add))
                step.wait()
                for c in (2 * b, 2 * b + 1):
                    dve.wait_ge(S["yg_ready"], b + 1)
                    dve.tensor_tensor(tile(mT, c), tile(lru[7], c), tile(lru[1], c), ALU.mult)\
                        .then_inc(S["gated_ready"], 1)
            add_to_x("a_out", 8)

            def top16(vals, idx, src, tmp):
                link(dve.max(vals[:, 0:8], src))
                mark(dve.max_index(idx[:, 0:8], vals[:, 0:8], src))
                link(dve.match_replace(tmp, vals[:, 0:8], src, -3e38))
                link(dve.max(vals[:, 8:16], tmp))
                link(dve.max_index(idx[:, 8:16], vals[:, 8:16], tmp))

            def peer(L, norm_no, gain):
                norm(norm_no, [gain])
                for b in range(4):
                    dve.wait_ge(S["h_high"], 4 * L + b + 1)
                    dve.tensor_tensor(tile(h_lo, b, 512), tile(hT, b, 512), tile(h_hi, b, 512), ALU.subtract)\
                        .then_inc(S["h_split"], 1)
                for tt in (1, 0):
                    used_through(dve, f"keys{L}", 2)
                    if tt == 0:
                        dve.wait_ge(S["bank_read"], READS * L + 4)
                    for hp in range(16):
                        src = ps[:, 4 + hp // 4, (hp % 4) * P:(hp % 4 + 1) * P] if tt else mT[:, hp * P:(hp + 1) * P]
                        top16(sv[:, hp * 16:hp * 16 + 16], si[:, hp * 16:hp * 16 + 16], src, p_tmp)
                    link(dve.tensor_copy(sif, si))
                    vals = cv[:, tt * P:(tt + 1) * P]
                    for h in range(PH):
                        a = sv[:, 32 * h:32 * h + 16].unsqueeze(2).broadcast_to((P, 16, 16))
                        b = sv[:, 32 * h + 16:32 * h + 32].unsqueeze(1).broadcast_to((P, 16, 16))
                        link(dve.tensor_tensor(cand.rearrange("p (a b) -> p a b", a=16), a, b, ALU.add))
                        top16(vals[:, h * 16:h * 16 + 16], ci[:, h * 16:h * 16 + 16], cand, cand2)
                    for which in range(2):
                        if which == 0:
                            link(dve.tensor_scalar(cc, ci, 4, None, ALU.logical_shift_right))
                        else:
                            link(dve.tensor_scalar(cc, ci, 15, None, ALU.bitwise_and))
                        link(dve.tensor_copy(ccf, cc))
                        place = iota[:, 0:16].unsqueeze(1).broadcast_to((P, P, 16))
                        pk = pick.rearrange("p (k i) -> p k i", i=16)
                        link(dve.tensor_tensor(pk, ccf.unsqueeze(2).broadcast_to((P, P, 16)), place, ALU.is_equal))
                        for h in range(PH):
                            ids = sif[:, 32 * h + 16 * which:32 * h + 16 * which + 16]
                            mark(dve.tensor_tensor(pk[:, h * 16:h * 16 + 16, :], pk[:, h * 16:h * 16 + 16, :],
                                                   ids.unsqueeze(1).broadcast_to((P, 16, 16)), ALU.mult))
                        step.wait()
                        link(dve.tensor_reduce(i12[:, (which * TT + tt) * P:(which * TT + tt + 1) * P], pk, AX_X, ALU.add))
                    v3 = vals.rearrange("p (h k) -> p h k", h=PH)
                    link(dve.tensor_copy(p_sum[:, 0:8], v3[:, :, 0]))
                    ins = dve.tensor_tensor(v3, v3, p_sum[:, 0:8].unsqueeze(2).broadcast_to((P, PH, 16)), ALU.subtract)
                    if tt:
                        link(ins)
                    else:
                        ins.then_inc(S["cv_ready"], 1)

                def u_low(start, end):
                    with dve.Fori(start, end) as i:
                        for k in range(BODY):
                            for z in range(2):
                                dve.wait_ge(S["u_high"], i * (2 * BODY) + (2 * CHUNKS * L + 2 * k + z + 1))
                                low(dve, k, z).then_inc(S["u_split_dve"], 1)

                u_low(POOL_BODIES, EXP_BODY)
                dve.wait_ge(S["cv_exp"], L + 1)
                c3 = cv.rearrange("p (h k) -> p h k", k=16)
                link(dve.tensor_reduce(p_sum, c3, AX_X, ALU.add))
                link(dve.reciprocal(p_sum, p_sum))
                dve.tensor_tensor(c3, c3, p_sum.unsqueeze(2).broadcast_to((P, 2 * PH, 16)), ALU.mult)\
                    .then_inc(S["sel_done"], 1)
                u_low(EXP_BODY, COPY_BODY)
                dve.wait_ge(S["selT_done"], L + 1)
                for k in range(3):
                    dve.tensor_copy(selT[:, k * T:(k + 1) * T], ps[:, 4 + k, 0:T]).then_inc(S["selT_ready"], 1)
                u_low(COPY_BODY, CHUNKS // BODY)
                dve.wait_ge(S["selT_ready"], 3 * L + 3)
                dve.wait_ge(S["bank_read"], READS * (L + 1))
                act3 = big[:, :].rearrange("p (j t) -> p j t", t=T)

                def hots(i, g):
                    dve.wait_ge(S["offsets_ready"], i * GROUPS + (T // GROUP * L + g + 1))
                    dst = group_hot(g)
                    dve.tensor_scalar(dst[:, 0:BANK], dst[:, 0:BANK], 0.0, None, ALU.is_equal)
                    ids = selT[:, bass.ds(i * TOKENS + (T + g * GROUP), GROUP)].unsqueeze(2)
                    dve.tensor_tensor(by_token(dst[:, BANK:2 * BANK]), places, ids.broadcast_to((P, GROUP, P)),
                                      ALU.is_equal).then_inc(S["hots_ready"], 1)

                def gates(i, g):
                    dve.wait_ge(S["g_done"], i * GROUPS + (T // GROUP * L + g + 1))
                    dst = act3[:, :, bass.ds(i * TOKENS + g * GROUP, GROUP)]
                    dve.tensor_tensor(dst, ps[:, 4 + g % GROUPS, :].rearrange("p (t j) -> p j t", t=GROUP), dst,
                                      ALU.mult).then_inc(S["g_used"], 1)

                for g in range(GROUPS):
                    hots(0, g)
                gates(0, 0)
                with dve.Fori(1, T // TOKENS) as i:
                    for g in range(GROUPS):
                        hots(i, g)
                        gates(i, g - GROUPS + 1)
                for g in range(1 - GROUPS, 0):
                    gates(T // TOKENS, g)
                with dve.Fori(0, CHUNKS // BODY) as i:
                    for k in range(BODY):
                        a_hi, a_lo = parts(k)
                        dve.wait_ge(S["v_high"], i * (2 * BODY) + (2 * CHUNKS * L + 2 * k + 1))
                        low(dve, k, 0)
                        dve.tensor_tensor(a_lo, big[:, bass.ds(i * (BODY * T) + k * T, T)], a_hi, ALU.subtract)\
                            .then_inc(S["v_split"], 1)
                        dve.wait_ge(S["v_high"], i * (2 * BODY) + (2 * CHUNKS * L + 2 * k + 2))
                        low(dve, k, 1).then_inc(S["v_split"], 1)
                used_through(dve, f"v{L}", CHUNKS)
                for b in range(4):
                    dve.tensor_copy(tile(xT, b, 512), ps[:, b, :]).then_inc(x_ready, 1)

            peer(0, 5, ("norm_ffn", 0))
            ple(1, 6, ("norm_ple", 0))

            norm(7, [("kv_norm", 0), ("norm_mix", DT)], (hT, mT))
            used_through(dve, "kv", 16)
            for b in range(4):
                dve.tensor_copy(tile(v2, b, 512), ps[:, 4 + b, :]).then_inc(S["v2_ready"], 1)
            mask2 = triu.unsqueeze(1).broadcast_to((P, 2, P))
            diag = lambda x: x.rearrange("p (k t) -> p k t", k=3)[:, 0:3:2, :]

            def softplus(h):
                dve.wait_ge(S["a_exp"], h + 1)
                if h >= 4:
                    dve.wait_ge(S["rc_done"], h - 3)
                link(dve.scalar_tensor_tensor(st[4 + h % 4], ps[:, h % 4, 0:SPAN], 0.0, st[16 + h % 4],
                                              op0=ALU.max, op1=ALU.add))
                dve.tensor_tensor(diag(st[8 + h % 4]), diag(st[4 + h % 4]), mask2, ALU.mult)\
                    .then_inc(S["spm_ready"], 1)
                if h >= 8:
                    dve.wait_ge(S["w_exp"], h - 7)
                dve.tensor_tensor(st[20 + h % 8], ps[:, h % 4, 0:SPAN], st[4 + h % 4], ALU.subtract)\
                    .then_inc(S["z_used"], 1)

            def exponent(h):
                dve.wait_ge(S["z_used"], h + 1)
                dve.wait_ge(S["rc_done"], h + 1)
                dve.tensor_tensor(st[20 + h % 8], ps[:, 4 + h % 2, 0:SPAN], st[20 + h % 8], ALU.add)\
                    .then_inc(S["arg_ready"], 1)

            for h in range(4):
                softplus(h)
            for g in range(HEADS2 // 4):
                for h in range(4 * g, 4 * g + 4):
                    exponent(h)
                if g < HEADS2 // 4 - 1:
                    for h in range(4 * g + 4, 4 * g + 8):
                        softplus(h)
            add_to_x("bo", 8)
            peer(1, 8, ("norm_ffn", DT))
            ple(2, 9, ("norm_ple", DT))
            norm(10, [("final", 0)], (mT,), S["out_ready"])

        @block.gpsimd
        def _(pool):
            for h in range(HEADS1):
                pool.wait_ge(S["row_ready"], h + 1)
                pool.dma_start(toeplitz[h], row[h % 2]).then_inc(row_stored[h % 2], 16)
            for h in range(HEADS1):
                pool.wait_ge(row_stored[h % 2], 16 * (HEADS1 // 2))
                flat = toeplitz[h].rearrange("p x -> (p x)")
                skew = flat[0:P * (SPAN - 1)].rearrange("(p x) -> p x", p=P)
                dst = toep[:, h * SPAN:(h + 1) * SPAN]
                pool.dma_start(dst[:, 0:P], skew[:, P - 1 + P:2 * P - 1 + P]).then_inc(S["toep_loaded"], 16)
                pool.dma_start(dst[:, P:SPAN], skew[:, P - 1:P - 1 + T]).then_inc(S["toep_loaded"], 16)
            def split(level):
                with pool.Fori(0, EXPERTS) as e:
                    for k in range(MOE_CHUNKS):
                        pool.wait_ge(S["hi_ready"], e * MOE_CHUNKS + (EXPERTS * level * MOE_CHUNKS + k + 1))
                        moe_low(pool, k, MOE_DVE, MOE_COLS).then_inc(S["split_rest"], 1)

            def fetch(level):
                pool.wait_ge(S["y_stored"], 16 * EXPERTS * (level + 1))
                for k in range(TT * TOP_K):
                    pool.indirect_dma_start(out=fetched[:, k * D:(k + 1) * D], out_offset=None, in_=expert_out,
                                            in_offset=bass.IndirectOffsetOnAxis(ap=r_slot[:, k:k + 1], axis=0))\
                        .then_inc(S["y_fetched"], 16)

            split(0)
            pool.wait_ge(S["slots_ready"], 1)
            fetch(0)
            count = pool.value_load(r_cnt, min_val=0, max_val=T)
            with ExitStack() as nest:
                for level in range(1, PASSES):
                    nest.enter_context(pool.If(count > CAP * level))
                    split(level)
                    fetch(level)
            def peer(L, norm):
                pool.wait_ge(x_ready, 4 * norm)
                pool.dma_start(x_aside, xT[:, :]).then_inc(S["x_spilled"], 16)
                with pool.Fori(0, POOL_BODIES) as i:
                    for k in range(BODY):
                        for z in range(2):
                            pool.wait_ge(S["u_high"], i * (2 * BODY) + (2 * CHUNKS * L + 2 * k + z + 1))
                            low(pool, k, z).then_inc(S["u_split_pool"], 1)
                used_through(pool, f"u{L}", CHUNKS)
                pool.wait_ge(S["x_spilled"], 16 * (L + 1))
                pool.dma_start(xT[:, :], x_aside).then_inc(S["x_back"], 16)
                pool.wait_ge(S["selT_ready"], 3 * L + 3)

                def offsets(i, start=False):
                    for g in range(GROUPS):
                        if not start:
                            pool.wait_ge(S["g_done"], i * GROUPS + (T // GROUP * L + g + 1 - GROUPS))
                        ids = selT[:, bass.ds(i * TOKENS + g * GROUP, GROUP)].unsqueeze(2)
                        pool.tensor_tensor(by_token(group_hot(g)[:, 0:BANK]), places, ids.broadcast_to((P, GROUP, P)),
                                           ALU.subtract).then_inc(S["offsets_ready"], 1)

                offsets(0, True)
                with pool.Fori(1, T // TOKENS) as i:
                    offsets(i)

            peer(0, 5)
            mask2 = triu.unsqueeze(1).broadcast_to((P, 2, P))
            for h in range(HEADS2):
                pool.wait_ge(S["w_exp"], h + 1)
                a = st[12 + h % 4].rearrange("p (k t) -> p k t", k=3)[:, 0:3:2, :]
                pool.tensor_tensor(a, a, mask2, ALU.mult).then_inc(S["a_ready"], 1)
            peer(1, 8)


def kernel(**inputs):
    import concourse.bacc as bacc
    from concourse.bass_utils import run_bass_kernel_spmd

    a = {k: np.asarray(v) for k, v in inputs.items()}

    def cols(v):
        v = v.reshape(-1, v.shape[-1] // P, P)
        return v.transpose(2, 0, 1).reshape(P, -1)

    def t_form(v):
        return v.reshape(T, -1, P).transpose(2, 1, 0).reshape(P, -1)

    named = {
        "g_mix": a["g_mix"], "g_ffn": a["g_ffn"], "g_ple": a["g_ple"], "g_final": a["g_final"],
        "pool_scale": a["pool_scale"], "norm_mix": a["norm_mix_2"], "conv_w": a["a_conv_w_2"][0],
        "conv_b": a["a_conv_b_2"], "b_r": a["a_b_r_2"], "b_i": a["a_b_i_2"], "lam": a["a_lambda_2"],
        "kv_norm": a["kv_norm_2"], "norm_ffn": a["norm_ffn_2"], "norm_ple": a["norm_ple_2"],
        "final": a["final_norm_2"],
    }
    base, twice, reach, hot = constants()
    arrays = {
        "x": t_form(a["x"][0]),
        "consts": base, "twice": twice, "reach": reach, "hot": hot,
        "params": np.concatenate([cols(np.atleast_2d(named[n])) for n in PARAMS], axis=1),
        "rel_bias": a["rel_bias"],
        "w_in": a["w_in"][0],
        "w_pool": a["w_pool"][0].transpose(1, 0, 2).reshape(P, -1),
        "w_out": a["w_out"][0],
        "w_router": a["w_router"][0].reshape(DT, P, EXPERTS).transpose(1, 0, 2).reshape(P, -1),
        "b_router": a["b_router"][0],
        "w_gate_up": a["w_gate_up"][0], "w_down": a["w_down"][0], "b_down": a["b_down"][0],
        "b_gate_up": cols(a["b_gate_up"][0]),
        "p0": t_form(a["p"][0, 0]), "w_ple_gate": a["w_ple_gate"][0], "w_ple_proj": a["w_ple_proj"][0],
        "p2": np.stack([t_form(a["p_2"][L, 0]) for L in range(2)]),
        "ple_w_gate": a["ple_w_gate_2"], "ple_w_proj": a["ple_w_proj_2"],
        "a_w_in": np.concatenate([a["a_w_in_2"][0][:, D:], a["a_w_in_2"][0][:, :D]], axis=1),
        "w_r": a["a_w_r_2"][0].transpose(1, 0, 2).reshape(P, -1),
        "w_i": a["a_w_i_2"][0].transpose(1, 0, 2).reshape(P, -1),
        "a_w_out": a["a_w_out_2"][0],
        "w_kv": a["w_kv_2"], "b_w_q": a["b_w_q_2"][0], "b_w_o": a["b_w_o_2"][0],
        "peer_w_q": a["peer_w_q_2"],
        "sub_keys": a["peer_sub_keys_2"].reshape(2, 16, P, P).transpose(0, 3, 1, 2).reshape(2, P, -1),
    }
    for L in range(2):
        arrays[f"u{L}"] = a["peer_u_2"][L].reshape(P, P, DT, P).transpose(1, 3, 2, 0).reshape(P, P, D)
        arrays[f"v{L}"] = a["peer_v_2"][L].reshape(P, P, D).transpose(1, 0, 2)
    arrays = {k: np.ascontiguousarray(v) for k, v in arrays.items()}

    nc = bacc.Bacc("TRN2", target_bir_lowering=False, num_devices=1)
    io = {k: nc.dram_tensor(f"in_{k}", v.shape, mybir.dt.from_np(v.dtype), kind="ExternalInput").ap()
          for k, v in arrays.items()}
    out = nc.dram_tensor("out", (P, W), F32, kind="ExternalOutput").ap()
    program(nc, io, out)
    r = run_bass_kernel_spmd(nc, [{f"in_{k}": v for k, v in arrays.items()}], core_ids=[0])
    y = r.results[0]["out"]
    return y.reshape(P, DT, T).transpose(2, 1, 0).reshape(1, T, D)
```
